# Optimizing a Trainium2 kernel written in Bass

```python
import math
import jax, jax.numpy as jnp
from jax import lax
import numpy as np

D_MODEL = 1024
BATCH = 1
SEQ = 256
DEPTH = 1

MEM_TOKENS = 256
EPS = 1e-6
MLA_HEADS = 8
MLA_NOPE = 64
MLA_ROPE = 32
MLA_V = 64
MLA_Q_RANK = 256
MLA_KV_RANK = 128
ROPE_BASE = 10000.0
Q_BLOCK = 128
HY_WIDTH = D_MODEL - MLA_HEADS * MLA_V
HY_ORDER = 2
HY_DIRS = 2
HY_BANDS = 16
HY_EMB = 1 + 2 * HY_BANDS
HY_FFN = 64
HY_TARGET = 1e-2
HY_FAST_PCT = 0.3
HY_SLOW_PCT = 1.5
OFF_Q = 0
OFF_KV = OFF_Q + MLA_Q_RANK
OFF_KR = OFF_KV + MLA_KV_RANK
OFF_HY = OFF_KR + MLA_ROPE
IN_COLS = OFF_HY + 3 * HY_WIDTH
MEM_HEADS = 4
MEM_HEAD_DIM = D_MODEL // MEM_HEADS
N_GROUPS = 4
EXPERTS_PER_GROUP = 8
TOP_K_IN_GROUP = 2
D_EXPERT = 256


def _rms(x, g):
    xf = x.astype(jnp.float32)
    y = xf * lax.rsqrt(jnp.mean(xf * xf, axis=-1, keepdims=True) + EPS)
    return (y * g.astype(jnp.float32)).astype(x.dtype)

def _rope(x, cos, sin):
    x1, x2 = jnp.split(x.astype(jnp.float32), 2, axis=-1)
    return jnp.concatenate([x1 * cos - x2 * sin, x1 * sin + x2 * cos], axis=-1).astype(x.dtype)

def _mla(h_q, h_kv, h_kr, q_norm_g, kv_norm_g, w_uq, w_ukv):
    B, S, _ = h_q.shape
    q = (_rms(h_q, q_norm_g) @ w_uq).reshape(B, S, MLA_HEADS, MLA_NOPE + MLA_ROPE)
    q_nope, q_rot = q[..., :MLA_NOPE], q[..., MLA_NOPE:]
    kv = (_rms(h_kv, kv_norm_g) @ w_ukv).reshape(B, S, MLA_HEADS, MLA_NOPE + MLA_V)
    k_nope, v = kv[..., :MLA_NOPE], kv[..., MLA_NOPE:]
    pos = jnp.arange(S, dtype=jnp.float32)
    half = MLA_ROPE // 2
    inv = ROPE_BASE ** (-jnp.arange(half, dtype=jnp.float32) / half)
    ang = pos[:, None] * inv[None, :]
    cos, sin = jnp.cos(ang), jnp.sin(ang)
    q_rot = _rope(q_rot, cos[:, None, :], sin[:, None, :])
    k_rot = _rope(h_kr, cos, sin)
    scale = (MLA_NOPE + MLA_ROPE) ** -0.5
    nb = S // Q_BLOCK

    def to_blocks(t):
        return jnp.moveaxis(t.reshape(B, nb, Q_BLOCK, *t.shape[2:]), 1, 0)

    def attend(blk):
        qn, qr = blk
        s = (jnp.einsum('bqhd,bkhd->bhqk', qn, k_nope)
             + jnp.einsum('bqhr,bkr->bhqk', qr, k_rot)).astype(jnp.float32) * scale
        p = jax.nn.softmax(s, axis=-1).astype(v.dtype)
        return jnp.einsum('bhqk,bkhd->bqhd', p, v)

    o = lax.map(attend, (to_blocks(q_nope), to_blocks(q_rot)))
    return jnp.moveaxis(o, 0, 1).reshape(B, S, MLA_HEADS * MLA_V)

def _hyena_filters(L, w1, b1, freq, w2, b2, w3, b3, decay):
    f32 = jnp.float32
    t = jnp.arange(L, dtype=f32)
    t01 = t / L
    bands = jnp.linspace(1e-4, HY_BANDS - 1, HY_BANDS, dtype=f32)
    ang = 2.0 * math.pi * t[:, None] * bands[None, :] / L
    z = jnp.concatenate([t01[:, None], jnp.cos(ang), -jnp.sin(ang)], axis=-1)
    fr = freq.astype(f32)
    h = jnp.sin(fr[0] * (z @ w1.astype(f32) + b1.astype(f32)))
    h = jnp.sin(fr[1] * (h @ w2.astype(f32) + b2.astype(f32)))
    h = h @ w3.astype(f32) + b3.astype(f32)
    h = h * jnp.exp(-t01[:, None] * jnp.abs(decay.astype(f32))[None, :])
    h = h.reshape(L, HY_ORDER, HY_DIRS, HY_WIDTH)
    fwd, bwd = h[:, :, 0], h[:, :, 1]
    k = jnp.concatenate([fwd, jnp.zeros((1, HY_ORDER, HY_WIDTH), f32), bwd[:0:-1]], axis=0)
    return jnp.fft.rfft(k, axis=0)

def _hyena(u, conv_w, conv_b, kf, skip):
    B, S, _ = u.shape
    up = jnp.pad(u, ((0, 0), (1, 1), (0, 0)))
    u = up[:, :-2] * conv_w[0] + up[:, 1:-1] * conv_w[1] + up[:, 2:] * conv_w[2] + conv_b
    x1, x2, v = jnp.split(u, 3, axis=-1)
    gates = (x1, x2)
    z = v.astype(jnp.float32)
    for n in range(HY_ORDER):
        zf = jnp.fft.rfft(z, n=2 * S, axis=1)
        conv = jnp.fft.irfft(zf * kf[None, :, n], n=2 * S, axis=1)[:, :S]
        z = gates[n].astype(jnp.float32) * (conv + skip[n].astype(jnp.float32) * z)
    return z.astype(u.dtype)

def _mem_xattn(hx, hm, w_mq, w_mkv, w_mo):
    B, S, _ = hx.shape
    M = hm.shape[1]
    q = (hx @ w_mq).reshape(B, S, MEM_HEADS, MEM_HEAD_DIM)
    k, v = jnp.split(hm @ w_mkv, 2, axis=-1)
    k = k.reshape(B, M, MEM_HEADS, MEM_HEAD_DIM)
    v = v.reshape(B, M, MEM_HEADS, MEM_HEAD_DIM)
    s = jnp.einsum('bshd,bmhd->bhsm', q, k).astype(jnp.float32) * MEM_HEAD_DIM ** -0.5
    p = jax.nn.softmax(s, axis=-1).astype(v.dtype)
    o = jnp.einsum('bhsm,bmhd->bshd', p, v).reshape(B, S, MEM_HEADS * MEM_HEAD_DIM)
    return o @ w_mo

def _hier_moe(h, w_rg, b_rg, w_re, b_re, w_gate, w_up, w_down):
    B, S, D = h.shape
    t = h.reshape(B * S, D)
    g_logits = (t @ w_rg).astype(jnp.float32) + b_rg.astype(jnp.float32)
    g_prob = jax.nn.softmax(g_logits, axis=-1)
    _, g_idx = lax.top_k(g_logits, 1)
    p_group = jnp.take_along_axis(g_prob, g_idx, axis=1)
    e_logits = ((t @ w_re).astype(jnp.float32) + b_re.astype(jnp.float32)).reshape(-1, N_GROUPS, EXPERTS_PER_GROUP)
    e_in = jnp.take_along_axis(e_logits, g_idx[:, :, None], axis=1)[:, 0]
    top_v, top_i = lax.top_k(e_in, TOP_K_IN_GROUP)
    p_exp = jax.nn.softmax(top_v, axis=-1)
    w_e = jnp.sum(jax.nn.one_hot(top_i, EXPERTS_PER_GROUP, dtype=jnp.float32) * p_exp[..., None], axis=1)
    combine = ((p_group * w_e)[:, None, :]
               * jax.nn.one_hot(g_idx[:, 0], N_GROUPS, dtype=jnp.float32)[:, :, None]).astype(t.dtype)
    y = jnp.zeros_like(t)
    for g in range(N_GROUPS):
        a = jnp.einsum('td,edf->tef', t, w_gate[g])
        b = jnp.einsum('td,edf->tef', t, w_up[g])
        m = jax.nn.silu(a) * b * combine[:, g, :, None]
        y = y + jnp.einsum('tef,efd->td', m, w_down[g])
    return y.reshape(B, S, D)

def first_inputs(seed: int = 0) -> dict:
    key = jax.random.key(seed)
    ks = iter(jax.random.split(key, 40))
    f32 = jnp.float32
    L_ = DEPTH

    def nrm(shape, fan_in, scale=1.0):
        return jax.random.normal(next(ks), shape, f32) * (scale * fan_in ** -0.5)

    def gain(shape):
        return 1.0 + 0.02 * jax.random.normal(next(ks), shape, f32)

    def small(shape, s=0.02):
        return s * jax.random.normal(next(ks), shape, f32)

    G, E, F = N_GROUPS, EXPERTS_PER_GROUP, D_EXPERT
    d_min = math.log(1.0 / HY_TARGET) / HY_SLOW_PCT
    d_max = math.log(1.0 / HY_TARGET) / HY_FAST_PCT
    return {
        "x": jax.random.normal(next(ks), (BATCH, SEQ, D_MODEL), f32),
        "mem": jax.random.normal(next(ks), (BATCH, MEM_TOKENS, D_MODEL), f32),
        "mix_norm_g": gain((L_, D_MODEL)),
        "w_in": nrm((L_, D_MODEL, IN_COLS), D_MODEL),
        "q_norm_g": gain((L_, MLA_Q_RANK)),
        "kv_norm_g": gain((L_, MLA_KV_RANK)),
        "w_uq": nrm((L_, MLA_Q_RANK, MLA_HEADS * (MLA_NOPE + MLA_ROPE)), MLA_Q_RANK),
        "w_ukv": nrm((L_, MLA_KV_RANK, MLA_HEADS * (MLA_NOPE + MLA_V)), MLA_KV_RANK),
        "hy_conv_w": nrm((L_, 3, 3 * HY_WIDTH), 3),
        "hy_conv_b": small((L_, 3 * HY_WIDTH)),
        "hy_w1": nrm((L_, HY_EMB, HY_FFN), HY_EMB),
        "hy_b1": small((L_, HY_FFN), 0.1),
        "hy_freq": gain((L_, 2, HY_FFN)),
        "hy_w2": nrm((L_, HY_FFN, HY_FFN), HY_FFN),
        "hy_b2": small((L_, HY_FFN), 0.1),
        "hy_w3": nrm((L_, HY_FFN, HY_ORDER * HY_DIRS * HY_WIDTH), HY_FFN, 0.1),
        "hy_b3": small((L_, HY_ORDER * HY_DIRS * HY_WIDTH), 0.01),
        "hy_decay": jax.random.uniform(next(ks), (L_, HY_ORDER * HY_DIRS * HY_WIDTH), f32, d_min, d_max),
        "hy_skip": jax.random.normal(next(ks), (L_, HY_ORDER, HY_WIDTH), f32),
        "attn_out_g": gain((L_, MLA_HEADS * MLA_V)),
        "hy_out_g": gain((L_, HY_WIDTH)),
        "w_out": nrm((L_, D_MODEL, D_MODEL), D_MODEL),
        "cross_norm_g": gain((L_, D_MODEL)),
        "mem_norm_g": gain((L_, D_MODEL)),
        "w_mq": nrm((L_, D_MODEL, MEM_HEADS * MEM_HEAD_DIM), D_MODEL),
        "w_mkv": nrm((L_, D_MODEL, 2 * MEM_HEADS * MEM_HEAD_DIM), D_MODEL),
        "w_mo": nrm((L_, MEM_HEADS * MEM_HEAD_DIM, D_MODEL), MEM_HEADS * MEM_HEAD_DIM),
        "ffn_norm_g": gain((L_, D_MODEL)),
        "w_route_group": nrm((L_, D_MODEL, G), D_MODEL),
        "b_route_group": small((L_, G), 0.01),
        "w_route_expert": nrm((L_, D_MODEL, G * E), D_MODEL),
        "b_route_expert": small((L_, G * E), 0.01),
        "w_gate": nrm((L_, G, E, D_MODEL, F), D_MODEL),
        "w_up": nrm((L_, G, E, D_MODEL, F), D_MODEL),
        "w_down": nrm((L_, G, E, F, D_MODEL), F),
        "final_norm_g": gain((D_MODEL,)),
    }

def first_block(x, mem, mix_norm_g, w_in, q_norm_g, kv_norm_g, w_uq, w_ukv, hy_conv_w, hy_conv_b,
              hy_w1, hy_b1, hy_freq, hy_w2, hy_b2, hy_w3, hy_b3, hy_decay, hy_skip, attn_out_g, hy_out_g,
              w_out, cross_norm_g, mem_norm_g, w_mq, w_mkv, w_mo, ffn_norm_g, w_route_group, b_route_group,
              w_route_expert, b_route_expert, w_gate, w_up, w_down, final_norm_g):
    S = x.shape[1]
    for l in range(DEPTH):
        h = _rms(x, mix_norm_g[l])
        p = h @ w_in[l]
        a_out = _mla(p[..., OFF_Q:OFF_KV], p[..., OFF_KV:OFF_KR], p[..., OFF_KR:OFF_HY],
                     q_norm_g[l], kv_norm_g[l], w_uq[l], w_ukv[l])
        kf = _hyena_filters(S, hy_w1[l], hy_b1[l], hy_freq[l], hy_w2[l], hy_b2[l], hy_w3[l], hy_b3[l], hy_decay[l])
        h_out = _hyena(p[..., OFF_HY:], hy_conv_w[l], hy_conv_b[l], kf, hy_skip[l])
        mixed = jnp.concatenate([_rms(a_out, attn_out_g[l]), _rms(h_out, hy_out_g[l])], axis=-1)
        x = x + mixed @ w_out[l]
        x = x + _mem_xattn(_rms(x, cross_norm_g[l]), _rms(mem, mem_norm_g[l]), w_mq[l], w_mkv[l], w_mo[l])
        x = x + _hier_moe(_rms(x, ffn_norm_g[l]), w_route_group[l], b_route_group[l], w_route_expert[l],
                          b_route_expert[l], w_gate[l], w_up[l], w_down[l])
    return _rms(x, final_norm_g)


D_MIX = D_MODEL
D_LRU = D_MIX // 2
D_ATTN = D_MIX - D_LRU
N_LRU_BLOCKS = 8
LRU_BLOCK = D_LRU // N_LRU_BLOCKS
CONV_WIDTH = 4
LRU_C = 8.0
N_HEADS = 8
HEAD_DIM = D_ATTN // N_HEADS
MOBA_BLOCK = 256
MOBA_TOPK = 3
Q_CHUNK = 32
REL_BUCKETS = 32
REL_MAX_DIST = 128
N_EXPERTS = N_GROUPS * EXPERTS_PER_GROUP
EXPERT_TOPK = 2
MOE_ROWS = 128
LN_EPS = 1e-5
DEEPNORM_ALPHA = (2.0 * DEPTH) ** 0.25
DEEPNORM_BETA = (8.0 * DEPTH) ** -0.25
N_MOD = 6
D_IN_PROJ = 2 * D_LRU + 3 * D_ATTN


def _normalize(x):
    xf = x.astype(jnp.float32)
    mu = jnp.mean(xf, axis=-1, keepdims=True)
    var = jnp.mean(jnp.square(xf - mu), axis=-1, keepdims=True)
    return (xf - mu) * lax.rsqrt(var + LN_EPS)

def layernorm(x, g, b):
    return (_normalize(x) * g + b).astype(x.dtype)

def rmsnorm(x, g):
    xf = x.astype(jnp.float32)
    y = xf * lax.rsqrt(jnp.mean(jnp.square(xf), axis=-1, keepdims=True) + LN_EPS)
    return (y * g).astype(x.dtype)

def modulate(x, shift, scale):
    return (_normalize(x) * (1.0 + scale) + shift).astype(x.dtype)

def causal_depthwise_conv(x, w, b):
    s = x.shape[1]
    xp = jnp.pad(x, ((0, 0), (CONV_WIDTH - 1, 0), (0, 0)))
    return sum(w[k] * xp[:, k:k + s] for k in range(CONV_WIDTH)) + b

def rg_lru(xc, w_a, b_a, w_x, b_x, lam):
    bsz, s, _ = xc.shape
    xb = xc.reshape(bsz, s, N_LRU_BLOCKS, LRU_BLOCK)
    r = jax.nn.sigmoid(jnp.einsum('bsni,nij->bsnj', xb, w_a) + b_a).reshape(bsz, s, D_LRU)
    i = jax.nn.sigmoid(jnp.einsum('bsni,nij->bsnj', xb, w_x) + b_x).reshape(bsz, s, D_LRU)
    log_a = -LRU_C * r.astype(jnp.float32) * jax.nn.softplus(-lam.astype(jnp.float32))
    a = jnp.exp(log_a)
    mult = jnp.sqrt(-jnp.expm1(2.0 * log_a))
    u = mult * (i * xc).astype(jnp.float32)

    def combine(left, right):
        a1, b1 = left
        a2, b2 = right
        return a1 * a2, a2 * b1 + b2

    _, h = lax.associative_scan(combine, (a, u), axis=1)
    return h.astype(xc.dtype)

def t5_bucket(rel):
    n = jnp.maximum(rel, 0)
    max_exact = REL_BUCKETS // 2
    large = max_exact + (jnp.log(jnp.maximum(n, 1).astype(jnp.float32) / max_exact)
                         / math.log(REL_MAX_DIST / max_exact)
                         * (REL_BUCKETS - max_exact)).astype(jnp.int32)
    large = jnp.minimum(large, REL_BUCKETS - 1)
    return jnp.where(n < max_exact, n, large)

def moba_attention(q, k, v, rel_bias):
    bsz, s, h, dh = q.shape
    nb = -(-s // MOBA_BLOCK)
    sp = nb * MOBA_BLOCK
    pad = ((0, 0), (0, sp - s), (0, 0), (0, 0))
    qp = jnp.pad(q, pad).transpose(0, 2, 1, 3)
    kp = jnp.pad(k, pad).transpose(0, 2, 1, 3)
    vp = jnp.pad(v, pad).transpose(0, 2, 1, 3)
    scale = HEAD_DIM ** -0.5
    k_blocks = kp.reshape(bsz, h, nb, MOBA_BLOCK, dh)
    v_blocks = vp.reshape(bsz, h, nb, MOBA_BLOCK, dh)
    k_mean = jnp.mean(k_blocks, axis=3)

    own_all = jnp.arange(sp) // MOBA_BLOCK
    past = jnp.arange(nb)[None, :] < own_all[:, None]
    gate = jnp.einsum('bhqd,bhnd->bhqn', qp, k_mean).astype(jnp.float32)
    gate = jnp.where(past, gate, -jnp.inf)
    if nb < MOBA_TOPK:
        gate = jnp.pad(gate, ((0, 0), (0, 0), (0, 0), (0, MOBA_TOPK - nb)), constant_values=-jnp.inf)
    _, sel = lax.top_k(gate, MOBA_TOPK)

    table_h = rel_bias.T
    b_idx = jnp.arange(bsz)
    h_idx = jnp.arange(h)
    kv_offsets = jnp.arange(MOBA_BLOCK)

    def chunk(ci):
        start = ci * Q_CHUNK
        qc = lax.dynamic_slice_in_dim(qp, start, Q_CHUNK, axis=2)
        selc = lax.dynamic_slice_in_dim(sel, start, Q_CHUNK, axis=2)
        qpos = start + jnp.arange(Q_CHUNK)
        own = start // MOBA_BLOCK
        valid = selc < own
        selg = jnp.minimum(selc, nb - 1)
        kg = k_blocks[b_idx[:, None, None, None], h_idx[None, :, None, None], selg]
        vg = v_blocks[b_idx[:, None, None, None], h_idx[None, :, None, None], selg]
        kpos_p = selg[..., None] * MOBA_BLOCK + kv_offsets
        s_p = jnp.einsum('bhqd,bhqnkd->bhqnk', qc, kg).astype(jnp.float32) * scale
        s_p = s_p + table_h[h_idx[None, :, None, None, None], t5_bucket(qpos[:, None, None] - kpos_p)]
        s_p = jnp.where(valid[..., None], s_p, -jnp.inf)
        ko = lax.dynamic_slice_in_dim(kp, own * MOBA_BLOCK, MOBA_BLOCK, axis=2)
        vo = lax.dynamic_slice_in_dim(vp, own * MOBA_BLOCK, MOBA_BLOCK, axis=2)
        rel_o = qpos[:, None] - (own * MOBA_BLOCK + kv_offsets)[None, :]
        s_o = jnp.einsum('bhqd,bhkd->bhqk', qc, ko).astype(jnp.float32) * scale
        s_o = s_o + table_h[:, t5_bucket(rel_o)]
        s_o = jnp.where(rel_o >= 0, s_o, -jnp.inf)
        logits = jnp.concatenate([s_p.reshape(bsz, h, Q_CHUNK, MOBA_TOPK * MOBA_BLOCK), s_o], axis=-1)
        p = jax.nn.softmax(logits, axis=-1)
        p_p = p[..., :MOBA_TOPK * MOBA_BLOCK].reshape(bsz, h, Q_CHUNK, MOBA_TOPK, MOBA_BLOCK).astype(v.dtype)
        p_o = p[..., MOBA_TOPK * MOBA_BLOCK:].astype(v.dtype)
        return (jnp.einsum('bhqnk,bhqnkd->bhqd', p_p, vg)
                + jnp.einsum('bhqk,bhkd->bhqd', p_o, vo))

    outs = lax.map(chunk, jnp.arange(sp // Q_CHUNK))
    out = outs.transpose(1, 2, 0, 3, 4).reshape(bsz, h, sp, dh)[:, :, :s]
    return out.transpose(0, 2, 1, 3).reshape(bsz, s, h * dh)

def hybrid_mixer(u, w_in, conv_w, conv_b, w_gate_a, b_gate_a, w_gate_x, b_gate_x,
                 lru_lambda, rel_bias, norm_lru_g, norm_attn_g, w_out):
    bsz, s, _ = u.shape
    proj = u @ w_in
    x_lru, y_lru, q, k, v = jnp.split(
        proj, [D_LRU, 2 * D_LRU, 2 * D_LRU + D_ATTN, 2 * D_LRU + 2 * D_ATTN], axis=-1)
    h = rg_lru(causal_depthwise_conv(x_lru, conv_w, conv_b),
               w_gate_a, b_gate_a, w_gate_x, b_gate_x, lru_lambda)
    lru_out = h * jax.nn.gelu(y_lru)
    attn_out = moba_attention(q.reshape(bsz, s, N_HEADS, HEAD_DIM),
                              k.reshape(bsz, s, N_HEADS, HEAD_DIM),
                              v.reshape(bsz, s, N_HEADS, HEAD_DIM), rel_bias)
    merged = jnp.concatenate([rmsnorm(lru_out, norm_lru_g), rmsnorm(attn_out, norm_attn_g)], axis=-1)
    return merged @ w_out

def hierarchical_moe(u, w_rg, b_rg, w_re, b_re, w1, w3, w2):
    bsz, s, d = u.shape
    nc = s // MOE_ROWS
    xt = u.reshape(bsz, nc, MOE_ROWS, d).transpose(1, 0, 2, 3).reshape(nc, bsz * MOE_ROWS, d)

    def body(xc):
        g_prob = jax.nn.softmax((xc @ w_rg + b_rg).astype(jnp.float32), axis=-1)
        g_top, g_idx = lax.top_k(g_prob, 1)
        e_logits = (xc @ w_re + b_re).astype(jnp.float32).reshape(-1, N_GROUPS, EXPERTS_PER_GROUP)
        e_in = jnp.take_along_axis(e_logits, g_idx[:, :, None], axis=1)[:, 0]
        e_top, e_loc = lax.top_k(jax.nn.softmax(e_in, axis=-1), EXPERT_TOPK)
        e_top = e_top / jnp.sum(e_top, axis=-1, keepdims=True)
        weights = g_top * e_top
        e_glob = g_idx * EXPERTS_PER_GROUP + e_loc
        gate = jnp.sum(jax.nn.one_hot(e_glob, N_EXPERTS, dtype=jnp.float32) * weights[..., None], axis=1)
        hdn = jax.nn.silu(jnp.einsum('td,edf->tef', xc, w1)) * jnp.einsum('td,edf->tef', xc, w3)
        return jnp.einsum('tef,efd->td', hdn * gate[:, :, None].astype(hdn.dtype), w2)

    ys = lax.map(body, xt)
    return ys.reshape(nc, bsz, MOE_ROWS, d).transpose(1, 0, 2, 3).reshape(bsz, s, d)

def second_inputs(seed: int = 0) -> dict:
    key = jax.random.key(seed)
    ks = jax.random.split(key, 28)
    f32 = jnp.float32
    L = DEPTH

    def nrm(k, shape, scale):
        return jax.random.normal(k, shape, f32) * scale

    a_c = jax.random.uniform(ks[11], (L, D_LRU), f32, 0.9, 0.999)
    a_base = a_c ** (1.0 / LRU_C)
    return {
        'x': nrm(ks[0], (BATCH, SEQ, D_MODEL), 1.0),
        'c': nrm(ks[1], (BATCH, D_MODEL), 1.0),
        'w_ada': nrm(ks[2], (L, D_MODEL, N_MOD * D_MODEL), 0.5 * D_MODEL ** -0.5),
        'b_ada': nrm(ks[3], (L, N_MOD * D_MODEL), 0.02),
        'w_in': nrm(ks[4], (L, D_MODEL, D_IN_PROJ), D_MODEL ** -0.5),
        'conv_w': nrm(ks[5], (L, CONV_WIDTH, D_LRU), CONV_WIDTH ** -0.5),
        'conv_b': nrm(ks[6], (L, D_LRU), 0.02),
        'w_gate_a': nrm(ks[7], (L, N_LRU_BLOCKS, LRU_BLOCK, LRU_BLOCK), LRU_BLOCK ** -0.5),
        'b_gate_a': nrm(ks[8], (L, N_LRU_BLOCKS, LRU_BLOCK), 0.02),
        'w_gate_x': nrm(ks[9], (L, N_LRU_BLOCKS, LRU_BLOCK, LRU_BLOCK), LRU_BLOCK ** -0.5),
        'b_gate_x': nrm(ks[10], (L, N_LRU_BLOCKS, LRU_BLOCK), 0.02),
        'lru_lambda': jnp.log(a_base) - jnp.log1p(-a_base),
        'rel_bias': nrm(ks[12], (REL_BUCKETS, N_HEADS), 0.5),
        'norm_lru_g': 1.0 + nrm(ks[13], (L, D_LRU), 0.05),
        'norm_attn_g': 1.0 + nrm(ks[14], (L, D_ATTN), 0.05),
        'w_out': nrm(ks[15], (L, D_MIX, D_MODEL), DEEPNORM_BETA * D_MIX ** -0.5),
        'ln1_g': 1.0 + nrm(ks[16], (L, D_MODEL), 0.05),
        'ln1_b': nrm(ks[17], (L, D_MODEL), 0.02),
        'w_router_group': nrm(ks[18], (L, D_MODEL, N_GROUPS), D_MODEL ** -0.5),
        'b_router_group': nrm(ks[19], (L, N_GROUPS), 0.01),
        'w_router_expert': nrm(ks[20], (L, D_MODEL, N_EXPERTS), D_MODEL ** -0.5),
        'b_router_expert': nrm(ks[21], (L, N_EXPERTS), 0.01),
        'w1': nrm(ks[22], (L, N_EXPERTS, D_MODEL, D_EXPERT), D_MODEL ** -0.5),
        'w3': nrm(ks[23], (L, N_EXPERTS, D_MODEL, D_EXPERT), D_MODEL ** -0.5),
        'w2': nrm(ks[24], (L, N_EXPERTS, D_EXPERT, D_MODEL), DEEPNORM_BETA * D_EXPERT ** -0.5),
        'ln2_g': 1.0 + nrm(ks[25], (L, D_MODEL), 0.05),
        'ln2_b': nrm(ks[26], (L, D_MODEL), 0.02),
    }

def second_block(x, c, w_ada, b_ada, w_in, conv_w, conv_b, w_gate_a, b_gate_a, w_gate_x, b_gate_x,
              lru_lambda, rel_bias, norm_lru_g, norm_attn_g, w_out, ln1_g, ln1_b,
              w_router_group, b_router_group, w_router_expert, b_router_expert,
              w1, w3, w2, ln2_g, ln2_b):
    bsz, _, d = x.shape
    silu_c = jax.nn.silu(c)
    for l in range(DEPTH):
        mod = (silu_c @ w_ada[l] + b_ada[l]).reshape(bsz, N_MOD, d)
        sh1, sc1, g1, sh2, sc2, g2 = [mod[:, j, None, :] for j in range(N_MOD)]
        u = modulate(x, sh1, sc1)
        mix = hybrid_mixer(u, w_in[l], conv_w[l], conv_b[l], w_gate_a[l], b_gate_a[l],
                           w_gate_x[l], b_gate_x[l], lru_lambda[l], rel_bias,
                           norm_lru_g[l], norm_attn_g[l], w_out[l])
        x = layernorm(DEEPNORM_ALPHA * x + g1 * mix, ln1_g[l], ln1_b[l])
        u2 = modulate(x, sh2, sc2)
        ffn = hierarchical_moe(u2, w_router_group[l], b_router_group[l], w_router_expert[l],
                               b_router_expert[l], w1[l], w3[l], w2[l])
        x = layernorm(DEEPNORM_ALPHA * x + g2 * ffn, ln2_g[l], ln2_b[l])
    return x


def setup_inputs(seed=0):
    out = dict(first_inputs(seed))
    for name, value in second_inputs(seed + 1).items():
        if name != "x":
            out[name + "_2"] = value
    return out


def reference(
    x, mem, mix_norm_g, w_in, q_norm_g, kv_norm_g, w_uq, w_ukv, hy_conv_w, hy_conv_b, hy_w1,
    hy_b1, hy_freq, hy_w2, hy_b2, hy_w3, hy_b3, hy_decay, hy_skip, attn_out_g, hy_out_g, w_out,
    cross_norm_g, mem_norm_g, w_mq, w_mkv, w_mo, ffn_norm_g, w_route_group, b_route_group,
    w_route_expert, b_route_expert, w_gate, w_up, w_down, final_norm_g, c_2, w_ada_2, b_ada_2,
    w_in_2, conv_w_2, conv_b_2, w_gate_a_2, b_gate_a_2, w_gate_x_2, b_gate_x_2, lru_lambda_2,
    rel_bias_2, norm_lru_g_2, norm_attn_g_2, w_out_2, ln1_g_2, ln1_b_2, w_router_group_2,
    b_router_group_2, w_router_expert_2, b_router_expert_2, w1_2, w3_2, w2_2, ln2_g_2, ln2_b_2,
):
    x = first_block(
        x, mem, mix_norm_g, w_in, q_norm_g, kv_norm_g, w_uq, w_ukv, hy_conv_w, hy_conv_b, hy_w1,
        hy_b1, hy_freq, hy_w2, hy_b2, hy_w3, hy_b3, hy_decay, hy_skip, attn_out_g, hy_out_g,
        w_out, cross_norm_g, mem_norm_g, w_mq, w_mkv, w_mo, ffn_norm_g, w_route_group,
        b_route_group, w_route_expert, b_route_expert, w_gate, w_up, w_down, final_norm_g,
    )
    return second_block(
        x, c_2, w_ada_2, b_ada_2, w_in_2, conv_w_2, conv_b_2, w_gate_a_2, b_gate_a_2,
        w_gate_x_2, b_gate_x_2, lru_lambda_2, rel_bias_2, norm_lru_g_2, norm_attn_g_2, w_out_2,
        ln1_g_2, ln1_b_2, w_router_group_2, b_router_group_2, w_router_expert_2,
        b_router_expert_2, w1_2, w3_2, w2_2, ln2_g_2, ln2_b_2,
    )


_drawn_inputs = setup_inputs


def setup_inputs(seed=0):
    import zlib

    import numpy as np

    out = dict(_drawn_inputs(seed))
    spreads = {}
    factors = {'q_norm_g': 2.975,
     'hy_freq': 5.737,
     'attn_out_g': 3.166,
     'hy_out_g': 2.954,
     'cross_norm_g': 8.0,
     'mem_norm_g': 5.685,
     'ffn_norm_g': 3.702,
     'b_route_group': 7.656,
     'b_route_expert': 4.25,
     'final_norm_g': 20.798,
     'b_ada_2': 3.617,
     'conv_b_2': 8.0,
     'w_gate_a_2': 3.259,
     'b_gate_a_2': 64.0,
     'b_gate_x_2': 23.312,
     'rel_bias_2': 2.814,
     'norm_lru_g_2': 94.589,
     'norm_attn_g_2': 79.118,
     'ln1_b_2': 2.69,
     'b_router_group_2': 38.42,
     'b_router_expert_2': 60.756,
     'ln2_b_2': 2.76}
    for name, (base, spread) in spreads.items():
        noise = np.random.default_rng([zlib.crc32(name.encode()), seed]).standard_normal(out[name].shape)
        drawn = base * np.exp(spread * noise) if base else spread * noise
        out[name] = __import__('jax').numpy.asarray(drawn.astype(out[name].dtype))
    for name, factor in factors.items():
        out[name] = (out[name] * factor).astype(out[name].dtype)
    return out
```

```python
from contextlib import ExitStack

import concourse.bass as bass
import numpy as np
from concourse import mybir

F32 = mybir.dt.float32
I32 = mybir.dt.int32
ALU = mybir.AluOpType
ACT = mybir.ActivationFunctionType
AXX = mybir.AxisListType.X

P = 128
S = 256
D = 1024
KD = D // P
TT = S // P
H1, NOPE, ROPE, VD = 8, 64, 32, 64
QR, KVR = 256, 128
LAT = QR + KVR + ROPE
HW = 512
ORDER = 2
EMB, FFN = 33, 64
XH, XHD = 4, 256
G, EPG = 4, 8
NE = G * EPG
FE = 256
NPAIR = 2 * S
WIN = 64
SORTED = NPAIR + WIN
NX = NPAIR // WIN
RING = 4
SLOT = 3 * KD * FE
EPS1, EPS2 = 1e-6, 1e-5
ALPHA = float(2.0 ** 0.25)
LRU_C = 8.0
BUCKETS, MAX_DIST = 32, 128
BW = S + P
NEG = -1e30
TWO_PI = 2 * np.pi
PI_HI = 6.28125
PI_LO = float(TWO_PI - PI_HI)
MAGIC = 12582912.0
PI_IN = 3.1415925

COLS = [("mix_norm_g", 8), ("q_norm_g", 2), ("kv_norm_g", 1), ("hy_conv_w", 36), ("hy_conv_b", 12),
        ("attn_out_g", 4), ("hy_out_g", 4), ("cross_norm_g", 8), ("mem_norm_g", 8), ("ffn_norm_g", 8),
        ("c_2", 8), ("b_ada_2", 48), ("conv_w_2", 16), ("conv_b_2", 4), ("b_gate_a_2", 4),
        ("b_gate_x_2", 4), ("lru_lambda_2", 4), ("norm_lru_g_2", 4), ("norm_attn_g_2", 4),
        ("hy_b1", 1), ("hy_b2", 1), ("hy_freq", 2)]
COL_AT, _n = {}, 0
for _name, _w in COLS:
    COL_AT[_name] = _n
    _n += _w
NCOL = _n

TABS = [("ident", P), ("stack", WIN), ("ones", P), ("tri", P), ("iota", NPAIR), ("g99", G), ("e99", EPG),
        ("eid", NE), ("negt", TT), ("tmask", TT), ("kcos", TT * ROPE), ("ksin", TT * ROPE), ("qtab", S)]
TAB_AT, _n = {}, 0
for _name, _w in TABS:
    TAB_AT[_name] = _n
    _n += _w
NTAB = _n


def _tables():
    f = np.float32
    t = np.zeros((P, NTAB), f)

    def put(name, v):
        v = np.asarray(v, f)
        t[:v.shape[0], TAB_AT[name]:TAB_AT[name] + v.shape[1]] = v

    p = np.arange(P)
    put("ident", np.eye(P))
    put("stack", p[:, None] % WIN == np.arange(WIN)[None, :])
    put("ones", np.ones((P, P)))
    put("tri", p[:, None] < p[None, :])
    put("iota", np.tile(np.arange(NPAIR), (P, 1)))
    put("g99", np.tile(np.arange(G) - 99.0, (P, 1)))
    put("e99", np.tile(np.arange(EPG) - 99.0, (P, 1)))
    put("eid", np.tile(np.arange(NE), (P, 1)))
    tok = np.arange(TT)[None, :] * P + p[:, None]
    put("negt", -(tok / S))
    put("tmask", tok != 0)
    half = ROPE // 2
    inv = f(10000.0) ** (-np.arange(half, dtype=f) / f(half))
    ang = np.arange(S, dtype=f)[:, None] * inv[None, :]
    cos, sin = np.cos(ang.astype(np.float64)), np.sin(ang.astype(np.float64))
    c2 = np.concatenate([cos, cos], 1).reshape(TT, P, ROPE).transpose(1, 0, 2)
    s2 = np.concatenate([-sin, sin], 1).reshape(TT, P, ROPE).transpose(1, 0, 2)
    put("kcos", c2.reshape(P, -1))
    put("ksin", s2.reshape(P, -1))
    scale = (NOPE + ROPE) ** -0.5
    put("qtab", np.concatenate([np.full((NOPE, S), scale), scale * cos.T, scale * cos.T,
                                -scale * sin.T, scale * sin.T], 0))
    tt, ff = np.arange(S)[:, None], np.arange(S)[None, :]
    th = 2 * np.pi * tt * ff / (2 * S)
    alt = (-1.0) ** np.arange(S)
    cosm, sinm = np.cos(th), -np.sin(th)
    packed = sinm.copy()
    packed[:, 0] = alt
    cos0 = cosm[:, :P].copy()
    cos0[:, 0] = alt
    inv_c, inv_s = 2 * np.cos(th.T) / (2 * S), -2 * np.sin(th.T) / (2 * S)
    inv_c[0] = 1 / (2 * S)
    inv_s[0] = alt / (2 * S)

    def split(m):
        return m.reshape(TT, P, -1).transpose(1, 0, 2).reshape(P, -1)

    dft = np.concatenate([split(cosm), split(packed), split(inv_c), split(inv_s)], 1).astype(f)
    filt = np.concatenate([split(sinm), split(cos0)], 1).astype(f)
    pos = np.arange(S, dtype=f)
    bands = np.linspace(1e-4, (EMB - 1) // 2 - 1, (EMB - 1) // 2, dtype=f)
    za = (f(2.0 * np.pi) * pos[:, None] * bands[None, :] / f(S)).astype(np.float64)
    z = np.concatenate([(pos / S)[:, None], np.cos(za), -np.sin(za)], 1).T
    feat = np.zeros((P, S), f)
    feat[:EMB] = z
    n = S - 1 - np.arange(2 * S)
    exact = BUCKETS // 2
    large = exact + (np.log(np.maximum(n, 1).astype(f) / f(exact)) / f(np.log(MAX_DIST / exact))
                     * f(BUCKETS - exact)).astype(np.int32)
    bucket = np.where(n < 0, BUCKETS, np.where(n < exact, n, np.minimum(large, BUCKETS - 1)))
    onehot = np.zeros((P, 2 * S), f)
    onehot[bucket, np.arange(2 * S)] = 1
    return t, dft, filt, feat, onehot


UNITS = [("filt", 2048 + 2048 + 512 + 256 + 256 + 64 + 64), ("lat", KD * LAT), ("hya", KD * 768), ("hyb", KD * 768),
         ("mla", 2 * H1 * P + H1 * NOPE + H1 * VD),
         ("mk0", 4096), ("mk1", 4096), ("mv0", 4096), ("mv1", 4096), ("wo0", 4096), ("wo1", 4096),
         ("mq0", 4096), ("mq1", 4096), ("mo0", 4096), ("mo1", 4096)]
UNITS1 = len(UNITS)
UNITS2 = [(f"ada{i}", 4096) for i in range(12)] + [(f"win{i}", 4096) for i in range(5)] \
    + [("wp0", 4096), ("wp1", 4096)]
PLACE = {n: i for i, (n, _) in enumerate(UNITS)}
MOE_AT = [UNITS1, UNITS1 + NE + len(UNITS2)]
PLACE.update({n: UNITS1 + NE + i for i, (n, _) in enumerate(UNITS2)})

STAGES = [("f1", 1), ("hT", 4), ("f2", 1), ("lat", 2), ("hy0", 2), ("f3_0", 4), ("hyT0", 2), ("hy1", 2),
          ("latT", 2), ("sp0", 5), ("hyT1", 2), ("hy2", 2), ("f3_1", 4), ("hyT2", 2), ("sp1", 5),
          ("uq", 4), ("uk", 4), ("uv", 2), ("zs0", 4)]
STAGES += [("sc0", 1), ("sc1", 1)]
for _h in range(H1):
    STAGES += [(f"pT{_h}", 1), (f"pv{_h}", 1)] + ([(f"sc{_h + 2}", 1)] if _h + 2 < H1 else [])
    if _h == 2:
        STAGES += [("cv0", 2)]
    if _h == 5:
        STAGES += [("zs1", 4)]
STAGES += [("cv1", 2), ("memT", 4), ("mk", 4), ("mv", 4), ("mixT", 4), ("wo", 4), ("cT", 4), ("mq", 4),
           ("xs0", 1), ("xs1", 1)]
for _h in range(XH):
    STAGES += [(f"xT{_h}", 1), (f"xv{_h}", 1)] + ([(f"xs{_h + 2}", 1)] if _h + 2 < XH else [])
STAGES += [("mo", 4)]


def _moe_stages(b):
    return [(f"rT{b}", 4), (f"rt{b}", 1), (f"cnt{b}", 1), (f"gx{b}", 8), (f"swT{b}", 2), (f"yT{b}", 8)] \
        + [("g2r", 2)] * (b == 2) + [(f"sct{b}", 4)]


STAGES += _moe_stages(1)
STAGES += [("bias", 1), ("ada0", 1)]
for _i in range(12):
    STAGES += ([(f"ada{_i + 1}", 1)] if _i < 11 else []) + [(f"adac{_i}", 1)]
STAGES += [("g1r", 2), ("uT", 4), ("xl", 2), ("yl", 2), ("ga", 2), ("gx", 2), ("aq", 2), ("ak", 2), ("av", 2)]
STAGES += [("as0", 1), ("as1", 1)]
for _h in range(H1):
    STAGES += [(f"aT{_h}", 1), (f"ap{_h}", 1)] + ([(f"as{_h + 2}", 1)] if _h + 2 < H1 else [])
STAGES += [("lss", 1), ("aoT", 2), ("wp", 8)]
STAGES += _moe_stages(2)
BANK_AT, _n = {}, 0
for _name, _w in STAGES:
    BANK_AT[_name] = (_n, _w)
    _n += _w



LAST = {"filt": ("sp1", 4), "lat": ("lat", 1), "hya": ("hy1", 0), "hyb": ("hy2", 1), "mla": ("uv", 1)}
for _s, _st in (("mk", "mk"), ("mv", "mv"), ("wo", "wo"), ("mq", "mq"), ("mo", "mo")):
    LAST.update({f"{_s}0": (_st, 1), f"{_s}1": (_st, 3)})
LAST.update({f"ada{_i}": (f"ada{_i}", 0) for _i in range(12)})
LAST.update({f"win{_i}": (_st, 1) for _i, _st in enumerate(("xl", "yl", "aq", "ak", "av"))})
LAST.update({"wp0": ("wp", 3), "wp1": ("wp", 7)})


SQUARES = [("x", 2), ("l", 4), ("ao", 2), ("m", 2), ("z", 2), ("c", 2), ("r", 2), ("f", 2), ("a", 2)]
ROOTS = [(_t, 1) for _t in ("x", "lq", "lkv", "ao", "m", "z", "c", "r", "f", "ln0", "a", "lru", "ln1", "ln2", "ln3")]
NORMS = [(_t, 2) for _t in ("xn_x", "ao_n", "xn_m", "z_n", "xn_c", "xn_r1", "xn_u", "ao2_n", "ln1", "xn_r2", "ln2")]


def upto(order, tag, t=None):
    n = 0
    for name, w in order:
        if name == tag:
            return n + (w if t is None else t + 1)
        n += w
    raise KeyError(tag)


def two_blocks(nc, A, out):
    ctx = ExitStack()
    with ctx:
        def sb(name, shape, dt=F32):
            return ctx.enter_context(nc.sbuf_tensor(name, shape, dt))

        made = {}

        def sem(name):
            if name not in made:
                made[name] = ctx.enter_context(nc.semaphore(name))
            return made[name]

        ring = sb("ring", [P, RING, SLOT])
        tab = sb("tab", [P, NTAB])
        col = sb("col", [P, NCOL])
        X = sb("X", [P, TT, D])
        HTf = sb("HT", [P, KD * S])
        XNf = sb("XN", [P, TT * D])
        ROW = sb("ROW", [P, TT * D])
        st = sb("st", [P, 330])
        tabi = sb("tabi", [1, 64], I32)
        wr = sb("wr", [P, 2, KD * (G + NE)])
        keep = sb("keep", [P, 2 * (G + NE) + NE])
        biasr, zero32 = [keep[:, 0:36], keep[:, 36:72]], keep[:, 72:104]
        mod = sb("mod", [P, 48])
        cm = sb("cm", [P, KD, 32])
        AR = 17408
        arena = sb("arena", [P, AR])
        bank = [ctx.enter_context(nc.psum_tensor(f"bank{i}", [P, 512], F32)) for i in range(8)]
        bias_rows = nc.dram_tensor("bias_rows", (H1, P, BW), F32, kind="Internal").ap()

        def three(ap, a):
            return ap.rearrange("p (a b) -> p a b", a=a)

        HT = three(HTf[:, :], KD)
        XN = three(XNf[:, :], TT)

        def T(name, rows=P):
            return tab[0:rows, TAB_AT[name]:TAB_AT[name] + dict(TABS)[name]]

        def C(name, k=0, w=1, rows=P):
            return col[0:rows, COL_AT[name] + k:COL_AT[name] + k + w]

        ident, ones, stack = T("ident"), T("ones"), T("stack")
        used = {"st": 0, "route": 0}

        def stat(n):
            used["st"] += n
            assert used["st"] <= 330
            return st[:, used["st"] - n:used["st"]]

        def area(at, n):
            assert at + n <= AR
            return arena[:, at:at + n]

        dft = area(0, 2048)
        fwd_c, fwd_s = three(dft[:, 0:512], TT), three(dft[:, 512:1024], TT)
        inv_c, inv_s = three(dft[:, 1024:1536], TT), three(dft[:, 1536:2048], TT)
        even, odd = three(area(2048, 1024), TT), three(area(3072, 1024), TT)
        spec_r, spec_i = three(area(2048, 1024), TT), three(area(3072, 1024), TT)
        k_c = [three(area(4096 + 2560 * n, 1024), TT) for n in range(ORDER)]
        k_s = [three(area(5120 + 2560 * n, 1024), TT) for n in range(ORDER)]
        k_c0 = [area(6144 + 2560 * n, 512) for n in range(ORDER)]
        filt_f, filt_b = area(6656, 512), area(7168, 512)
        env = three(area(7680, 1024), 2)
        hytok = area(9216, 3072).rearrange("p (t w c) -> p t w c", t=TT, w=3)
        Z = hytok[:, :, 2, :]
        conv_t = three(area(12288, 1024), 4)
        skip_z = three(area(12288, 1024), TT)
        prod = three(area(13312, 1024), TT)
        krb = three(area(13312, 256), TT)
        arg, turn = area(13568, 256), area(13824, 256)
        lat = three(area(14336, TT * LAT), TT)
        latTb = three(area(15360, 1024), 4)
        h1, h2 = area(16384, 256), area(16640, 256)
        V1 = three(area(16384, 1024), TT)
        junk = area(16384, 1024)
        prob = area(14336, 1024).rearrange("p (i t k) -> p i t k", i=2, t=TT)
        probT = area(15360, 1024).rearrange("p (i t k) -> p i t k", i=2, t=TT)
        QT, KT = three(HTf[:, :], H1), three(XNf[:, :], H1)
        AO, skip = three(ROW[:, 0:1024], TT), three(ROW[:, 1024:2048], ORDER)
        KM, VM = three(area(4096, 2048), KD), three(area(6656, 2048), TT)
        QX, oT = three(area(0, 2048), KD), three(area(2048, 2048), KD)
        xsT, ysT = three(area(0, KD * SORTED), KD), three(area(KD * SORTED, KD * SORTED), KD)
        at = 2 * KD * SORTED
        gu_sb = three(area(at, 1024), 2)
        d_sb = area(at + 1024, 1024)
        xwin = area(at + 2048, 1024).rearrange("p (i k w) -> p i k w", i=2, k=KD)
        sg, hb = three(area(at + 3072, 256), 2), three(area(at + 3328, 128), 2)
        sel, selw = three(area(at + 3584, 1024), TT), three(area(at + 4608, 1024), TT)
        swT = three(area(at + 5632, 1024), NPAIR // P)
        ytok = three(area(0, NPAIR // P * D), NPAIR // P)
        diag2, g2row = three(area(at, 1024), KD), area(at + 1024, 1024)
        oneh, relb, brow = area(at + 3584, 512), area(at + 4096, H1), area(at + 4608, 512)
        route_at = at + 6656

        def route(n):
            used["route"] += n
            assert route_at + used["route"] <= AR
            return area(route_at + used["route"] - n, n)

        BT = three(area(0, 3072), H1)
        xc, rg, ig, aa, th, hh, gy, sq = [three(area(3072 + 1024 * i, 1024), 4) for i in range(8)]
        diag1 = three(area(10240, 1024), KD)
        Q2, K2 = three(area(11264, 1024), 4), three(area(12288, 1024), 4)
        V2 = three(area(13312, 1024), TT)
        adab = three(area(14336, 1024), 2)
        prob2, probT2 = three(area(14336, 768), 2), three(area(15104, 768), 2)
        score = area(15872, 384)
        g1row = area(16256, 1024)
        AO2 = XN[:, :, 0:HW]
        aoT, loT = rg, ig

        def place(stage, j):
            base, n = BANK_AT[stage]
            assert j < n, stage
            return (base + j) % 8, (base + j) // 8

        taken = [0]

        def take(pe, stage, j=0):
            assert BANK_AT[stage][0] + j == taken[0], (stage, j, taken)
            taken[0] += 1
            b, use = place(stage, j)
            if use:
                pe.wait_ge(sem(f"bank_free{b}"), use)
            return bank[b]

        def full(last, stage, j=0):
            last.then_inc(sem(f"bank_full{place(stage, j)[0]}"), 1)

        def got(eng, stage, j=0):
            b, use = place(stage, j)
            eng.wait_ge(sem(f"bank_full{b}"), use + 1)
            return bank[b]

        def free(last, stage, j=0):
            last.then_inc(sem(f"bank_free{place(stage, j)[0]}"), 1)

        def ready(eng, stage, j=0):
            b, use = place(stage, j)
            eng.wait_ge(sem(f"bank_free{b}"), use + 1)

        def slot(i):
            return i % RING

        def arrived(eng, name):
            i = PLACE[name]
            eng.wait_ge(sem(f"slot_full{slot(i)}"), 16 * (i // RING + 1))
            return ring[:, slot(i), :]

        def vacated(sp, i):
            prev = i - RING
            if prev < 0:
                return
            for b, m in enumerate(MOE_AT):
                if m <= prev < m + NE:
                    sp.wait_ge(sem(f"down_done{b + 1}"), prev - m + 1)
                    return
            name = next(n for n, q in PLACE.items() if q == prev)
            stage, j = LAST[name]
            b, use = place(stage, j)
            sp.wait_ge(sem(f"bank_full{b}"), use + 1)

        ssq_x, rstd_x = stat(2), stat(2)
        ssq_l, rstd_l = stat(4), stat(4)
        ssq_m, rstd_m = stat(2), stat(2)
        ssq_o, rstd_o = stat(4), stat(4)
        ssq_c, rstd_c = stat(2), stat(2)
        ssq_r, rstd_r = stat(2), stat(2)
        ssq_f, rstd_f = stat(2), stat(2)
        nmax, rsum, rinv = three(stat(16), H1), three(stat(16), H1), three(stat(16), H1)
        xmax, xsum, xinv = three(stat(8), XH), three(stat(8), XH), three(stat(8), XH)
        amax, asum, ainv = three(stat(16), H1), three(stat(16), H1), three(stat(16), H1)
        bn_ = [[stat(12) for _ in range(TT)] for _ in range(4)]
        mv_ = [three(stat(4), TT) for _ in range(4)]
        rstd_n = [stat(2) for _ in range(4)]
        ssq_a, rstd_a = stat(4), stat(4)
        sp_l, sp8 = stat(28), stat(4)
        sp8n = stat(4)
        half_neg = stat(4)
        L = three(route(72), TT)
        gmx, gex, gsum, pgrp = route(2), three(route(8), TT), route(2), route(2)
        ohg, cand4, i1g = three(route(8), TT), three(route(8), TT), route(2)
        ein, ein2, cand8 = three(route(16), TT), three(route(16), TT), three(route(16), TT)
        spread = route(64).rearrange("p (t g e) -> p t g e", t=TT, g=G)
        m1, m2, i1, i2, ex2, w1, w2 = [route(2) for _ in range(7)]
        oh1, oh2 = three(route(16), TT), three(route(16), TT)
        M1, M2, M12, posm = [three(route(64), TT) for _ in range(4)]
        counts, starts, incl, nx, xincl, xex, cm64 = [route(32) for _ in range(7)]
        pos1, pos2 = route(2), route(2)
        mk8, tm8, mk8b = [three(route(NX * NE), NX) for _ in range(3)]
        xst, xid = route(NX), route(NX)

        block = ctx.enter_context(nc.Block())
        W_MOE = [A["experts"], A["experts_2"]]

        @block.sync
        def _(sp):
            def load(i, src, width):
                vacated(sp, i)
                sp.dma_start(ring[:, slot(i), 0:width], src).then_inc(sem(f"slot_full{slot(i)}"), 16)

            def experts(b):
                base = MOE_AT[b]
                w = W_MOE[b]
                for e in range(RING):
                    load(base + e, w[e], SLOT)
                with sp.Fori(RING, NE - RING + 1, RING) as e0:
                    for r in range(RING):
                        sp.wait_ge(sem(f"down_done{b + 1}"), e0 + (r - RING + 1))
                        sp.dma_start(ring[:, slot(base + r), :],
                                     w[bass.ds(e0 + r, 1)].rearrange("a p f -> p (a f)")
                                     ).then_inc(sem(f"slot_full{slot(base + r)}"), 16)
                s = slot(base)
                sp.wait_ge(sem(f"routed{b + 1}"), 1)
                n = sp.value_load(tabi[0:1, 48:49], min_val=0, max_val=NX - 1)
                sp.wait_ge(sem(f"down_done{b + 1}"), NE - RING + 1)
                with sp.If(n > 0):
                    with sp.Fori(0, n) as j:
                        e = sp.value_load(tabi[0:1, bass.ds(40 + j, 1)], min_val=0, max_val=NE - 1)
                        sp.wait_ge(sem(f"extra_down{b + 1}"), j + 1)
                        sp.dma_start(ring[:, s, :], w[bass.ds(e, 1)].rearrange("a p f -> p (a f)")
                                     ).then_inc(sem(f"extra_w{b + 1}"), 16)
                return n

            for i, (name, width) in enumerate(UNITS):
                load(i, A[name], width)
            n = experts(0)
            for i, (name, width) in enumerate(UNITS2):
                if slot(MOE_AT[0] + NE + i) == slot(MOE_AT[0]) and i < RING:
                    sp.wait_ge(sem("extra_down1"), n + 1)
                load(MOE_AT[0] + NE + i, A[name], width)
            experts(1)
            sp.wait_ge(sem("stored"), 16 * TT)

        @block.tensor
        def _(pe):
            mm, tr = nc.tensor.matmul, nc.tensor.transpose

            def transposed(stage, src, n, ready_sem):
                for j in range(n // 2):
                    ps = take(pe, stage, j)
                    for a in range(2):
                        for t in range(TT):
                            pe.wait_ge(sem("normed"), upto(NORMS, ready_sem, t))
                            last = tr(ps[:, a * S + t * P:a * S + (t + 1) * P],
                                      src[:, t, (2 * j + a) * P:(2 * j + a + 1) * P], ident)
                    full(last, stage, j)

            def all_ready(stage, n):
                for j in range(n):
                    ready(pe, stage, j)

            def token_out(stage, units, src_stage, n_src):
                all_ready(src_stage, n_src)
                for u in range(2):
                    w = three(arrived(pe, units[u])[:, 0:4096], KD)
                    for t in range(TT):
                        ps = take(pe, stage, 2 * u + t)
                        for k in range(KD):
                            last = mm(ps[:, :], HT[:, k, t * P:(t + 1) * P], w[:, k, :], start=k == 0, stop=k == KD - 1)
                        full(last, stage, 2 * u + t)

            def channel_out(stage, units, cols=512):
                j = 0
                for name in units:
                    w = three(arrived(pe, name)[:, 0:KD * cols], KD)
                    for i in range(cols // P // 2):
                        ps = take(pe, stage, j)
                        for a in range(2):
                            c = (2 * i + a) * P
                            for k in range(KD):
                                last = mm(ps[:, a * S:(a + 1) * S], w[:, k, c:c + P], HT[:, k, :],
                                          start=k == 0, stop=k == KD - 1)
                        full(last, stage, j)
                        j += 1

            pe.wait_ge(sem("tab"), 32)
            fw = arrived(pe, "filt")
            w3, sin_m, cos_0 = fw[:, 0:2048], three(fw[:, 4096:4608], TT), three(fw[:, 4608:4864], TT)
            feat, fw1, fw2 = fw[0:EMB, 4864:5120], fw[0:EMB, 5120:5184], fw[0:FFN, 5184:5248]
            ps = take(pe, "f1")
            full(mm(ps[0:FFN, 0:S], fw1, feat, start=True, stop=True), "f1")
            transposed("hT", XN, KD, "xn_x")
            pe.wait_ge(sem("sine"), 1)
            ps = take(pe, "f2")
            full(mm(ps[0:FFN, 0:S], fw2, h1[0:FFN, :], start=True, stop=True), "f2")
            w = three(arrived(pe, "lat")[:, 0:KD * LAT], KD)
            all_ready("hT", 4)
            for t in range(TT):
                ps = take(pe, "lat", t)
                for k in range(KD):
                    last = mm(ps[:, 0:LAT], HT[:, k, t * P:(t + 1) * P], w[:, k, :], start=k == 0, stop=k == KD - 1)
                full(last, "lat", t)

            def hyena_in(third):
                for j in range(2):
                    ps = take(pe, f"hy{third}", j)
                    for a in range(2):
                        tile = 4 * third + 2 * j + a
                        w = three(arrived(pe, "hya" if tile < 6 else "hyb")[:, 0:KD * 768], KD)
                        c = (tile % 6) * P
                        for k in range(KD):
                            last = mm(ps[:, a * S:(a + 1) * S], w[:, k, c:c + P], HT[:, k, :],
                                      start=k == 0, stop=k == KD - 1)
                    full(last, f"hy{third}", j)

            def hyena_tok(third):
                for j in range(2):
                    ready(pe, f"hy{third}", j)
                for t in range(TT):
                    ps = take(pe, f"hyT{third}", t)
                    for i in range(4):
                        last = tr(ps[:, i * P:(i + 1) * P], conv_t[:, i, t * P:(t + 1) * P], ident)
                    full(last, f"hyT{third}", t)

            def filters(n):
                pe.wait_ge(sem("sine"), 2)
                pe.wait_ge(sem("h2_one"), 1)
                for t in range(TT):
                    for d in range(2):
                        ps = take(pe, f"f3_{n}", 2 * t + d)
                        c = (2 * n + d) * HW
                        full(mm(ps[:, :], h2[0:FFN + 1, t * P:(t + 1) * P], w3[0:FFN + 1, c:c + HW],
                                start=True, stop=True), f"f3_{n}", 2 * t + d)

            def filter_spectra(n):
                pe.wait_ge(sem("parts"), 2 * TT * (n + 1))
                cases = [(fwd_c[:, :, 0:P], even), (fwd_c[:, :, P:S], even), (sin_m[:, :, 0:P], odd),
                         (sin_m[:, :, P:S], odd), (cos_0, even)]
                pe.wait_ge(sem("dft"), 16)
                for j, (m, src) in enumerate(cases):
                    ps = take(pe, f"sp{n}", j)
                    for t in range(TT):
                        last = mm(ps[:, :], m[:, t, :], src[:, t, :], start=t == 0, stop=t == TT - 1)
                    full(last, f"sp{n}", j)

            def z_spectrum(n):
                if n == 0:
                    for t in range(TT):
                        ready(pe, "hyT2", t)
                else:
                    pe.wait_ge(sem("zed"), TT * n)
                for f in range(TT):
                    for j, m in ((2 * f, fwd_c), (2 * f + 1, fwd_s)):
                        ps = take(pe, f"zs{n}", j)
                        for t in range(TT):
                            last = mm(ps[:, :], m[:, t, f * P:(f + 1) * P], Z[:, t, :], start=t == 0, stop=t == TT - 1)
                        full(last, f"zs{n}", j)

            def convolve(n):
                pe.wait_ge(sem("product"), TT * (n + 1))
                for t in range(TT):
                    ps = take(pe, f"cv{n}", t)
                    for f in range(TT):
                        mm(ps[:, :], inv_c[:, f, t * P:(t + 1) * P], spec_r[:, f, :], start=f == 0, stop=False)
                        last = mm(ps[:, :], inv_s[:, f, t * P:(t + 1) * P], spec_i[:, f, :],
                                  start=False, stop=f == TT - 1)
                    full(last, f"cv{n}", t)

            hyena_in(0)
            filters(0)
            hyena_tok(0)
            hyena_in(1)
            pe.wait_ge(sem("lat_n"), 3)
            for j, srcs in ((0, (lat[:, :, 0:P], lat[:, :, P:QR])), (1, (lat[:, :, QR:QR + KVR], krb))):
                ps = take(pe, "latT", j)
                for a, src in enumerate(srcs):
                    for t in range(TT):
                        last = tr(ps[:, a * S + t * P:a * S + (t + 1) * P], src[:, t, :], ident)
                full(last, "latT", j)
            filter_spectra(0)
            hyena_tok(1)
            hyena_in(2)
            filters(1)
            hyena_tok(2)
            filter_spectra(1)
            w = arrived(pe, "mla")
            wq, wk, wv = three(w[:, 0:2048], 2), w[:, 2048:2560], w[:, 2560:3072]
            for j in range(2):
                ready(pe, "latT", j)
            for j in range(4):
                ps = take(pe, "uq", j)
                for a in range(2):
                    h = 2 * j + a
                    for k in range(2):
                        last = mm(ps[:, a * S:(a + 1) * S], wq[:, k, h * P:(h + 1) * P], latTb[:, k, :],
                                  start=k == 0, stop=k == 1)
                full(last, "uq", j)
            for j in range(4):
                ps = take(pe, "uk", j)
                for a in range(2):
                    h = 2 * j + a
                    last = mm(ps[0:NOPE, a * S:(a + 1) * S], wk[:, h * NOPE:(h + 1) * NOPE], latTb[:, 2, :],
                              start=True, stop=True)
                full(last, "uk", j)
            for t in range(TT):
                ps = take(pe, "uv", t)
                full(mm(ps[:, :], latTb[:, 2, t * P:(t + 1) * P], wv, start=True, stop=True), "uv", t)
            z_spectrum(0)
            for j in range(4):
                ready(pe, "uq", j)
                ready(pe, "uk", j)
            pe.wait_ge(sem("k_rope"), 1)
            for t in range(TT):
                ready(pe, "uv", t)

            def mla_scores(h):
                ps = take(pe, f"sc{h}")
                for t in range(TT):
                    last = mm(ps[:, t * S:(t + 1) * S], QT[:, h, t * P:(t + 1) * P], KT[:, h, :], start=True, stop=True)
                full(last, f"sc{h}")

            def probs_T(stage, src):
                ps = take(pe, stage)
                for kt in range(TT):
                    for t in range(TT):
                        last = tr(ps[:, kt * S + t * P:kt * S + (t + 1) * P], src[:, t, kt * P:(kt + 1) * P], ident)
                full(last, stage)

            mla_scores(0)
            mla_scores(1)
            for h in range(H1):
                ready(pe, f"sc{h}")
                probs_T(f"pT{h}", prob[:, h % 2])
                ready(pe, f"pT{h}")
                ps = take(pe, f"pv{h}")
                for t in range(TT):
                    for kt in range(TT):
                        last = mm(ps[:, t * VD:(t + 1) * VD], probT[:, h % 2, kt, t * P:(t + 1) * P],
                                  V1[:, kt, h * VD:(h + 1) * VD], start=kt == 0, stop=kt == TT - 1)
                full(last, f"pv{h}")
                if h + 2 < H1:
                    mla_scores(h + 2)
                if h == 2:
                    convolve(0)
                if h == 5:
                    z_spectrum(1)
            convolve(1)
            transposed("memT", XN, KD, "xn_m")
            all_ready("memT", 4)
            channel_out("mk", ["mk0", "mk1"])
            token_out("mv", ["mv0", "mv1"], "memT", 4)
            for j in range(4):
                ps = take(pe, "mixT", j)
                src, c = (AO, 2 * j) if j < 2 else (Z, 2 * j - 4)
                for a in range(2):
                    for t in range(TT):
                        pe.wait_ge(sem("normed"), upto(NORMS, "ao_n" if j < 2 else "z_n", t))
                        last = tr(ps[:, a * S + t * P:a * S + (t + 1) * P], src[:, t, (c + a) * P:(c + a + 1) * P], ident)
                full(last, "mixT", j)
            token_out("wo", ["wo0", "wo1"], "mixT", 4)
            transposed("cT", XN, KD, "xn_c")
            all_ready("cT", 4)
            channel_out("mq", ["mq0", "mq1"])
            all_ready("mq", 4)
            all_ready("mk", 4)

            def x_scores(h):
                ps = take(pe, f"xs{h}")
                for t in range(TT):
                    for k in range(2):
                        last = mm(ps[:, t * S:(t + 1) * S], QX[:, 2 * h + k, t * P:(t + 1) * P], KM[:, 2 * h + k, :],
                                  start=k == 0, stop=k == 1)
                full(last, f"xs{h}")

            x_scores(0)
            x_scores(1)
            for h in range(XH):
                pe.wait_ge(sem("x_prob"), TT * (h + 1))
                probs_T(f"xT{h}", prob[:, h % 2])
                ready(pe, f"xT{h}")
                ps = take(pe, f"xv{h}")
                for d in range(2):
                    for m in range(TT):
                        last = mm(ps[:, d * S:(d + 1) * S], VM[:, m, h * XHD + d * P:h * XHD + (d + 1) * P],
                                  probT[:, h % 2, m, :], start=m == 0, stop=m == TT - 1)
                full(last, f"xv{h}")
                if h + 2 < XH:
                    x_scores(h + 2)
            for h in range(XH):
                ready(pe, f"xv{h}")
            for u in range(2):
                w = three(arrived(pe, f"mo{u}")[:, 0:4096], KD)
                for t in range(TT):
                    ps = take(pe, "mo", 2 * u + t)
                    for k in range(KD):
                        last = mm(ps[:, :], oT[:, k, t * P:(t + 1) * P], w[:, k, :], start=k == 0, stop=k == KD - 1)
                    full(last, "mo", 2 * u + t)

            def moe(b):
                transposed(f"rT{b}", XN, KD, f"xn_r{b}")
                all_ready(f"rT{b}", 4)
                pe.wait_ge(sem("wr"), 16 * b)
                w = three(wr[:, b - 1, :], KD)
                ps = take(pe, f"rt{b}")
                for t in range(TT):
                    for k in range(KD):
                        last = mm(ps[:, t * 64:t * 64 + G + NE], HT[:, k, t * P:(t + 1) * P], w[:, k, :],
                                  start=k == 0, stop=k == KD - 1)
                full(last, f"rt{b}")
                pe.wait_ge(sem(f"hot{b}"), 1)
                ps = take(pe, f"cnt{b}")
                mm(ps[:, 0:NE], T("tri"), M12[:, 0, :], start=True, stop=True)
                mm(ps[:, NE:2 * NE], T("tri"), M12[:, 1, :], start=True, stop=False)
                mm(ps[:, NE:2 * NE], ones, M12[:, 0, :], start=False, stop=True)
                mm(ps[:, 2 * NE:3 * NE], ones, M12[:, 0, :], start=True, stop=False)
                full(mm(ps[:, 2 * NE:3 * NE], ones, M12[:, 1, :], start=False, stop=True), f"cnt{b}")
                pe.wait_ge(sem(f"sel{b}"), TT)
                for k in range(KD):
                    ps = take(pe, f"gx{b}", k)
                    for t in range(TT):
                        last = mm(ps[:, :], XN[:, t, k * P:(k + 1) * P], sel[:, t, :], start=t == 0, stop=t == TT - 1)
                    full(last, f"gx{b}", k)
                pe.wait_ge(sem(f"selw{b}"), TT)
                for j in range(2):
                    ps = take(pe, f"swT{b}", j)
                    for a in range(2):
                        for t in range(TT):
                            last = tr(ps[:, a * S + t * P:a * S + (t + 1) * P],
                                      selw[:, t, (2 * j + a) * P:(2 * j + a + 1) * P], ident)
                    full(last, f"swT{b}", j)
                for j in range(2):
                    ready(pe, f"swT{b}", j)

                def gate_up(xw, w, i, ks):
                    for k in ks:
                        g = 64 * (k % 2)
                        last = mm(bank[i][g:g + WIN, :], xw[:, k, :], w[:, k * 512:(k + 1) * 512],
                                  start=k < 2, stop=k >= KD - 2)
                    return last

                def gu_T(i):
                    for c in range(4):
                        last = mm(bank[2][:, c * WIN:(c + 1) * WIN], gu_sb[:, i, c * P:(c + 1) * P], stack,
                                  start=True, stop=True)
                    return last

                def down(w):
                    for half in range(2):
                        for f in range(2):
                            o = KD * 512 + f * D + half * 512
                            last = mm(bank[3 + half][64 * f:64 * f + WIN, :], hb[:, f, :], w[:, o:o + 512],
                                      start=True, stop=True)
                    return last

                def down_T():
                    for c in range(KD):
                        last = mm(bank[5][:, c * WIN:(c + 1) * WIN], d_sb[:, c * P:(c + 1) * P], stack,
                                  start=True, stop=True)
                    return last

                base = MOE_AT[b - 1]

                def step(e, r, count, first=(), tail=True):
                    w = ring[:, slot(base + r), :]
                    i = r % 2
                    if 0 not in first:
                        pe.wait_ge(sem(f"gu_sb{b}"), e - 1)
                    pe.wait_ge(sem(f"xwin{b}"), e + 1)
                    pe.wait_ge(sem(f"slot_full{slot(base + r)}"), count)
                    gate_up(xwin[:, i], w, i, range(0, 4))
                    if 0 not in first:
                        pe.wait_ge(sem(f"d_lo{b}"), e - 1)
                        pe.wait_ge(sem(f"d_hi{b}"), e - 1)
                        if 2 not in first:
                            pe.wait_ge(sem(f"y_out{b}"), e - 2)
                        down_T().then_inc(sem(f"yT_done{b}"), 1)
                    if 1 not in first:
                        pe.wait_ge(sem(f"gu_sb{b}"), e)
                        if 0 not in first:
                            pe.wait_ge(sem(f"hb{b}"), e - 1)
                        gu_T(1 - i).then_inc(sem(f"guT_done{b}"), 1)
                    gate_up(xwin[:, i], w, i, range(4, 8)).then_inc(sem(f"gu_done{b}"), 1)
                    if 1 not in first:
                        pe.wait_ge(sem(f"hb{b}"), e)
                        pw = ring[:, slot(base + r - 1), :]
                        down(pw).then_inc(sem(f"down_done{b}"), 1)

                for e in range(RING):
                    skip_ = ({0: (0, 1, 2), 1: (0, 2), 2: (2,)}).get(e, ())
                    step(e, e, 16 * ((base + e) // RING + 1), skip_)
                with pe.Fori(RING, NE - RING + 1, RING) as e0:
                    for r in range(RING):
                        c0 = 16 * ((base + r) // RING + 1)
                        step(e0 + r, r, e0 * (16 // RING) + c0)
                pe.wait_ge(sem(f"d_lo{b}"), NE - 1)
                pe.wait_ge(sem(f"d_hi{b}"), NE - 1)
                pe.wait_ge(sem(f"y_out{b}"), NE - 2)
                down_T().then_inc(sem(f"yT_done{b}"), 1)
                pe.wait_ge(sem(f"gu_sb{b}"), NE)
                gu_T((NE - 1) % 2).then_inc(sem(f"guT_done{b}"), 1)
                pe.wait_ge(sem(f"hb{b}"), NE)
                down(ring[:, slot(base + NE - 1), :]).then_inc(sem(f"down_done{b}"), 1)
                pe.wait_ge(sem(f"d_lo{b}"), NE)
                pe.wait_ge(sem(f"d_hi{b}"), NE)
                pe.wait_ge(sem(f"y_out{b}"), NE - 1)
                down_T().then_inc(sem(f"yT_done{b}"), 1)
                pe.wait_ge(sem(f"routed{b}"), 1)
                n = pe.value_load(tabi[0:1, 48:49], min_val=0, max_val=NX - 1)
                with pe.If(n > 0):
                    with pe.Fori(0, n) as j:
                        w = ring[:, slot(base), :]
                        pe.wait_ge(sem(f"extra_x{b}"), j + 1)
                        pe.wait_ge(sem(f"extra_w{b}"), j * 16 + 16)
                        gate_up(xwin[:, 0], w, 0, range(KD)).then_inc(sem(f"extra_gu{b}"), 1)
                        pe.wait_ge(sem(f"extra_gs{b}"), j + 1)
                        gu_T(0).then_inc(sem(f"extra_gT{b}"), 1)
                        pe.wait_ge(sem(f"extra_h{b}"), j + 1)
                        down(w).then_inc(sem(f"extra_down{b}"), 1)
                        pe.wait_ge(sem(f"extra_d{b}"), 2 * j + 2)
                        down_T().then_inc(sem(f"extra_yT{b}"), 1)
                pe.wait_ge(sem(f"y_out{b}"), NE)
                pe.wait_ge(sem(f"extra_y{b}"), n + 1)
                for j in range(8):
                    pt, half = j // 2, j % 2
                    ps = take(pe, f"yT{b}", j)
                    for c in range(4):
                        last = tr(ps[:, c * P:(c + 1) * P], ysT[:, 4 * half + c, pt * P:(pt + 1) * P], ident)
                    full(last, f"yT{b}", j)
                if b == 2:
                    gate_row("g2r", diag2, "diag2")
                for j in range(8):
                    ready(pe, f"yT{b}", j)
                for t in range(TT):
                    for half in range(2):
                        ps = take(pe, f"sct{b}", 2 * t + half)
                        for pt in range(NPAIR // P):
                            last = mm(ps[:, :], swT[:, pt, t * P:(t + 1) * P], ytok[:, pt, half * 512:(half + 1) * 512],
                                      start=pt == 0, stop=pt == NPAIR // P - 1)
                        full(last, f"sct{b}", 2 * t + half)

            def gate_row(stage, dg, ready_sem):
                pe.wait_ge(sem(ready_sem), 1)
                for j in range(2):
                    ps = take(pe, stage, j)
                    full(mm(ps[:, :], ones, dg[:, 4 * j:4 * j + 4, :].rearrange("p a b -> p (a b)"),
                            start=True, stop=True), stage, j)

            moe(1)

            pe.wait_ge(sem("onehot"), 32)
            pe.wait_ge(sem("mask_row"), 1)
            ps = take(pe, "bias")
            full(mm(ps[0:H1, :], relb[0:BUCKETS + 1, :], oneh[0:BUCKETS + 1, :], start=True, stop=True), "bias")
            pe.wait_ge(sem("cm"), 1)

            def ada(i):
                w = three(arrived(pe, f"ada{i}")[:, 0:4096], KD)
                ps = take(pe, f"ada{i}")
                for k in range(KD):
                    g = 32 * (k % 4)
                    last = mm(ps[g:g + 32, :], cm[:, k, :], w[:, k, :], start=k < 4, stop=k >= 4)
                full(last, f"ada{i}")

            def ada_col(i):
                ready(pe, f"ada{i}")
                ps = take(pe, f"adac{i}")
                for c in range(4):
                    last = mm(ps[:, c:c + 1], adab[:, i % 2, c * P:(c + 1) * P], ones[:, 0:1], start=True, stop=True)
                full(last, f"adac{i}")

            ada(0)
            for i in range(12):
                if i < 11:
                    ada(i + 1)
                ada_col(i)
            gate_row("g1r", diag1, "diag1")
            transposed("uT", XN, KD, "xn_u")
            all_ready("uT", 4)
            channel_out("xl", ["win0"])
            channel_out("yl", ["win1"])
            pe.wait_ge(sem("gates_w"), 16)
            for j in range(2):
                ready(pe, "xl", j)
            for stage, o in (("ga", 0), ("gx", 4 * P)):
                for j in range(2):
                    ps = take(pe, stage, j)
                    for a in range(2):
                        i = 2 * j + a
                        last = mm(ps[:, a * S:(a + 1) * S], ROW[:, o + i * P:o + (i + 1) * P], xc[:, i, :],
                                  start=True, stop=True)
                    full(last, stage, j)
            channel_out("aq", ["win2"])
            channel_out("ak", ["win3"])
            w = three(arrived(pe, "win4")[:, 0:4096], KD)
            for t in range(TT):
                ps = take(pe, "av", t)
                for k in range(KD):
                    last = mm(ps[:, :], HT[:, k, t * P:(t + 1) * P], w[:, k, :], start=k == 0, stop=k == KD - 1)
                full(last, "av", t)
            for stage in ("aq", "ak", "av"):
                all_ready(stage, 2)

            def a_scores(h):
                g, i = 64 * (h % 2), h // 2
                ps = take(pe, f"as{h}")
                mm(ps[:, 0:P], Q2[g:g + 64, i, 0:P], K2[g:g + 64, i, 0:P], start=True, stop=True)
                full(mm(ps[:, P:P + S], Q2[g:g + 64, i, P:S], K2[g:g + 64, i, :], start=True, stop=True), f"as{h}")

            a_scores(0)
            a_scores(1)
            for h in range(H1):
                pe.wait_ge(sem("a_prob"), TT * (h + 1))
                ps = take(pe, f"aT{h}")
                for c in range(3):
                    last = tr(ps[:, c * P:(c + 1) * P], prob2[:, h % 2, c * P:(c + 1) * P], ident)
                full(last, f"aT{h}")
                ready(pe, f"aT{h}")
                ps = take(pe, f"ap{h}")
                hc = slice(h * 64, (h + 1) * 64)
                mm(ps[:, 0:64], probT2[:, h % 2, 0:P], V2[:, 0, hc], start=True, stop=True)
                mm(ps[:, 64:128], probT2[:, h % 2, P:2 * P], V2[:, 0, hc], start=True, stop=False)
                full(mm(ps[:, 64:128], probT2[:, h % 2, 2 * P:3 * P], V2[:, 1, hc], start=False, stop=True), f"ap{h}")
                if h + 2 < H1:
                    a_scores(h + 2)
            pe.wait_ge(sem("lru_sq"), 4)
            ps = take(pe, "lss")
            for t in range(TT):
                for i in range(4):
                    last = mm(ps[:, t:t + 1], sq[:, i, t * P:(t + 1) * P], ones[:, 0:1], start=i == 0, stop=i == 3)
            full(last, "lss")
            for j in range(2):
                ps = take(pe, "aoT", j)
                for a in range(2):
                    for t in range(TT):
                        pe.wait_ge(sem("normed"), upto(NORMS, "ao2_n", t))
                        last = tr(ps[:, a * S + t * P:a * S + (t + 1) * P],
                                  AO2[:, t, (2 * j + a) * P:(2 * j + a + 1) * P], ident)
                full(last, "aoT", j)
            pe.wait_ge(sem("lo_g"), 4)
            all_ready("aoT", 2)
            for u in range(2):
                w = three(arrived(pe, f"wp{u}")[:, 0:4096], KD)
                for t in range(TT):
                    for part, src in ((0, loT), (1, aoT)):
                        ps = take(pe, "wp", 4 * u + 2 * t + part)
                        for i in range(4):
                            last = mm(ps[:, :], src[:, i, t * P:(t + 1) * P], w[:, 4 * part + i, :],
                                      start=i == 0, stop=i == 3)
                        full(last, "wp", 4 * u + 2 * t + part)
            moe(2)

        @block.scalar
        def _(act):
            A_ = nc.scalar.activation
            steps = [0]

            def link(ins):
                steps[0] += 1
                ins.then_inc(sem("act_step"), 1)
                act.wait_ge(sem("act_step"), steps[0])

            squared = [0]

            def square(junk_, src, total):
                if squared[0]:
                    act.wait_ge(sem("squares"), squared[0])
                squared[0] += 1
                A_(junk_, src, ACT.Square, accum_out=total).then_inc(sem("squares"), 1)

            def squares(tag, src, junk_, sums, wait):
                for t in range(TT):
                    wait(t)
                    square(junk_(t), src(t), sums[:, t:t + 1])

            def channel_evac(stage, dst, n, scale, bias=None, even=0):
                for j in range(even, n, 2):
                    ps = got(act, stage, j)
                    for a in range(2):
                        k = 2 * j + a
                        src = ps[:, a * S:(a + 1) * S]
                        if scale is None:
                            last = A_(dst[:, k, :], src, ACT.Copy)
                        elif bias is None:
                            last = A_(dst[:, k, :], src, ACT.Copy, scale=scale(k))
                        else:
                            last = A_(dst[:, k, :], src, ACT.Identity, scale=scale(k), bias=bias(k))
                    free(last, stage, j)

            for t in range(TT):
                act.dma_start(X[:, t, :], A["x"][t * P:(t + 1) * P, :]).then_inc(sem(f"x_in{t}"), 16)
            act.dma_start(tab[:, :], A["tab"]).then_inc(sem("tab"), 16)
            act.dma_start(col[:, :], A["col"]).then_inc(sem("tab"), 16)
            act.dma_start(dft, A["dft"]).then_inc(sem("dft"), 16)
            row = A["hy_skip"]
            act.dma_start(ROW[:, 1024:2048], bass.AP(row.tensor, 0, [[0, P], [1, ORDER * HW]])).then_inc(sem("skip"), 16)
            squares("x", lambda t: X[:, t, :], lambda t: XN[:, t, :], ssq_x,
                    lambda t: act.wait_ge(sem(f"x_in{t}"), 16))
            act.wait_ge(sem("arg"), 1)
            A_(h1[0:FFN, :], arg[0:FFN, :], ACT.Sin).then_inc(sem("sine"), 1)
            channel_evac("hT", HT, 4, lambda k: C("mix_norm_g", k))
            act.wait_ge(sem("arg"), 2)
            A_(h2[0:FFN, :], arg[0:FFN, :], ACT.Sin).then_inc(sem("sine"), 1)
            dec = arrived(act, "filt")[:, 2048:4096]
            link(A_(dec, dec, ACT.Abs))
            for t in range(TT):
                ready(act, "lat", t)
                square(latTb[:, 0, :], lat[:, t, 0:QR], ssq_l[:, t:t + 1])
                square(latTb[:, 1, 0:KVR], lat[:, t, QR:QR + KVR], ssq_l[:, 2 + t:3 + t])

            def hyena_conv(third):
                if third:
                    got(act, f"hyT{third - 1}", 1)
                for j in range(2):
                    ps = got(act, f"hy{third}", j)
                    for a in range(2):
                        i = 4 * third + 2 * j + a
                        A_(conv_t[:, 2 * j + a, :], ps[:, a * S:(a + 1) * S], ACT.Identity,
                           scale=C("hy_conv_w", 12 + i), bias=C("hy_conv_b", i)).then_inc(sem("mid_tap"), 1)

            def decays(n):
                for t in range(TT):
                    for d in range(2):
                        i = 4 * n + 2 * t + d
                        if i >= 2:
                            act.wait_ge(sem("parts"), i - 1)
                        c = (2 * n + d) * HW
                        A_(env[:, i % 2, :], dec[:, c:c + HW], ACT.Exp, scale=T("negt")[:, t:t + 1]
                           ).then_inc(sem("env"), 1)

            def copies(stage, dsts):
                for j, dst in enumerate(dsts):
                    ps = got(act, stage, j)
                    free(A_(dst, ps[:, :], ACT.Copy), stage, j)

            def spectra(n):
                copies(f"sp{n}", [k_c[n][:, 0, :], k_c[n][:, 1, :], k_s[n][:, 0, :], k_s[n][:, 1, :], k_c0[n]])

            hyena_conv(0)
            decays(0)
            copies("hyT0", [hytok[:, t, 0, :] for t in range(TT)])
            hyena_conv(1)
            ps = got(act, "latT", 0)
            A_(latTb[:, 0, :], ps[:, 0:S], ACT.Copy, scale=C("q_norm_g", 0))
            free(A_(latTb[:, 1, :], ps[:, S:2 * S], ACT.Copy, scale=C("q_norm_g", 1)), "latT", 0)
            ps = got(act, "latT", 1)
            A_(latTb[:, 2, :], ps[:, 0:S], ACT.Copy, scale=C("kv_norm_g"))
            free(A_(latTb[:, 3, :], ps[:, S:2 * S], ACT.Copy), "latT", 1)
            spectra(0)
            copies("hyT1", [hytok[:, t, 1, :] for t in range(TT)])
            hyena_conv(2)
            decays(1)
            copies("hyT2", [hytok[:, t, 2, :] for t in range(TT)])
            spectra(1)
            for j in range(4):
                ps = got(act, "uk", j)
                free(A_(KT[0:NOPE, 2 * j:2 * j + 2, :], three(ps[0:NOPE, :], 2), ACT.Copy), "uk", j)
            copies("uv", [V1[:, t, :] for t in range(TT)])
            for h in range(H1):
                ps = got(act, f"sc{h}")
                act.wait_ge(sem("neg_max"), h + 1)
                if h >= 2:
                    got(act, f"pT{h - 2}")
                for t in range(TT):
                    last = A_(prob[:, h % 2, t, :], ps[:, t * S:(t + 1) * S], ACT.Exp, bias=nmax[:, h, t:t + 1],
                              accum_out=rsum[:, h, t:t + 1])
                free(last, f"sc{h}")
            act.dma_start(XN, A["mem"].rearrange("(t p) d -> p t d", p=P)).then_inc(sem("mem_in"), 16)
            ready(act, "pv7")
            squares("ao", lambda t: AO[:, t, :], lambda t: junk[:, 0:HW], ssq_o, lambda t: None)
            act.wait_ge(sem("mem_in"), 16)
            squares("m", lambda t: XN[:, t, :], lambda t: junk, ssq_m, lambda t: None)
            act.wait_ge(sem("zed"), 2 * TT)
            squares("z", lambda t: Z[:, t, :], lambda t: junk[:, 0:HW], ssq_o[:, 2:4], lambda t: None)
            channel_evac("memT", HT, 4, lambda k: C("mem_norm_g", k))
            channel_evac("mk", KM, 4, None)
            for j in (0, 2):
                ps = got(act, "mv", j)
                free(A_(VM[:, j % 2, (j // 2) * 512:(j // 2 + 1) * 512], ps[:, :], ACT.Copy), "mv", j)
            channel_evac("mixT", HT, 4, lambda k: C("attn_out_g", k))
            squares("c", lambda t: X[:, t, :], lambda t: XN[:, t, :], ssq_c,
                    lambda t: (ready(act, "wo", t), ready(act, "wo", 2 + t)))
            channel_evac("cT", HT, 4, lambda k: C("cross_norm_g", k))
            channel_evac("mq", QX, 4, None)
            for h in range(XH):
                ps = got(act, f"xs{h}")
                act.wait_ge(sem("x_max"), h + 1)
                if h >= 2:
                    got(act, f"xT{h - 2}")
                for t in range(TT):
                    last = A_(prob[:, h % 2, t, :], ps[:, t * S:(t + 1) * S], ACT.Exp, bias=xmax[:, h, t:t + 1],
                              scale=float(XHD ** -0.5), accum_out=xsum[:, h, t:t + 1])
                free(last, f"xs{h}")
                if h >= 1:
                    ps = got(act, f"xT{h - 1}")
                    if h >= 3:
                        got(act, f"xv{h - 3}")
                    free(A_(probT[:, (h - 1) % 2, :, :], three(ps[:, :], TT), ACT.Copy), f"xT{h - 1}")
            ps = got(act, f"xT{XH - 1}")
            got(act, f"xv{XH - 3}")
            free(A_(probT[:, (XH - 1) % 2, :, :], three(ps[:, :], TT), ACT.Copy), f"xT{XH - 1}")

            def moe(b):
                if b == 1:
                    squares("r", lambda t: X[:, t, :], lambda t: XN[:, t, :], ssq_r,
                            lambda t: (ready(act, "mo", t), ready(act, "mo", 2 + t)))
                    gain, shift = (lambda k: C("ffn_norm_g", k)), None
                else:
                    gain, shift = (lambda k: mod[:, 32 + k:33 + k]), (lambda k: mod[:, 24 + k:25 + k])
                channel_evac(f"rT{b}", HT, 4, gain, shift)
                act.wait_ge(sem(f"g_diff{b}"), 1)
                A_(gex, cand4, ACT.Exp).then_inc(sem(f"g_exp{b}"), 1)
                act.wait_ge(sem(f"e_diff{b}"), 1)
                A_(ex2, m2, ACT.Exp).then_inc(sem(f"e_exp{b}"), 1)
                for k in range(0, KD, 2):
                    ps = got(act, f"gx{b}", k)
                    if shift is None:
                        last = A_(xsT[:, k, 0:NPAIR], ps[:, :], ACT.Copy, scale=gain(k))
                    else:
                        last = A_(xsT[:, k, 0:NPAIR], ps[:, :], ACT.Identity, scale=gain(k), bias=shift(k))
                    free(last, f"gx{b}", k)
                copies(f"swT{b}", [swT[:, 2 * j:2 * j + 2, :].rearrange("p a b -> p (a b)") for j in range(2)])

                def silu(e, i):
                    act.wait_ge(sem(f"guT_done{b}"), e + 1)
                    A_(sg[:, i, :], bank[2][:, 0:2 * WIN], ACT.Silu).then_inc(sem(f"silu{b}"), 1)

                def evac_gu(e, i, first=False):
                    act.wait_ge(sem(f"gu_done{b}"), e + 1)
                    if not first:
                        act.wait_ge(sem(f"guT_done{b}"), e - 1)
                    A_(gu_sb[:, i, :], bank[i][:, :], ACT.Copy).then_inc(sem(f"gu_sb{b}"), 1)

                def evac_down(e, first=False):
                    act.wait_ge(sem(f"down_done{b}"), e + 1)
                    if not first:
                        act.wait_ge(sem(f"yT_done{b}"), e)
                    A_(d_sb[:, 0:512], bank[3][:, :], ACT.Copy).then_inc(sem(f"d_lo{b}"), 1)

                for e in range(RING):
                    if e >= 1:
                        silu(e - 1, (e - 1) % 2)
                    evac_gu(e, e % 2, e < 2)
                    if e >= 1:
                        evac_down(e - 1, e == 1)
                with act.Fori(RING, NE - RING + 1, RING) as e0:
                    for r in range(RING):
                        silu(e0 + (r - 1), (r - 1) % 2)
                        evac_gu(e0 + r, r % 2)
                        evac_down(e0 + (r - 1))
                silu(NE - 1, (NE - 1) % 2)
                evac_down(NE - 1)
                act.wait_ge(sem(f"routed{b}"), 1)
                n = act.value_load(tabi[0:1, 48:49], min_val=0, max_val=NX - 1)
                with act.If(n > 0):
                    with act.Fori(0, n) as j:
                        act.wait_ge(sem(f"extra_gu{b}"), j + 1)
                        A_(gu_sb[:, 0, :], bank[0][:, :], ACT.Copy).then_inc(sem(f"extra_gs{b}"), 1)
                        act.wait_ge(sem(f"extra_gT{b}"), j + 1)
                        A_(sg[:, 0, :], bank[2][:, 0:2 * WIN], ACT.Silu).then_inc(sem(f"extra_s{b}"), 1)
                        act.wait_ge(sem(f"extra_down{b}"), j + 2)
                        A_(d_sb[:, 0:512], bank[3][:, :], ACT.Copy).then_inc(sem(f"extra_d{b}"), 1)
                for j in range(0, 8, 2):
                    ps = got(act, f"yT{b}", j)
                    free(A_(ytok[:, j // 2, 0:512], ps[:, :], ACT.Copy), f"yT{b}", j)

            moe(1)
            squares("f", lambda t: X[:, t, :], lambda t: XN[:, t, :], ssq_f,
                    lambda t: (ready(act, "sct1", 2 * t), ready(act, "sct1", 2 * t + 1)))

            ps = got(act, "bias")
            free(A_(brow[0:H1, :], ps[0:H1, :], ACT.Copy), "bias")
            ready(act, "bias")
            act.dma_start(bias_rows, brow[0:H1, 0:BW].unsqueeze(1).broadcast_to([H1, P, BW])).then_inc(sem("bias_out"), 16)
            act.wait_ge(sem("bias_out"), 16)
            for o, q0, nk in ((0, 0, P), (P, P, S)):
                act.dma_start(BT[:, :, o:o + nk], bass.AP(bias_rows.tensor, S - 1 - q0, [[BW - 1, P], [P * BW, H1], [1, nk]])
                              ).then_inc(sem("bias_in"), 16)
            A_(mod[:, 0:8], C("c_2", 0, 8), ACT.Silu).then_inc(sem("silu_c"), 1)
            lam = C("lru_lambda_2", 0, 4)
            spa, spy = sp_l[:, 0:4], sp_l[:, 4:8]
            link(A_(spa, lam, ACT.Abs))
            A_(spy, spa, ACT.Exp, scale=-1.0).then_inc(sem("lam_exp"), 1)
            act.wait_ge(sem("lam_one"), 1)
            A_(sp_l[:, 12:16], sp_l[:, 8:12], ACT.Ln).then_inc(sem("lam_ln"), 1)
            for i in range(12):
                ps = got(act, f"ada{i}")
                if i >= 2:
                    got(act, f"adac{i - 2}")
                free(A_(adab[:, i % 2, :], ps[:, :], ACT.Copy), f"ada{i}")
            copies("g1r", [g1row[:, 0:512], g1row[:, 512:1024]])
            act.wait_ge(sem("mod"), 1)
            channel_evac("uT", HT, 4, lambda k: mod[:, 8 + k:9 + k], lambda k: mod[:, k:k + 1])
            for j in range(2):
                ps = got(act, "xl", j)
                for a in range(2):
                    i = 2 * j + a
                    A_(xc[:, i, :], ps[:, a * S:(a + 1) * S], ACT.Identity, scale=C("conv_w_2", 12 + i),
                       bias=C("conv_b_2", i)).then_inc(sem("last_tap"), 1)
            for j in range(2):
                ps = got(act, "yl", j)
                free(A_(gy[:, 2 * j:2 * j + 2, :], three(ps[:, :], 2), ACT.Gelu_apprx_tanh), "yl", j)
            for stage, dst, bias in (("ga", rg, "b_gate_a_2"), ("gx", ig, "b_gate_x_2")):
                for j in range(2):
                    ps = got(act, stage, j)
                    for a in range(2):
                        i = 2 * j + a
                        last = A_(dst[:, i, :], ps[:, a * S:(a + 1) * S], ACT.Sigmoid, bias=C(bias, i))
                    free(last, stage, j)
            act.wait_ge(sem("lam"), 1)
            ready(act, "ga", 1)
            for i in range(4):
                A_(th[:, i, :], rg[:, i, :], ACT.Tanh, scale=sp8[:, i:i + 1])
            for i in range(4):
                last = A_(aa[:, i, :], rg[:, i, :], ACT.Exp, scale=sp8n[:, i:i + 1])
            last.then_inc(sem("decay"), 1)
            copies("av", [V2[:, t, :] for t in range(TT)])
            act.wait_ge(sem("mult2"), 1)
            A_(th[:, :, :], th[:, :, :], ACT.Sqrt).then_inc(sem("mult"), 1)
            for h in range(H1):
                act.wait_ge(sem("a_max"), h + 1)
                if h >= 2:
                    got(act, f"aT{h - 2}")
                A_(prob2[:, h % 2, 0:P], score[:, 0:P], ACT.Exp, bias=amax[:, h, 0:1],
                   accum_out=asum[:, h, 0:1]).then_inc(sem("a_prob"), 1)
                A_(prob2[:, h % 2, P:P + S], score[:, P:P + S], ACT.Exp, bias=amax[:, h, 1:2],
                   accum_out=asum[:, h, 1:2]).then_inc(sem("a_prob"), 1)
                if h == 3:
                    act.wait_ge(sem("lru_out"), 1)
                    for i in range(4):
                        A_(sq[:, i, :], hh[:, i, :], ACT.Square).then_inc(sem("lru_sq"), 1)
                        A_(loT[:, i, :], hh[:, i, :], ACT.Copy, scale=C("norm_lru_g_2", i)).then_inc(sem("lo_g"), 1)
            ready(act, "ap7")
            squares("a", lambda t: AO2[:, t, :], lambda t: area(14336, HW), ssq_a, lambda t: None)
            for j in range(2):
                ps = got(act, "aoT", j)
                for a in range(2):
                    last = A_(aoT[:, 2 * j + a, :], ps[:, a * S:(a + 1) * S], ACT.Copy, scale=C("norm_attn_g_2", 2 * j + a))
                free(last, "aoT", j)
            moe(2)

        @block.vector
        def _(dve):
            V = nc.vector
            steps = [0]

            def link(ins):
                steps[0] += 1
                ins.then_inc(sem("dve_step"), 1)
                dve.wait_ge(sem("dve_step"), steps[0])

            order = []

            def norm_done(tag):
                order.append(tag)
                assert tuple(order) == tuple(n for n, _ in NORMS[:len(order)])

            def normalised(tag, src, dst, rstd, done):
                dve.wait_ge(sem("roots"), upto(ROOTS, tag))
                for t in range(TT):
                    V.tensor_scalar(dst(t), src(t), rstd[:, t:t + 1], None, ALU.mult).then_inc(sem("normed"), 1)
                norm_done(done)

            def layer_norm(i, dst, done):
                for t in range(TT):
                    link(V.bn_stats(bn_[i][t][:, 0:6], X[:, t, 0:512]))
                    link(V.bn_stats(bn_[i][t][:, 6:12], X[:, t, 512:1024]))
                    V.bn_aggr(mv_[i][:, t, :], bn_[i][t][:, :].rearrange("p (a b) -> p a b", a=2)).then_inc(sem("moments"), 1)
                dve.wait_ge(sem("roots"), upto(ROOTS, f"ln{i}"))
                for t in range(TT):
                    V.tensor_scalar(dst[:, t, :], X[:, t, :], mv_[i][:, t, 0:1], rstd_n[i][:, t:t + 1],
                                    ALU.subtract, ALU.mult).then_inc(sem("normed"), 1)
                norm_done(done)

            def channel_evac(stage, dst, n, scale, bias=None, even=1):
                for j in range(even, n, 2):
                    ps = got(dve, stage, j)
                    for a in range(2):
                        k = 2 * j + a
                        src = ps[:, a * S:(a + 1) * S]
                        if scale is None:
                            last = V.tensor_copy(dst[:, k, :], src)
                        elif bias is None:
                            last = V.tensor_scalar(dst[:, k, :], src, scale(k), None, ALU.mult)
                        else:
                            last = V.tensor_scalar(dst[:, k, :], src, scale(k), bias(k), ALU.mult, ALU.add)
                    free(last, stage, j)

            def sine_argument(stage, bias, freq):
                ps = got(dve, stage)
                y, n = arg[0:FFN, :], turn[0:FFN, :]
                free(V.tensor_scalar(y, ps[0:FFN, 0:S], C(bias, 0, 1, FFN), freq, ALU.add, ALU.mult), stage)
                ready(dve, stage)
                link(V.tensor_scalar(n, y, float(1 / TWO_PI), MAGIC, ALU.mult, ALU.add))
                link(V.tensor_scalar(n, n, MAGIC, None, ALU.subtract))
                link(V.scalar_tensor_tensor(out=y, in0=n, scalar=-PI_HI, in1=y, op0=ALU.mult, op1=ALU.add))
                link(V.scalar_tensor_tensor(out=y, in0=n, scalar=-PI_LO, in1=y, op0=ALU.mult, op1=ALU.add))
                V.tensor_scalar(y, y, PI_IN, -PI_IN, ALU.min, ALU.max).then_inc(sem("arg"), 1)

            dve.wait_ge(sem("tab"), 32)
            sine_argument("f1", "hy_b1", C("hy_freq", 0, 1, FFN))
            normalised("x", lambda t: X[:, t, :], lambda t: XN[:, t, :], rstd_x, "xn_x")
            channel_evac("hT", HT, 4, lambda k: C("mix_norm_g", k))
            sine_argument("f2", "hy_b2", C("hy_freq", 1, 1, FFN))
            for t in range(TT):
                ps = got(dve, "lat", t)
                free(V.tensor_copy(lat[:, t, :], ps[:, 0:LAT]), "lat", t)
                ready(dve, "lat", t)
            dve.wait_ge(sem("zeros"), 1)
            kr, kc, ks = lat[:, :, QR + KVR:LAT], three(T("kcos"), TT), three(T("ksin"), TT)
            hf = ROPE // 2
            link(V.tensor_tensor(krb[:, :, 64:96], kr, kc, ALU.mult))
            link(V.tensor_tensor(krb[:, :, 96:96 + hf], kr[:, :, hf:ROPE], ks[:, :, 0:hf], ALU.mult))
            link(V.tensor_tensor(krb[:, :, 96 + hf:128], kr[:, :, 0:hf], ks[:, :, hf:ROPE], ALU.mult))
            link(V.tensor_tensor(krb[:, :, 64:96], krb[:, :, 64:96], krb[:, :, 96:128], ALU.add))
            V.tensor_copy(krb[:, :, 96:128], krb[:, :, 64:96]).then_inc(sem("lat_n"), 1)

            def outer_taps(third):
                for j in range(2):
                    ps = got(dve, f"hy{third}", j)
                    for a in range(2):
                        i = 4 * third + 2 * j + a
                        u, c = ps[:, a * S:(a + 1) * S], conv_t[:, 2 * j + a, :]
                        dve.wait_ge(sem("mid_tap"), 4 * third + 2 * j + 2)
                        link(V.scalar_tensor_tensor(out=c[:, 1:S], in0=u[:, 0:S - 1], scalar=C("hy_conv_w", i),
                                                    in1=c[:, 1:S], op0=ALU.mult, op1=ALU.add))
                        last = V.scalar_tensor_tensor(out=c[:, 0:S - 1], in0=u[:, 1:S], scalar=C("hy_conv_w", 24 + i),
                                                      in1=c[:, 0:S - 1], op0=ALU.mult, op1=ALU.add)
                    free(last, f"hy{third}", j)

            def filter_parts(n):
                for t in range(TT):
                    if n:
                        got(dve, "sp0", 4)
                    i = 4 * n + 2 * t
                    if i:
                        dve.wait_ge(sem("parts"), i)
                    dve.wait_ge(sem("env"), i + 1)
                    ps = got(dve, f"f3_{n}", 2 * t)
                    free(V.tensor_tensor(filt_f, ps[:, :], env[:, 0, :], ALU.mult), f"f3_{n}", 2 * t)
                    ps = got(dve, f"f3_{n}", 2 * t + 1)
                    dve.wait_ge(sem("env"), i + 2)
                    free(V.scalar_tensor_tensor(out=filt_b, in0=ps[:, :], scalar=T("tmask")[:, t:t + 1],
                                                in1=env[:, 1, :], op0=ALU.mult, op1=ALU.mult), f"f3_{n}", 2 * t + 1)
                    ready(dve, f"f3_{n}", 2 * t)
                    ready(dve, f"f3_{n}", 2 * t + 1)
                    V.tensor_tensor(even[:, t, :], filt_f, filt_b, ALU.add).then_inc(sem("parts"), 1)
                    V.tensor_tensor(odd[:, t, :], filt_f, filt_b, ALU.subtract).then_inc(sem("parts"), 1)

            outer_taps(0)
            dve.wait_ge(sem("roots"), upto(ROOTS, "lkv"))
            for t in range(TT):
                V.tensor_scalar(lat[:, t, 0:QR], lat[:, t, 0:QR], rstd_l[:, t:t + 1], None, ALU.mult)
                last = V.tensor_scalar(lat[:, t, QR:QR + KVR], lat[:, t, QR:QR + KVR], rstd_l[:, 2 + t:3 + t],
                                       None, ALU.mult)
                last.then_inc(sem("lat_n"), 1)
            filter_parts(0)
            outer_taps(1)
            outer_taps(2)
            filter_parts(1)
            qtab = T("qtab").unsqueeze(1).broadcast_to([P, 2, S])
            for j in range(4):
                ps = got(dve, "uq", j)
                free(V.tensor_tensor(QT[:, 2 * j:2 * j + 2, :], three(ps[:, :], 2), qtab, ALU.mult), "uq", j)
            ready(dve, "latT", 1)
            V.tensor_copy(KT[64:128, :, :], latTb[64:128, 3:4, :].broadcast_to([64, H1, S])).then_inc(sem("k_rope"), 1)

            def spectrum_product(n):
                for f in range(TT):
                    cosf = k_c0[n] if f == 0 else k_c[n][:, 1, :]
                    a = got(dve, f"zs{n}", 2 * f)
                    V.tensor_tensor(spec_r[:, f, :], a[:, :], k_c[n][:, f, :], ALU.mult)
                    free(V.tensor_tensor(spec_i[:, f, :], a[:, :], k_s[n][:, f, :], ALU.mult), f"zs{n}", 2 * f)
                    b = got(dve, f"zs{n}", 2 * f + 1)
                    V.tensor_tensor(prod[:, 0, :], b[:, :], k_s[n][:, f, :], ALU.mult)
                    free(V.tensor_tensor(prod[:, 1, :], b[:, :], cosf, ALU.mult), f"zs{n}", 2 * f + 1)
                    ready(dve, f"zs{n}", 2 * f)
                    ready(dve, f"zs{n}", 2 * f + 1)
                    V.tensor_tensor(spec_r[:, f, :], spec_r[:, f, :], prod[:, 0, :], ALU.subtract)
                    V.tensor_tensor(spec_i[:, f, :], spec_i[:, f, :], prod[:, 1, :], ALU.add).then_inc(sem("product"), 1)
                    dve.wait_ge(sem("product"), TT * n + f + 1)

            def gated(n):
                dve.wait_ge(sem("skip_z"), TT * (n + 1))
                for t in range(TT):
                    ps = got(dve, f"cv{n}", t)
                    free(V.tensor_tensor(prod[:, t, :], ps[:, :], skip_z[:, t, :], ALU.add), f"cv{n}", t)
                    ready(dve, f"cv{n}", t)
                    V.tensor_tensor(Z[:, t, :], prod[:, t, :], hytok[:, t, n, :], ALU.mult).then_inc(sem("zed"), 1)

            def mla_max(h):
                ps = got(dve, f"sc{h}")
                link(V.reduce_max(nmax[:, h, :], three(ps[:, :], TT), AXX))
                V.tensor_scalar(nmax[:, h, :], nmax[:, h, :], -1.0, None, ALU.mult).then_inc(sem("neg_max"), 1)

            for t in range(TT):
                ready(dve, "hyT2", t)
            spectrum_product(0)
            mla_max(0)
            mla_max(1)
            for h in range(H1):
                ready(dve, f"sc{h}")
                link(V.reciprocal(rinv[:, h, :], rsum[:, h, :]))
                ps = got(dve, f"pT{h}")
                if h >= 2:
                    got(dve, f"pv{h - 2}")
                free(V.tensor_copy(probT[:, h % 2, :, :], three(ps[:, :], TT)), f"pT{h}")
                ps = got(dve, f"pv{h}")
                free(V.tensor_tensor(AO[:, :, h * VD:(h + 1) * VD], three(ps[:, 0:TT * VD], TT),
                                     rinv[:, h, :].unsqueeze(2).broadcast_to([P, TT, VD]), ALU.mult), f"pv{h}")
                if h + 2 < H1:
                    mla_max(h + 2)
                if h == 2:
                    gated(0)
                if h == 5:
                    spectrum_product(1)
            gated(1)
            normalised("ao", lambda t: AO[:, t, :], lambda t: AO[:, t, :], rstd_o, "ao_n")
            normalised("m", lambda t: XN[:, t, :], lambda t: XN[:, t, :], rstd_m, "xn_m")
            normalised("z", lambda t: Z[:, t, :], lambda t: Z[:, t, :], rstd_o[:, 2:4], "z_n")
            channel_evac("memT", HT, 4, lambda k: C("mem_norm_g", k))
            channel_evac("mk", KM, 4, None)
            for j in (1, 3):
                ps = got(dve, "mv", j)
                free(V.tensor_copy(VM[:, j % 2, (j // 2) * 512:(j // 2 + 1) * 512], ps[:, :]), "mv", j)
            channel_evac("mixT", HT, 4, lambda k: C("attn_out_g", k))

            def residual(stage):
                for j in range(4):
                    u, t = j // 2, j % 2
                    ps = got(dve, stage, j)
                    x = X[:, t, u * 512:(u + 1) * 512]
                    free(V.tensor_tensor(x, x, ps[:, :], ALU.add), stage, j)

            residual("wo")
            normalised("c", lambda t: X[:, t, :], lambda t: XN[:, t, :], rstd_c, "xn_c")
            channel_evac("cT", HT, 4, lambda k: C("cross_norm_g", k))
            channel_evac("mq", QX, 4, None)

            def x_max(h):
                ps = got(dve, f"xs{h}")
                link(V.reduce_max(xmax[:, h, :], three(ps[:, :], TT), AXX))
                V.tensor_scalar(xmax[:, h, :], xmax[:, h, :], -float(XHD ** -0.5), None, ALU.mult
                                ).then_inc(sem("x_max"), 1)

            x_max(0)
            x_max(1)
            for h in range(XH):
                ready(dve, f"xs{h}")
                link(V.reciprocal(xinv[:, h, :], xsum[:, h, :]))
                for t in range(TT):
                    p = prob[:, h % 2, t, :]
                    V.tensor_scalar(p, p, xinv[:, h, t:t + 1], None, ALU.mult).then_inc(sem("x_prob"), 1)
                ps = got(dve, f"xv{h}")
                free(V.tensor_copy(oT[:, 2 * h:2 * h + 2, :], three(ps[:, :], 2)), f"xv{h}")
                if h + 2 < XH:
                    x_max(h + 2)
            residual("mo")

            def first_hit(hit, values, cand, best, n):
                link(V.tensor_tensor(hit, values, best.unsqueeze(2).broadcast_to([P, TT, n]), ALU.is_equal))
                idx = T("g99" if n == G else "e99").unsqueeze(1).broadcast_to([P, TT, n])
                link(V.tensor_tensor(cand, hit, idx, ALU.mult))
                link(V.tensor_reduce(out=i1g, in_=cand, axis=AXX, op=ALU.min))
                link(V.tensor_tensor(hit, idx, i1g.unsqueeze(2).broadcast_to([P, TT, n]), ALU.is_equal))

            def moe(b):
                if b == 1:
                    normalised("r", lambda t: X[:, t, :], lambda t: XN[:, t, :], rstd_r, "xn_r1")
                    gain, shift = (lambda k: C("ffn_norm_g", k)), None
                else:
                    layer_norm(2, XN, "xn_r2")
                    gain, shift = (lambda k: mod[:, 32 + k:33 + k]), (lambda k: mod[:, 24 + k:25 + k])
                channel_evac(f"rT{b}", HT, 4, gain, shift)
                ps = got(dve, f"rt{b}")
                dve.wait_ge(sem("bias_r"), 32)
                dve.wait_ge(sem("zeros"), 3)
                lg = three(ps[:, 0:128], TT)[:, :, 0:G + NE]
                free(V.tensor_tensor(L, lg, biasr[b - 1].unsqueeze(1).broadcast_to([P, TT, G + NE]), ALU.add), f"rt{b}")
                ready(dve, f"rt{b}")
                lgg = L[:, :, 0:G]
                link(V.reduce_max(gmx, lgg, AXX))
                V.tensor_tensor(cand4, lgg, gmx.unsqueeze(2).broadcast_to([P, TT, G]), ALU.subtract
                                ).then_inc(sem(f"g_diff{b}"), 1)
                dve.wait_ge(sem(f"g_exp{b}"), 1)
                link(V.reduce_sum(gsum, gex, AXX))
                link(V.reciprocal(pgrp, gsum))
                first_hit(ohg, lgg, cand4, gmx, G)
                le = L[:, :, G:G + NE].rearrange("p t (g e) -> p t g e", g=G)
                link(V.tensor_tensor(spread, le, ohg.unsqueeze(3).broadcast_to([P, TT, G, EPG]), ALU.mult))
                link(V.reduce_sum(ein, spread.rearrange("p t g e -> p t e g"), AXX))
                link(V.reduce_max(m1, ein, AXX))
                first_hit(oh1, ein, cand8, m1, EPG)
                link(V.scalar_tensor_tensor(out=ein2, in0=oh1, scalar=NEG, in1=ein, op0=ALU.mult, op1=ALU.add))
                link(V.reduce_max(i2, ein2, AXX))
                first_hit(oh2, ein2, cand8, i2, EPG)
                V.tensor_tensor(m2, i2, m1, ALU.subtract).then_inc(sem(f"e_diff{b}"), 1)
                for oh, m in ((oh1, M1), (oh2, M2)):
                    link(V.tensor_tensor(m.rearrange("p t (g e) -> p t g e", g=G),
                                         ohg.unsqueeze(3).broadcast_to([P, TT, G, EPG]),
                                         oh.unsqueeze(2).broadcast_to([P, TT, G, EPG]), ALU.mult))
                V.tensor_tensor(M12, M1, M2, ALU.add).then_inc(sem(f"hot{b}"), 1)
                dve.wait_ge(sem(f"e_exp{b}"), 1)
                link(V.tensor_scalar(w2, ex2, 1.0, None, ALU.add))
                link(V.reciprocal(w1, w2))
                link(V.tensor_tensor(w1, w1, pgrp, ALU.mult))
                link(V.tensor_tensor(w2, w1, ex2, ALU.mult))
                ps = got(dve, f"cnt{b}")
                link(V.tensor_copy(counts, ps[:, 2 * NE:3 * NE]))
                link(V.tensor_tensor_scan(incl, counts, zero32, 0.0, ALU.add, ALU.add))
                link(V.tensor_tensor(starts, incl, counts, ALU.subtract))
                free(V.tensor_tensor(posm, three(ps[:, 0:2 * NE], TT), starts.unsqueeze(1).broadcast_to([P, TT, NE]),
                                     ALU.add), f"cnt{b}")
                ready(dve, f"cnt{b}")
                for m, pos in ((M1, pos1), (M2, pos2)):
                    link(V.tensor_tensor(m, m, posm, ALU.mult))
                    link(V.reduce_sum(pos, m, AXX))
                iota = T("iota")
                for t in range(TT):
                    link(V.tensor_scalar(sel[:, t, :], iota, pos1[:, t:t + 1], None, ALU.is_equal))
                    V.scalar_tensor_tensor(out=sel[:, t, :], in0=iota, scalar=pos2[:, t:t + 1], in1=sel[:, t, :],
                                           op0=ALU.is_equal, op1=ALU.add).then_inc(sem(f"sel{b}"), 1)
                for t in range(TT):
                    tmp = ysT[:, 0, 0:NPAIR]
                    V.tensor_scalar(selw[:, t, :], iota, pos1[:, t:t + 1], w1[:, t:t + 1], ALU.is_equal, ALU.mult)
                    link(V.tensor_scalar(tmp, iota, pos2[:, t:t + 1], w2[:, t:t + 1], ALU.is_equal, ALU.mult))
                    V.tensor_tensor(selw[:, t, :], selw[:, t, :], tmp, ALU.add).then_inc(sem(f"selw{b}"), 1)
                    dve.wait_ge(sem(f"selw{b}"), t + 1)
                for k in range(1, KD, 2):
                    ps = got(dve, f"gx{b}", k)
                    if shift is None:
                        last = V.tensor_scalar(xsT[:, k, 0:NPAIR], ps[:, :], gain(k), None, ALU.mult)
                    else:
                        last = V.tensor_scalar(xsT[:, k, 0:NPAIR], ps[:, :], gain(k), shift(k), ALU.mult, ALU.add)
                    free(last, f"gx{b}", k)
                V.memset(xsT[:, :, NPAIR:SORTED], 0.0).then_inc(sem(f"pad{b}"), 1)
                link(V.tensor_copy(tabi[0:1, 0:NE], starts[0:1, :]))
                r = slice(0, 1)
                c1, s1, x1, xi1, xe1 = counts[r, :], starts[r, :], nx[r, :], xincl[r, :], xex[r, :]
                link(V.tensor_scalar(x1, c1, float(WIN), None, ALU.is_gt))
                for k in range(2, S // WIN):
                    link(V.scalar_tensor_tensor(out=x1, in0=c1, scalar=float(k * WIN), in1=x1, op0=ALU.is_gt, op1=ALU.add))
                link(V.tensor_tensor_scan(xi1, x1, zero32[r, :], 0.0, ALU.add, ALU.add))
                link(V.tensor_tensor(xe1, xi1, x1, ALU.subtract))
                link(V.tensor_scalar(cm64[r, :], c1, float(WIN), None, ALU.subtract))
                slots = T("iota")[r, 0:NX].unsqueeze(2).broadcast_to([1, NX, NE])

                def each(v):
                    return v.unsqueeze(1).broadcast_to([1, NX, NE])

                mk, tm, mb = mk8[r], tm8[r], mk8b[r]
                link(V.tensor_tensor(mk, slots, each(xe1), ALU.is_ge))
                link(V.tensor_tensor(mb, slots, each(xi1), ALU.is_lt))
                link(V.tensor_tensor(mk, mk, mb, ALU.mult))
                link(V.tensor_tensor(tm, slots, each(xe1), ALU.subtract))
                link(V.tensor_scalar(tm, tm, 1.0, float(WIN), ALU.add, ALU.mult))
                link(V.tensor_tensor(tm, tm, each(cm64[r, :]), ALU.min))
                link(V.tensor_tensor(tm, tm, each(s1), ALU.add))
                link(V.tensor_tensor(tm, tm, mk, ALU.mult))
                link(V.reduce_sum(xst[r, :], tm, AXX))
                link(V.tensor_tensor(mk, mk, each(T("eid")[r, :]), ALU.mult))
                link(V.reduce_sum(xid[r, :], mk, AXX))
                V.tensor_copy(tabi[0:1, 32:40], xst[r, :]).then_inc(sem(f"extra_down{b}"), 1)
                V.tensor_copy(tabi[0:1, 40:48], xid[r, :]).then_inc(sem(f"extra_y{b}"), 1)
                V.tensor_copy(tabi[0:1, 48:49], xi1[:, NE - 1:NE]).then_inc(sem(f"routed{b}"), 1)
                dve.wait_ge(sem(f"routed{b}"), 1)
                dve.wait_ge(sem(f"pad{b}"), 1)
                for k in range(0, KD):
                    ready(dve, f"gx{b}", k)

                def window(e, i, table=0):
                    s = dve.value_load(tabi[0:1, bass.ds(table + e, 1)] if not isinstance(e, int)
                                       else tabi[0:1, table + e:table + e + 1], min_val=0, max_val=NPAIR)
                    return s

                def x_window(e, i, first=False):
                    s = window(e, i)
                    if not first:
                        dve.wait_ge(sem(f"gu_done{b}"), e - 1)
                    V.tensor_copy(xwin[:, i], xsT[:, :, bass.ds(s, WIN)]).then_inc(sem(f"xwin{b}"), 1)

                def y_window(e, first=False):
                    s = window(e, 0)
                    dve.wait_ge(sem(f"yT_done{b}"), e + 1)
                    if not first:
                        dve.wait_ge(sem(f"y_out{b}"), e)
                    V.tensor_copy(ysT[:, :, bass.ds(s, WIN)], three(bank[5][:, :], KD)).then_inc(sem(f"y_out{b}"), 1)

                def hidden(e, i, first=False):
                    dve.wait_ge(sem(f"silu{b}"), e + 1)
                    if not first:
                        dve.wait_ge(sem(f"down_done{b}"), e)
                    V.tensor_tensor(hb.rearrange("p a b -> p (a b)"), sg[:, i, :], bank[2][:, 2 * WIN:4 * WIN], ALU.mult
                                    ).then_inc(sem(f"hb{b}"), 1)

                def evac_down(e, first=False):
                    dve.wait_ge(sem(f"down_done{b}"), e + 1)
                    if not first:
                        dve.wait_ge(sem(f"yT_done{b}"), e)
                    V.tensor_copy(d_sb[:, 512:1024], bank[4][:, :]).then_inc(sem(f"d_hi{b}"), 1)

                x_window(0, 0, True)
                x_window(1, 1, True)
                for e in range(RING):
                    if e >= 2:
                        y_window(e - 2, e == 2)
                    if e >= 1:
                        hidden(e - 1, (e - 1) % 2, e == 1)
                        x_window(e + 1, (e + 1) % 2)
                        evac_down(e - 1, e == 1)
                with dve.Fori(RING, NE - RING + 1, RING) as e0:
                    for q in range(RING):
                        y_window(e0 + (q - 2))
                        hidden(e0 + (q - 1), (q - 1) % 2)
                        x_window(e0 + (q + 1), (q + 1) % 2)
                        evac_down(e0 + (q - 1))
                y_window(NE - 2)
                hidden(NE - 1, (NE - 1) % 2)
                evac_down(NE - 1)
                y_window(NE - 1)
                dve.wait_ge(sem(f"y_out{b}"), NE)
                dve.wait_ge(sem(f"xwin{b}"), NE + 1)
                n = dve.value_load(tabi[0:1, 48:49], min_val=0, max_val=NX - 1)
                with dve.If(n > 0):
                    with dve.Fori(0, n) as j:
                        s = dve.value_load(tabi[0:1, bass.ds(32 + j, 1)], min_val=0, max_val=NPAIR)
                        dve.wait_ge(sem(f"extra_down{b}"), j + 1)
                        V.tensor_copy(xwin[:, 0], xsT[:, :, bass.ds(s, WIN)]).then_inc(sem(f"extra_x{b}"), 1)
                        dve.wait_ge(sem(f"extra_s{b}"), j + 1)
                        V.tensor_tensor(hb.rearrange("p a b -> p (a b)"), sg[:, 0, :], bank[2][:, 2 * WIN:4 * WIN],
                                        ALU.mult).then_inc(sem(f"extra_h{b}"), 1)
                        dve.wait_ge(sem(f"extra_down{b}"), j + 2)
                        V.tensor_copy(d_sb[:, 512:1024], bank[4][:, :]).then_inc(sem(f"extra_d{b}"), 1)
                        dve.wait_ge(sem(f"extra_yT{b}"), j + 1)
                        V.tensor_copy(ysT[:, :, bass.ds(s, WIN)], three(bank[5][:, :], KD)).then_inc(sem(f"extra_y{b}"), 1)
                for j in range(1, 8, 2):
                    ps = got(dve, f"yT{b}", j)
                    free(V.tensor_copy(ytok[:, j // 2, 512:1024], ps[:, :]), f"yT{b}", j)

            moe(1)
            for j in range(4):
                t, u = j // 2, j % 2
                ps = got(dve, "sct1", j)
                x = X[:, t, u * 512:(u + 1) * 512]
                free(V.tensor_tensor(x, x, ps[:, :], ALU.add), "sct1", j)
            dve.wait_ge(sem("roots"), upto(ROOTS, "f"))
            dve.wait_ge(sem("rows"), 16)
            for t in range(TT):
                link(V.scalar_tensor_tensor(out=X[:, t, :], in0=X[:, t, :], scalar=rstd_f[:, t:t + 1],
                                            in1=ROW[:, 0:1024], op0=ALU.mult, op1=ALU.mult))

            dve.wait_ge(sem("silu_c"), 1)
            dve.wait_ge(sem("zeros"), 2)
            V.tensor_copy(cm[:, :, 0:1], mod[:, 0:8].unsqueeze(2)).then_inc(sem("cm"), 1)
            dve.wait_ge(sem("lam_exp"), 1)
            spy, one_y, ln_y, den, is0, ratio = [sp_l[:, 4 * i:4 * i + 4] for i in range(1, 7)]
            V.tensor_scalar(one_y, spy, 1.0, None, ALU.add).then_inc(sem("lam_one"), 1)
            dve.wait_ge(sem("lam_one"), 1)
            link(V.tensor_scalar(den, one_y, 1.0, None, ALU.subtract))
            link(V.tensor_scalar(is0, den, 0.0, None, ALU.is_equal))
            link(V.tensor_tensor(den, den, is0, ALU.add))
            link(V.reciprocal(ratio, den))
            dve.wait_ge(sem("lam_ln"), 1)
            link(V.tensor_tensor(den, ln_y, is0, ALU.add))
            link(V.tensor_tensor(ratio, ratio, den, ALU.mult))
            link(V.tensor_tensor(ratio, ratio, spy, ALU.mult))
            link(V.tensor_scalar(den, C("lru_lambda_2", 0, 4), -1.0, 0.0, ALU.mult, ALU.max))
            link(V.tensor_tensor(ratio, ratio, den, ALU.add))
            link(V.tensor_scalar(sp8, ratio, LRU_C, None, ALU.mult))
            V.tensor_scalar(sp8n, ratio, -LRU_C, None, ALU.mult).then_inc(sem("lam"), 1)
            for i in range(12):
                ps = got(dve, f"adac{i}")
                m = mod[:, 4 * i:4 * i + 4]
                free(V.tensor_tensor(m, ps[:, 0:4], C("b_ada_2", 4 * i, 4), ALU.add), f"adac{i}")
            ready(dve, "adac11")
            V.tensor_scalar(mod[:, 8:16], mod[:, 8:16], 1.0, None, ALU.add)
            V.tensor_scalar(mod[:, 32:40], mod[:, 32:40], 1.0, None, ALU.add).then_inc(sem("mod"), 1)
            idb = ident.unsqueeze(1).broadcast_to([P, KD, P])
            V.tensor_tensor(diag1, idb, mod[:, 16:24].unsqueeze(2).broadcast_to([P, KD, P]), ALU.mult
                            ).then_inc(sem("diag1"), 1)
            dve.wait_ge(sem("mod"), 1)
            layer_norm(0, XN, "xn_u")
            channel_evac("uT", HT, 4, lambda k: mod[:, 8 + k:9 + k], lambda k: mod[:, k:k + 1])
            for j in range(2):
                ps = got(dve, "xl", j)
                for a in range(2):
                    i = 2 * j + a
                    u, c = ps[:, a * S:(a + 1) * S], xc[:, i, :]
                    dve.wait_ge(sem("last_tap"), 2 * j + 2)
                    for back in (1, 2, 3):
                        last = V.scalar_tensor_tensor(out=c[:, back:S], in0=u[:, 0:S - back],
                                                      scalar=C("conv_w_2", 4 * (3 - back) + i), in1=c[:, back:S],
                                                      op0=ALU.mult, op1=ALU.add)
                        if back < 3:
                            link(last)
                        elif a == 0:
                            link(last)
                free(last, "xl", j)
            dve.wait_ge(sem("decay"), 1)
            for j in range(2):
                ready(dve, "gx", j)
                ready(dve, "yl", j)
            link(V.tensor_tensor(hh, aa, aa, ALU.mult))
            V.scalar_tensor_tensor(out=th, in0=hh, scalar=1.0, in1=th, op0=ALU.add, op1=ALU.mult).then_inc(sem("mult2"), 1)
            link(V.tensor_tensor(ig, ig, xc, ALU.mult))
            channel_evac("aq", Q2, 2, None, even=0)
            channel_evac("aq", Q2, 2, None, even=1)
            channel_evac("ak", K2, 2, None, even=0)
            channel_evac("ak", K2, 2, None, even=1)
            dve.wait_ge(sem("bias_in"), 32)

            def a_max(h):
                ps = got(dve, f"as{h}")
                if h >= 1:
                    dve.wait_ge(sem("a_prob"), TT * h)
                free(V.scalar_tensor_tensor(out=score, in0=ps[:, 0:P + S], scalar=0.125, in1=BT[:, h, :],
                                            op0=ALU.mult, op1=ALU.add), f"as{h}")
                ready(dve, f"as{h}")
                link(V.reduce_max(amax[:, h, 0:1], score[:, 0:P], AXX))
                link(V.reduce_max(amax[:, h, 1:2], score[:, P:P + S], AXX))
                V.tensor_scalar(amax[:, h, :], amax[:, h, :], -1.0, None, ALU.mult).then_inc(sem("a_max"), 1)

            a_max(0)
            a_max(1)
            for h in range(H1):
                dve.wait_ge(sem("a_prob"), TT * (h + 1))
                link(V.reciprocal(ainv[:, h, :], asum[:, h, :]))
                ps = got(dve, f"aT{h}")
                if h >= 2:
                    got(dve, f"ap{h - 2}")
                free(V.tensor_copy(probT2[:, h % 2, :], ps[:, 0:3 * P]), f"aT{h}")
                ps = got(dve, f"ap{h}")
                free(V.tensor_tensor(AO2[:, :, h * 64:(h + 1) * 64], three(ps[:, 0:128], TT),
                                     ainv[:, h, :].unsqueeze(2).broadcast_to([P, TT, 64]), ALU.mult), f"ap{h}")
                if h + 2 < H1:
                    a_max(h + 2)
                if h == 0:
                    dve.wait_ge(sem("mult"), 1)
                    link(V.tensor_tensor(ig, ig, th, ALU.mult))
                    for i in range(4):
                        link(V.tensor_tensor_scan(hh[:, i, :], aa[:, i, :], ig[:, i, :], 0.0, ALU.mult, ALU.add))
                    V.tensor_tensor(hh, hh, gy, ALU.mult).then_inc(sem("lru_out"), 1)
            ps = got(dve, "lss")
            free(V.tensor_copy(ssq_a[:, 2:4], ps[:, 0:2]), "lss")
            normalised("a", lambda t: AO2[:, t, :], lambda t: AO2[:, t, :], rstd_a, "ao2_n")
            dve.wait_ge(sem("roots"), upto(ROOTS, "lru"))
            mix = gy[:, 0:2, :].rearrange("p a b -> p (a b)")
            for u in range(2):
                for t in range(TT):
                    j = 4 * u + 2 * t
                    ps = got(dve, "wp", j)
                    free(V.tensor_scalar(mix, ps[:, :], rstd_a[:, 2 + t:3 + t], None, ALU.mult), "wp", j)
                    ready(dve, "wp", j)
                    ps = got(dve, "wp", j + 1)
                    free(V.tensor_tensor(mix, mix, ps[:, :], ALU.add), "wp", j + 1)
                    ready(dve, "wp", j + 1)
                    link(V.tensor_tensor(mix, mix, g1row[:, u * 512:(u + 1) * 512], ALU.mult))
                    x = X[:, t, u * 512:(u + 1) * 512]
                    link(V.scalar_tensor_tensor(out=x, in0=x, scalar=ALPHA, in1=mix, op0=ALU.mult, op1=ALU.add))

            def affine(done):
                for t in range(TT):
                    link(V.tensor_tensor(X[:, t, :], XN[:, t, :], ROW[:, 0:1024], ALU.mult))
                    V.tensor_tensor(X[:, t, :], X[:, t, :], ROW[:, 1024:2048], ALU.add).then_inc(sem(done), 1)
                    dve.wait_ge(sem(done), t + 1)

            layer_norm(1, XN, "ln1")
            dve.wait_ge(sem("normed"), upto(NORMS, "ln1"))
            dve.wait_ge(sem("rows"), 48)
            affine("x_mid")
            moe(2)
            mixf = diag2.rearrange("p a b -> p (a b)")[:, 0:512]
            V.tensor_tensor(diag2, idb, mod[:, 40:48].unsqueeze(2).broadcast_to([P, KD, P]), ALU.mult
                            ).then_inc(sem("diag2"), 1)
            for j in range(2):
                ps = got(dve, "g2r", j)
                free(V.tensor_copy(g2row[:, j * 512:(j + 1) * 512], ps[:, :]), "g2r", j)
                ready(dve, "g2r", j)
            for j in range(4):
                t, u = j // 2, j % 2
                ps = got(dve, "sct2", j)
                free(V.tensor_tensor(mixf, ps[:, :], g2row[:, u * 512:(u + 1) * 512], ALU.mult), "sct2", j)
                ready(dve, "sct2", j)
                x = X[:, t, u * 512:(u + 1) * 512]
                link(V.scalar_tensor_tensor(out=x, in0=x, scalar=ALPHA, in1=mixf, op0=ALU.mult, op1=ALU.add))
            layer_norm(3, XN, "ln2")
            dve.wait_ge(sem("normed"), upto(NORMS, "ln2"))
            dve.wait_ge(sem("rows"), 80)
            affine("x_end")

        @block.gpsimd
        def _(pool):
            G_ = nc.gpsimd
            steps = [0]

            def link(ins):
                steps[0] += 1
                ins.then_inc(sem("pool_step"), 1)
                pool.wait_ge(sem("pool_step"), steps[0])

            order = []

            def rooted(tag):
                order.append(tag)
                assert tuple(order) == tuple(n for n, _ in ROOTS[:len(order)])
                pool.wait_ge(sem("roots"), len(order))

            def root(waits, sums, out_, width, eps, done):
                for s in waits:
                    pool.wait_ge(sem("squares"), upto(SQUARES, s))
                link(G_.tensor_scalar(out_, sums, 1.0 / width, eps, ALU.mult, ALU.add))
                G_.tensor_tensor(out_, out_, half_neg[:, 0:2], ALU.pow).then_inc(sem("roots"), 1)
                rooted(done)

            def broadcast_row(dst, name, n, done):
                a = A[name]
                pool.dma_start(dst, bass.AP(a.tensor, 0, [[0, P], [1, n]])).then_inc(sem(done), 16)

            link(G_.memset(half_neg, -0.5))
            G_.memset(h2[64:65, :], 1.0).then_inc(sem("h2_one"), 1)
            pool.wait_ge(sem("h2_one"), 1)
            for n, m in enumerate((krb[:, :, :], cm[:, :, :], zero32)):
                G_.memset(m, 0.0).then_inc(sem("zeros"), 1)
                pool.wait_ge(sem("zeros"), n + 1)
            pool.dma_start(wr[:, 0, :], A["wr"]).then_inc(sem("wr"), 16)
            for b, name in enumerate(("rbias", "rbias_2")):
                broadcast_row(biasr[b], name, G + NE, "bias_r")
            root(["x"], ssq_x, rstd_x, D, EPS1, "x")
            root(["l"], ssq_l[:, 0:2], rstd_l[:, 0:2], QR, EPS1, "lq")
            root(["l"], ssq_l[:, 2:4], rstd_l[:, 2:4], KVR, EPS1, "lkv")
            pool.wait_ge(sem("wr"), 16)
            pool.dma_start(wr[:, 1, :], A["wr_2"]).then_inc(sem("wr"), 16)
            pool.wait_ge(sem("skip"), 16)
            for n in range(ORDER):
                if n == 0:
                    for t in range(TT):
                        ready(pool, "hyT2", t)
                        got(pool, "hyT2", t)
                else:
                    pool.wait_ge(sem("zed"), TT)
                for t in range(TT):
                    G_.tensor_tensor(skip_z[:, t, :], Z[:, t, :], skip[:, n, :], ALU.mult).then_inc(sem("skip_z"), 1)
                    pool.wait_ge(sem("skip_z"), TT * n + t + 1)
            root(["ao"], ssq_o[:, 0:2], rstd_o[:, 0:2], HW, EPS1, "ao")
            root(["m"], ssq_m, rstd_m, D, EPS1, "m")
            root(["z"], ssq_o[:, 2:4], rstd_o[:, 2:4], HW, EPS1, "z")
            root(["c"], ssq_c, rstd_c, D, EPS1, "c")
            for j in range(2):
                ready(pool, "mixT", j)
            broadcast_row(ROW[:, 0:1024], "final_norm_g", D, "rows")
            root(["r"], ssq_r, rstd_r, D, EPS1, "r")
            root(["f"], ssq_f, rstd_f, D, EPS1, "f")
            ready(pool, "swT1", 1)
            pool.dma_start(oneh, A["onehot"]).then_inc(sem("onehot"), 16)
            pool.dma_start(relb[0:BUCKETS, :], A["rel_bias_2"]).then_inc(sem("onehot"), 16)
            G_.memset(relb[BUCKETS:BUCKETS + 1, :], NEG).then_inc(sem("mask_row"), 1)
            pool.wait_ge(sem("moments"), TT)
            pool.dma_start(ROW[:, 0:1024], A["gates_w"]).then_inc(sem("gates_w"), 16)
            link(G_.tensor_scalar(rstd_n[0], mv_[0][:, :, 1], EPS2, 1.0, ALU.add, ALU.mult))
            G_.tensor_tensor(rstd_n[0], rstd_n[0], half_neg[:, 0:2], ALU.pow).then_inc(sem("roots"), 1)
            rooted("ln0")
            for j in range(2):
                got(pool, "gx", j)
            broadcast_row(ROW[:, 0:1024], "ln1_g_2", D, "rows")
            broadcast_row(ROW[:, 1024:2048], "ln1_b_2", D, "rows")
            root(["a"], ssq_a[:, 0:2], rstd_a[:, 0:2], HW, EPS2, "a")
            ready(pool, "lss")
            root([], ssq_a[:, 2:4], rstd_a[:, 2:4], HW, EPS2, "lru")

            def ln_root(i):
                pool.wait_ge(sem("moments"), TT * (i + 1))
                link(G_.tensor_scalar(rstd_n[i], mv_[i][:, :, 1], EPS2, 1.0, ALU.add, ALU.mult))
                G_.tensor_tensor(rstd_n[i], rstd_n[i], half_neg[:, 0:2], ALU.pow).then_inc(sem("roots"), 1)
                rooted(f"ln{i}")

            ln_root(1)
            ln_root(2)
            pool.wait_ge(sem("x_mid"), TT)
            broadcast_row(ROW[:, 0:1024], "ln2_g_2", D, "rows")
            broadcast_row(ROW[:, 1024:2048], "ln2_b_2", D, "rows")
            ln_root(3)
            for t in range(TT):
                pool.wait_ge(sem("x_end"), t + 1)
                pool.dma_start(out[t * P:(t + 1) * P, :], X[:, t, :]).then_inc(sem("stored"), 16)
            pool.wait_ge(sem("stored"), 16 * TT)


def _ktiles(w):
    k, n = w.shape
    return np.ascontiguousarray(w.reshape(k // P, P, n).transpose(1, 0, 2).reshape(P, -1))


def _padded(w, rows=P):
    out = np.zeros((rows,) + w.shape[1:], w.dtype)
    out[:w.shape[0]] = w
    return out


def _experts(gate, up, down):
    n = gate.shape[0]
    out = np.empty((n, P, SLOT), gate.dtype)
    gu = out[:, :, :KD * 512].reshape(n, P, KD, 2, FE)
    gu[:, :, :, 0] = gate.reshape(n, KD, P, FE).transpose(0, 2, 1, 3)
    gu[:, :, :, 1] = up.reshape(n, KD, P, FE).transpose(0, 2, 1, 3)
    out[:, :, KD * 512:] = down.reshape(n, FE // P, P, D).transpose(0, 2, 1, 3).reshape(n, P, -1)
    return out


def _arrays(i):
    t, dft, filt, feat, onehot = _tables()
    g = {k: np.asarray(v) for k, v in i.items()}
    a = {"x": g["x"][0], "mem": g["mem"][0], "tab": t, "dft": dft, "onehot": onehot,
         "hy_skip": g["hy_skip"][0], "final_norm_g": g["final_norm_g"], "rel_bias_2": g["rel_bias_2"],
         "ln1_g_2": g["ln1_g_2"][0], "ln1_b_2": g["ln1_b_2"][0], "ln2_g_2": g["ln2_g_2"][0], "ln2_b_2": g["ln2_b_2"][0]}
    cols = []
    for name, w in COLS:
        v = g[name]
        if name in ("hy_b1", "hy_b2", "hy_freq"):
            cols.append(_padded(v.reshape(w, FFN).T))
        else:
            cols.append(v.reshape(w, P).T)
    a["col"] = np.concatenate(cols, 1)
    w_in = g["w_in"][0]
    a["lat"] = _ktiles(w_in[:, :LAT])
    a["hya"], a["hyb"] = _ktiles(w_in[:, LAT:LAT + 768]), _ktiles(w_in[:, LAT + 768:])
    w3 = _padded(np.concatenate([g["hy_w3"][0], g["hy_b3"]], 0))
    decay = np.broadcast_to(g["hy_decay"][0], (P, 2048))
    a["filt"] = np.concatenate([w3, decay, filt, feat, _padded(g["hy_w1"][0]), _padded(g["hy_w2"][0])], 1)
    uq = g["w_uq"][0].reshape(QR, H1, NOPE + ROPE)
    half = ROPE // 2
    uq = np.concatenate([uq, uq[:, :, NOPE + half:], uq[:, :, NOPE:NOPE + half]], 2).reshape(QR, H1 * P)
    ukv = g["w_ukv"][0].reshape(KVR, H1, NOPE + VD)
    a["mla"] = np.concatenate([_ktiles(uq), ukv[:, :, :NOPE].reshape(KVR, -1), ukv[:, :, NOPE:].reshape(KVR, -1)], 1)
    for name, key in (("mk", None), ("mv", None), ("wo", "w_out"), ("mq", "w_mq"), ("mo", "w_mo"), ("wp", "w_out_2")):
        w = g["w_mkv"][0][:, :D] if name == "mk" else g["w_mkv"][0][:, D:] if name == "mv" else g[key][0]
        for u in range(2):
            a[f"{name}{u}"] = _ktiles(w[:, u * 512:(u + 1) * 512])
    for u in range(12):
        a[f"ada{u}"] = _ktiles(g["w_ada_2"][0][:, u * 512:(u + 1) * 512])
    for u in range(5):
        a[f"win{u}"] = _ktiles(g["w_in_2"][0][:, u * 512:(u + 1) * 512])
    a["wr"] = _ktiles(np.concatenate([g["w_route_group"][0], g["w_route_expert"][0]], 1))
    a["wr_2"] = _ktiles(np.concatenate([g["w_router_group_2"][0], g["w_router_expert_2"][0]], 1))
    a["rbias"] = np.concatenate([g["b_route_group"][0], g["b_route_expert"][0]])
    a["rbias_2"] = np.concatenate([g["b_router_group_2"][0], g["b_router_expert_2"][0]])
    gates = np.zeros((P, 2, 4, P), np.float32)
    for q, name in enumerate(("w_gate_a_2", "w_gate_x_2")):
        w = g[name][0]
        for n in range(8):
            gates[64 * (n % 2):64 * (n % 2) + 64, q, n // 2, 64 * (n % 2):64 * (n % 2) + 64] = w[n]
    a["gates_w"] = gates.reshape(P, -1)
    a["experts"] = _experts(g["w_gate"][0].reshape(NE, D, FE), g["w_up"][0].reshape(NE, D, FE),
                            g["w_down"][0].reshape(NE, FE, D))
    a["experts_2"] = _experts(g["w1_2"][0], g["w3_2"][0], g["w2_2"][0])
    return {k: np.ascontiguousarray(v) for k, v in a.items()}


def kernel(**inputs):
    import concourse.bacc as bacc
    from concourse.bass_utils import run_bass_kernel_spmd as run

    nc = bacc.Bacc("TRN2", target_bir_lowering=False, num_devices=1)
    arrays = {f"in_{k}": v for k, v in _arrays(inputs).items()}
    aps = {k[3:]: nc.dram_tensor(k, v.shape, mybir.dt.from_np(v.dtype), kind="ExternalInput").ap()
           for k, v in arrays.items()}
    out = nc.dram_tensor("out", (S, D), F32, kind="ExternalOutput").ap()
    two_blocks(nc, aps, out)
    r = run(nc, [arrays], core_ids=[0])
    return r.results[0]["out"].reshape(1, S, D)
```

```python
from contextlib import ExitStack

import concourse.bass as bass
import numpy as np
from concourse import mybir

F32 = mybir.dt.float32
F32R = mybir.dt.float32r
I32 = mybir.dt.int32
ALU = mybir.AluOpType
ACT = mybir.ActivationFunctionType
AXX = mybir.AxisListType.X

P = 128
S = 256
D = 1024
KD = D // P
TT = S // P
H1, NOPE, ROPE, VD = 8, 64, 32, 64
QR, KVR = 256, 128
LAT = QR + KVR + ROPE
HW = 512
ORDER = 2
EMB, FFN = 33, 64
XH, XHD = 4, 256
G, EPG = 4, 8
NE = G * EPG
FE = 256
NPAIR = 2 * S
WIN = 64
SORTED = NPAIR + WIN
NX = NPAIR // WIN
RING = 4
SLOT = 3 * KD * FE
EPS1, EPS2 = 1e-6, 1e-5
ALPHA = float(2.0 ** 0.25)
LRU_C = 8.0
BUCKETS, MAX_DIST = 32, 128
BW = S + P
NEG = -1e30
TWO_PI = 2 * np.pi
PI_HI = 6.28125
PI_LO = float(TWO_PI - PI_HI)
MAGIC = 12582912.0
PI_IN = 3.1415925

COLS = [("mix_norm_g", 8), ("q_norm_g", 2), ("kv_norm_g", 1), ("hy_conv_w", 36), ("hy_conv_b", 12),
        ("attn_out_g", 4), ("hy_out_g", 4), ("cross_norm_g", 8), ("mem_norm_g", 8), ("ffn_norm_g", 8),
        ("c_2", 8), ("b_ada_2", 48), ("conv_w_2", 16), ("conv_b_2", 4), ("b_gate_a_2", 4),
        ("b_gate_x_2", 4), ("lru_lambda_2", 4), ("norm_lru_g_2", 4), ("norm_attn_g_2", 4),
        ("hy_b1", 1), ("hy_b2", 1), ("hy_freq", 2)]
COL_AT, _n = {}, 0
for _name, _w in COLS:
    COL_AT[_name] = _n
    _n += _w
NCOL = _n

TABS = [("ident", P), ("stack", WIN), ("ones", P), ("tri", P), ("iota", NPAIR), ("g99", G), ("e99", EPG),
        ("eid", NE), ("negt", TT), ("tmask", TT), ("kcos", TT * ROPE), ("ksin", TT * ROPE), ("qtab", S)]
TAB_AT, _n = {}, 0
for _name, _w in TABS:
    TAB_AT[_name] = _n
    _n += _w
NTAB = _n


def _tables():
    f = np.float32
    t = np.zeros((P, NTAB), f)

    def put(name, v):
        v = np.asarray(v, f)
        t[:v.shape[0], TAB_AT[name]:TAB_AT[name] + v.shape[1]] = v

    p = np.arange(P)
    put("ident", np.eye(P))
    put("stack", p[:, None] % WIN == np.arange(WIN)[None, :])
    put("ones", np.ones((P, P)))
    put("tri", p[:, None] < p[None, :])
    put("iota", np.tile(np.arange(NPAIR), (P, 1)))
    put("g99", np.tile(np.arange(G) - 99.0, (P, 1)))
    put("e99", np.tile(np.arange(EPG) - 99.0, (P, 1)))
    put("eid", np.tile(np.arange(NE), (P, 1)))
    tok = np.arange(TT)[None, :] * P + p[:, None]
    put("negt", -(tok / S))
    put("tmask", tok != 0)
    half = ROPE // 2
    inv = f(10000.0) ** (-np.arange(half, dtype=f) / f(half))
    ang = np.arange(S, dtype=f)[:, None] * inv[None, :]
    cos, sin = np.cos(ang.astype(np.float64)), np.sin(ang.astype(np.float64))
    c2 = np.concatenate([cos, cos], 1).reshape(TT, P, ROPE).transpose(1, 0, 2)
    s2 = np.concatenate([-sin, sin], 1).reshape(TT, P, ROPE).transpose(1, 0, 2)
    put("kcos", c2.reshape(P, -1))
    put("ksin", s2.reshape(P, -1))
    scale = (NOPE + ROPE) ** -0.5
    put("qtab", np.concatenate([np.full((NOPE, S), scale), scale * cos.T, scale * cos.T,
                                -scale * sin.T, scale * sin.T], 0))
    tt, ff = np.arange(S)[:, None], np.arange(S)[None, :]
    th = 2 * np.pi * tt * ff / (2 * S)
    alt = (-1.0) ** np.arange(S)
    cosm, sinm = np.cos(th), -np.sin(th)
    packed = sinm.copy()
    packed[:, 0] = alt
    cos0 = cosm[:, :P].copy()
    cos0[:, 0] = alt
    inv_c, inv_s = 2 * np.cos(th.T) / (2 * S), -2 * np.sin(th.T) / (2 * S)
    inv_c[0] = 1 / (2 * S)
    inv_s[0] = alt / (2 * S)

    def split(m):
        return m.reshape(TT, P, -1).transpose(1, 0, 2).reshape(P, -1)

    dft = np.concatenate([split(cosm), split(packed), split(inv_c), split(inv_s)], 1).astype(f)
    filt = np.concatenate([split(sinm), split(cos0)], 1).astype(f)
    pos = np.arange(S, dtype=f)
    bands = np.linspace(1e-4, (EMB - 1) // 2 - 1, (EMB - 1) // 2, dtype=f)
    za = (f(2.0 * np.pi) * pos[:, None] * bands[None, :] / f(S)).astype(np.float64)
    z = np.concatenate([(pos / S)[:, None], np.cos(za), -np.sin(za)], 1).T
    feat = np.zeros((P, S), f)
    feat[:EMB] = z
    n = S - 1 - np.arange(2 * S)
    exact = BUCKETS // 2
    large = exact + (np.log(np.maximum(n, 1).astype(f) / f(exact)) / f(np.log(MAX_DIST / exact))
                     * f(BUCKETS - exact)).astype(np.int32)
    bucket = np.where(n < 0, BUCKETS, np.where(n < exact, n, np.minimum(large, BUCKETS - 1)))
    onehot = np.zeros((P, 2 * S), f)
    onehot[bucket, np.arange(2 * S)] = 1
    return t, dft, filt, feat, onehot


UNITS = [("filt", 2048 + 2048 + 512 + 256 + 256 + 64 + 64), ("lat", KD * LAT), ("hy0", KD * HW), ("hy1", KD * HW), ("hy2", KD * HW),
         ("mla", 2 * H1 * P + H1 * NOPE + H1 * VD)] \
    + [(f"ada{i}", 4096) for i in range(6)] \
    + [(n, 4096) for n in ("mk0", "mk1", "mv0", "mv1", "wo0", "wo1", "mq0", "mq1", "ada6", "ada7", "mo0", "mo1",
                           "ada8", "ada9")]
UNITS1 = len(UNITS)
UNITS2 = [(n, 4096) for n in ("ada10", "ada11", "win0", "win1", "win2", "win3", "win4", "wp0", "wp1")]
PLACE = {n: i for i, (n, _) in enumerate(UNITS)}
MOE_AT = [UNITS1, UNITS1 + NE + len(UNITS2)]
PLACE.update({n: UNITS1 + NE + i for i, (n, _) in enumerate(UNITS2)})

GU = 2 * KD * FE
FEAT = S + 2 * FFN

STAGES = [("f1", 1), ("f2", 1), ("f3_0", 4), ("hT", 4), ("sp0", 5), ("f3_1", 4), ("lat", 2), ("sp1", 5),
          ("hy0", 2), ("hy1", 2), ("hyT0", 2), ("latT", 2), ("hy2", 2), ("hyT1", 2),
          ("uq", 4), ("uk", 4), ("uv", 2), ("hyT2", 2), ("zs0", 4)]
STAGES += [("sc0", 1), ("sc1", 1)]
for _h in range(H1):
    STAGES += ([(f"ada{_h}", 1)] if _h < 6 else []) + [(f"pT{_h}", 1)] \
        + ([(f"adac{_h}", 1)] if _h < 6 else []) + ([(f"sc{_h + 2}", 1)] if _h + 2 < H1 else []) + [(f"pv{_h}", 1)]
    if _h == 2:
        STAGES += [("cv0", 2)]
    if _h == 5:
        STAGES += [("zs1", 4)]
STAGES += [("cv1", 2), ("memT", 4), ("mk", 4), ("mv", 4), ("mixT", 4), ("wo", 4), ("cT", 4), ("mq", 4),
           ("xs0", 1), ("xs1", 1)]
for _h in range(XH):
    STAGES += ([(f"ada{6 + _h}", 1)] if _h < 2 else []) + [(f"xT{_h}", 1)] \
        + ([(f"adac{6 + _h}", 1)] if _h < 2 else []) + ([(f"xs{_h + 2}", 1)] if _h + 2 < XH else []) + [(f"xv{_h}", 1)]
STAGES += [("mo", 4)]


def _moe_stages(b):
    ada = [[(f"ada{i}", 1), (f"adac{i}", 1)] if b == 1 else [] for i in (8, 9)]
    return [(f"rT{b}", 4), (f"rt{b}", 1)] + ada[0] + [(f"cnt{b}", 1)] + ada[1] + [(f"gx{b}", 8), (f"swT{b}", 2), (f"yT{b}", 8)] \
        + [("g2r", 2)] * (b == 2) + [(f"sct{b}", 4)]


STAGES += _moe_stages(1)
STAGES += [("bias", 1), ("ada10", 1), ("ada11", 1), ("adac10", 1), ("adac11", 1)]
STAGES += [("uT", 4), ("xl", 2), ("g1r", 2), ("yl", 2), ("ga", 2), ("gx", 2), ("aq", 2), ("ak", 2), ("av", 2)]
STAGES += [("as0", 1), ("as1", 1)]
for _h in range(H1):
    STAGES += [(f"aT{_h}", 1)] + ([(f"as{_h + 2}", 1)] if _h + 2 < H1 else []) + [(f"ap{_h}", 1)]
STAGES += [("lss", 1), ("wpa", 2), ("aoT", 2), ("wpb", 6)]
STAGES += _moe_stages(2)
BANK_AT, _n = {}, 0
for _name, _w in STAGES:
    BANK_AT[_name] = (_n, _w)
    _n += _w



WP = [("wpa", j) for j in range(2)] + [("wpb", j) for j in range(6)]

LAST = {"filt": ("sp1", 4), "lat": ("lat", 1), "hy0": ("hy0", 1), "hy1": ("hy1", 1), "hy2": ("hy2", 1), "mla": ("uv", 1)}
for _s, _st in (("mk", "mk"), ("mv", "mv"), ("wo", "wo"), ("mq", "mq"), ("mo", "mo")):
    LAST.update({f"{_s}0": (_st, 1), f"{_s}1": (_st, 3)})
LAST.update({f"ada{_i}": (f"adac{_i}", 0) for _i in range(12)})
LAST.update({f"win{_i}": (_st, 1) for _i, _st in enumerate(("xl", "yl", "aq", "ak", "av"))})
LAST.update({"wp0": WP[3], "wp1": WP[7]})


SPLIT = ["lat", "hy0", "hy1", "hy2", "mk0", "mk1", "mv0", "mv1", "wo0", "wo1", "mq0", "mq1", "mo0", "mo1",
         "win0", "win1", "win2", "win3", "win4", "wp0", "wp1"]
CHUNKS = KD // 2

SQUARES = [("x", 2), ("l", 4), ("ao", 2), ("m", 2), ("z", 2), ("c", 2), ("r", 2), ("f", 2), ("a", 2)]
ROOTS = [(_t, 1) for _t in ("x", "lq", "lkv", "ao", "m", "z", "c", "r", "f0", "f1", "ln0", "a", "lru", "ln1", "ln2", "ln3")]
NORMS = [(_t, 2) for _t in ("xn_x", "ao_n", "xn_m", "z_n", "xn_c", "xn_r1", "xn_u", "ao2_n", "xn_r2")]


def upto(order, tag, t=None):
    n = 0
    for name, w in order:
        if name == tag:
            return n + (w if t is None else t + 1)
        n += w
    raise KeyError(tag)


def two_blocks(nc, A, out):
    ctx = ExitStack()
    with ctx:
        def sb(name, shape, dt=F32):
            return ctx.enter_context(nc.sbuf_tensor(name, shape, dt))

        made = {}

        def sem(name):
            if name not in made:
                made[name] = ctx.enter_context(nc.semaphore(name))
            return made[name]

        tab = sb("tab", [P, NTAB])
        col = sb("col", [P, NCOL])
        X = sb("X", [P, TT, D])
        ROW = sb("ROW", [P, TT * D])
        st = sb("st", [P, 330])
        tabi = sb("tabi", [1, 64], I32)
        wr = sb("wr", [P, 2, KD * (G + NE)])
        keep = sb("keep", [P, 2 * (G + NE) + NE])
        biasr, zero32 = [keep[:, 0:36], keep[:, 36:72]], keep[:, 72:104]
        mod = sb("mod", [P, 48])
        cm = sb("cm", [P, KD, 32])
        AR = 17408
        with ExitStack() as again:
            def twice(name, shape):
                return again.enter_context(nc.sbuf_tensor(name, shape, F32))

            ring = twice("ring", [P, RING, SLOT])
            HTf = twice("HT", [P, KD * S])
            XNf = twice("XN", [P, TT * D])
            arena = twice("arena", [P, AR])
        rounded = {t.name: sb(t.name + "_r", shape, F32R)
                   for t, shape in ((ring, [P, RING, SLOT]), (HTf, [P, KD * S]), (XNf, [P, TT * D]), (arena, [P, AR]))}
        bank = [ctx.enter_context(nc.psum_tensor(f"bank{i}", [P, 512], F32)) for i in range(8)]
        bias_rows = nc.dram_tensor("bias_rows", (H1, P, BW), F32, kind="Internal").ap()

        def three(ap, a):
            return ap.rearrange("p (a b) -> p a b", a=a)

        HT = three(HTf[:, :], KD)
        XN = three(XNf[:, :], TT)

        def T(name, rows=P):
            return tab[0:rows, TAB_AT[name]:TAB_AT[name] + dict(TABS)[name]]

        def C(name, k=0, w=1, rows=P):
            return col[0:rows, COL_AT[name] + k:COL_AT[name] + k + w]

        ident, ones, stack = T("ident"), T("ones"), T("stack")
        used = {"st": 0, "route": 0}

        def stat(n):
            used["st"] += n
            assert used["st"] <= 330
            return st[:, used["st"] - n:used["st"]]

        def area(at, n):
            assert at + n <= AR
            return arena[:, at:at + n]

        dft = area(0, 2048)
        fwd_c, fwd_s = three(dft[:, 0:512], TT), three(dft[:, 512:1024], TT)
        inv_c, inv_s = three(dft[:, 1024:1536], TT), three(dft[:, 1536:2048], TT)
        even, odd = three(area(2048, 1024), TT), three(area(3072, 1024), TT)
        spec_r, spec_i = three(area(2048, 1024), TT), three(area(3072, 1024), TT)
        k_c = [three(area(4096 + 2560 * n, 1024), TT) for n in range(ORDER)]
        k_s = [three(area(5120 + 2560 * n, 1024), TT) for n in range(ORDER)]
        k_c0 = [area(6144 + 2560 * n, 512) for n in range(ORDER)]
        filt_f, filt_b = area(6656, 512), area(7168, 512)
        env = three(area(7680, 1024), 2)
        hytok = area(9216, 3072).rearrange("p (t w c) -> p t w c", t=TT, w=3)
        Z = hytok[:, :, 2, :]
        conv_t = three(area(12288, 1024), 4)
        skip_z = three(area(12288, 1024), TT)
        prod = three(area(13312, 1024), TT)
        krb = three(area(13312, 256), TT)
        arg, turn = area(13568, 256), area(13824, 256)
        lat = three(area(14336, TT * LAT), TT)
        latTb = three(area(15360, 1024), 4)
        h1, h2 = area(16384, 256), area(16640, 256)
        V1 = three(area(16384, 1024), TT)
        junk = area(16384, 1024)
        prob = area(14336, 1024).rearrange("p (i t k) -> p i t k", i=2, t=TT)
        probT = area(15360, 1024).rearrange("p (i t k) -> p i t k", i=2, t=TT)
        QT, KT = three(HTf[:, :], H1), three(XNf[:, :], H1)
        AO, skip = three(ROW[:, 0:1024], TT), three(ROW[:, 1024:2048], ORDER)
        KM, VM = three(area(4096, 2048), KD), three(area(6656, 2048), TT)
        low_x, low_m = three(XNf[:, :], KD), three(area(12288, 2048), KD)
        QX, oT = three(area(0, 2048), KD), three(area(2048, 2048), KD)
        xsT, ysT = three(area(0, KD * SORTED), KD), three(area(KD * SORTED, KD * SORTED), KD)
        at = 2 * KD * SORTED
        gu_sb = three(area(at, 1024), 2)
        d_sb = area(at + 1024, 1024)
        xwin = area(at + 2048, 1024).rearrange("p (i k w) -> p i k w", i=2, k=KD)
        sg, hb = three(area(at + 3072, 256), 2), three(area(at + 3328, 128), 2)
        sel, selw = three(area(at + 3584, 1024), TT), three(area(at + 4608, 1024), TT)
        swT = three(area(at + 5632, 1024), NPAIR // P)
        ytok = three(area(0, NPAIR // P * D), NPAIR // P)
        xn_high = three(area(KD * SORTED + NPAIR, 2048), TT)
        xn_low = three(area(KD * SORTED + NPAIR + 2048, 2048), TT)
        ytok_low = three(area(at + 1536, NPAIR // P * D), NPAIR // P)
        swT_low = three(XNf[:, 0:1024], NPAIR // P)
        diag2, g2row = three(HTf[:, 0:1024], KD), HTf[:, 1024:2048]
        oneh, relb, brow = HTf[:, 0:512], HTf[:, 512:512 + H1], HTf[:, 1024:1536]
        route_at = at + 6656

        def route(n):
            used["route"] += n
            assert route_at + used["route"] <= AR
            return area(route_at + used["route"] - n, n)

        BT = three(area(0, 3072), H1)
        xc, rg, ig, aa, th, hh, gy, sq = [three(area(3072 + 1024 * i, 1024), 4) for i in range(8)]
        diag1 = three(area(10240, 1024), KD)
        Q2, K2 = three(area(11264, 1024), 4), three(area(12288, 1024), 4)
        V2 = three(area(13312, 1024), TT)
        prob2, probT2 = three(area(14336, 768), 2), three(area(15104, 768), 2)
        score = area(15872, 384)
        g1row = area(16256, 1024)
        AO2 = XN[:, :, 0:HW]
        aoT, loT, ao_low, lo_low = rg, ig, xc, aa

        def place(stage, j):
            base, n = BANK_AT[stage]
            assert j < n, stage
            return (base + j) % 8, (base + j) // 8

        taken = [0]

        def take(pe, stage, j=0):
            assert BANK_AT[stage][0] + j == taken[0], (stage, j, taken)
            taken[0] += 1
            b, use = place(stage, j)
            if use:
                pe.wait_ge(sem(f"bank_free{b}"), use)
            return bank[b]

        def full(last, stage, j=0):
            last.then_inc(sem(f"bank_full{place(stage, j)[0]}"), 1)

        def got(eng, stage, j=0):
            b, use = place(stage, j)
            eng.wait_ge(sem(f"bank_full{b}"), use + 1)
            return bank[b]

        def free(last, stage, j=0):
            last.then_inc(sem(f"bank_free{place(stage, j)[0]}"), 1)

        def ready(eng, stage, j=0):
            b, use = place(stage, j)
            eng.wait_ge(sem(f"bank_free{b}"), use + 1)

        def slot(i):
            return i % RING

        def arrived(eng, name):
            i = PLACE[name]
            eng.wait_ge(sem(f"slot_full{slot(i)}"), 16 * (i // RING + 1))
            return ring[:, slot(i), :]

        def vacated(sp, i):
            prev = i - RING
            if prev < 0:
                return
            for b, m in enumerate(MOE_AT):
                if m <= prev < m + NE:
                    sp.wait_ge(sem(f"down_done{b + 1}"), prev - m + 1)
                    return
            name = next(n for n, q in PLACE.items() if q == prev)
            stage, j = LAST[name]
            b, use = place(stage, j)
            sp.wait_ge(sem(f"bank_full{b}"), use + 1)

        def R(ap):
            return bass.AP(rounded[ap.tensor.name], ap.offset, ap.ap)

        def part_at(name, c):
            cols = (dict(UNITS + UNITS2)[name]) // KD
            u = ring[:, slot(PLACE[name]), :]
            hi = KD * cols + (c % 2) * 2 * cols
            return three(u[:, 2 * c * cols:(2 * c + 2) * cols], 2), three(u[:, hi:hi + 2 * cols], 2)

        def chunks_to(name, c):
            return CHUNKS * SPLIT.index(name) + c + 1

        def high(act, name, chunks):
            arrived(act, name)
            for c in chunks:
                if c >= 2:
                    if name in ("wp0", "wp1") and c == 3:
                        got(act, *WP[4 * int(name[2]) + 1])
                    else:
                        act.wait_ge(sem("w_used"), 2 * SPLIT.index(name) + c - 1 - (name == "wp1"))
                w, h = part_at(name, c)
                nc.scalar.activation(R(h), w, ACT.Copy).then_inc(sem("w_high"), 1)

        def low(dve, name, chunks):
            for c in chunks:
                dve.wait_ge(sem("w_high"), chunks_to(name, c))
                w, h = part_at(name, c)
                nc.vector.tensor_tensor(R(w), w, R(h), ALU.subtract).then_inc(sem("w_low"), 1)

        def ada_sum(i):
            return ring[:, slot(PLACE[f"ada{i}"]), 4096:4608]

        ssq_x, rstd_x = stat(2), stat(2)
        ssq_l, rstd_l = stat(4), stat(4)
        ssq_m, rstd_m = stat(2), stat(2)
        ssq_o, rstd_o = stat(4), stat(4)
        ssq_c, rstd_c = stat(2), stat(2)
        ssq_r, rstd_r = stat(2), stat(2)
        ssq_f, rstd_f = stat(2), stat(2)
        nmax, rsum, rinv = three(stat(16), H1), three(stat(16), H1), three(stat(16), H1)
        xmax, xsum, xinv = three(stat(8), XH), three(stat(8), XH), three(stat(8), XH)
        amax, asum, ainv = three(stat(16), H1), three(stat(16), H1), three(stat(16), H1)
        bn_ = [[stat(12) for _ in range(TT)] for _ in range(4)]
        mv_ = [three(stat(4), TT) for _ in range(4)]
        rstd_n = [stat(2) for _ in range(4)]
        ssq_a, rstd_a = stat(4), stat(4)
        sp_l, sp8 = stat(28), stat(4)
        sp8n = stat(4)
        half_neg = stat(4)
        L = three(route(72), TT)
        gmx, gex, gsum, pgrp = route(2), three(route(8), TT), route(2), route(2)
        ohg, cand4, i1g = three(route(8), TT), three(route(8), TT), route(2)
        ein, ein2, cand8 = three(route(16), TT), three(route(16), TT), three(route(16), TT)
        spread = route(64).rearrange("p (t g e) -> p t g e", t=TT, g=G)
        m1, m2, i1, i2, ex2, w1, w2 = [route(2) for _ in range(7)]
        oh1, oh2 = three(route(16), TT), three(route(16), TT)
        M1, M2, M12, posm = [three(route(64), TT) for _ in range(4)]
        counts, starts, incl, nx, xincl, xex, cm64 = [route(32) for _ in range(7)]
        pos1, pos2 = route(2), route(2)
        mk8, tm8, mk8b = [three(route(NX * NE), NX) for _ in range(3)]
        xst, xid = route(NX), route(NX)

        block = ctx.enter_context(nc.Block())
        W_MOE = [A["experts"], A["experts_2"]]

        @block.sync
        def _(sp):
            def load(i, src, width):
                vacated(sp, i)
                sp.dma_start(ring[:, slot(i), 0:width], src).then_inc(sem(f"slot_full{slot(i)}"), 16)

            def experts(b):
                base = MOE_AT[b]
                w = W_MOE[b]
                for e in range(RING):
                    load(base + e, w[e, :, 0:GU], GU)
                    sp.dma_start(ring[:, slot(base + e), GU:SLOT], w[e, :, GU:SLOT]
                                 ).then_inc(sem(f"slot_down{e}"), 16)
                with sp.Fori(RING, NE - RING + 1, RING) as e0:
                    for r in range(RING):
                        s = slot(base + r)
                        src = w[bass.ds(e0 + r, 1)].rearrange("a p f -> p (a f)")
                        sp.wait_ge(sem(f"gu_done{b + 1}"), e0 + (r - RING + 1))
                        sp.dma_start(ring[:, s, 0:GU], src[:, 0:GU]).then_inc(sem(f"slot_full{s}"), 16)
                        sp.wait_ge(sem(f"down_done{b + 1}"), e0 + (r - RING + 1))
                        sp.dma_start(ring[:, s, GU:SLOT], src[:, GU:SLOT]).then_inc(sem(f"slot_down{r}"), 16)
                s = slot(base)
                sp.wait_ge(sem(f"routed{b + 1}"), 1)
                n = sp.value_load(tabi[0:1, 48:49], min_val=0, max_val=NX - 1)
                sp.wait_ge(sem(f"down_done{b + 1}"), NE - RING + 1)
                with sp.If(n > 0):
                    with sp.Fori(0, n) as j:
                        e = sp.value_load(tabi[0:1, bass.ds(40 + j, 1)], min_val=0, max_val=NE - 1)
                        sp.wait_ge(sem(f"extra_down{b + 1}"), j + 1)
                        sp.dma_start(ring[:, s, :], w[bass.ds(e, 1)].rearrange("a p f -> p (a f)")
                                     ).then_inc(sem(f"extra_w{b + 1}"), 16)
                return n

            at = dict(UNITS)["filt"] - FEAT
            sp.dma_start(ring[:, slot(0), at:at + FEAT], A["filt"][:, at:at + FEAT]).then_inc(sem("feat"), 16)
            sp.dma_start(col[:, :], A["col"]).then_inc(sem("tab"), 16)
            sp.dma_start(tab[:, :], A["tab"]).then_inc(sem("tab"), 16)
            sp.dma_start(ring[:, slot(0), 0:at], A["filt"][:, 0:at]).then_inc(sem(f"slot_full{slot(0)}"), 16)
            for t in range(TT):
                sp.dma_start(X[:, t, :], A["x"][t * P:(t + 1) * P, :]).then_inc(sem(f"x_in{t}"), 16)
            sp.dma_start(dft, A["dft"]).then_inc(sem("dft"), 16)
            for i, (name, width) in list(enumerate(UNITS))[1:]:
                load(i, A[name], width)
                if name == "hy0":
                    sp.dma_start(ROW[:, 1024:2048], bass.AP(A["hy_skip"].tensor, 0, [[0, P], [1, ORDER * HW]])
                                 ).then_inc(sem("skip"), 16)
            n = experts(0)
            for i, (name, width) in enumerate(UNITS2):
                if slot(MOE_AT[0] + NE + i) == slot(MOE_AT[0]) and i < RING:
                    sp.wait_ge(sem("extra_down1"), n + 1)
                load(MOE_AT[0] + NE + i, A[name], width)
            experts(1)
            sp.wait_ge(sem("stored"), 16 * TT)

        @block.tensor
        def _(pe):
            mm, tr = nc.tensor.matmul, nc.tensor.transpose

            def transposed(stage, src, n, ready_sem):
                for j in range(n // 2):
                    ps = take(pe, stage, j)
                    for a in range(2):
                        for t in range(TT):
                            pe.wait_ge(sem("normed"), upto(NORMS, ready_sem, t))
                            last = tr(ps[:, a * S + t * P:a * S + (t + 1) * P],
                                      src[:, t, (2 * j + a) * P:(2 * j + a + 1) * P], ident)
                    full(last, stage, j)

            def banks_of(stage):
                return [(stage, j) for j in range(4)]

            def all_ready(stage, n):
                for j in range(n):
                    ready(pe, stage, j)

            def three_pass(ps, sides, first, last_):
                (ah, al), (bh, bl) = sides
                mm(ps, R(ah), R(bh), start=first, stop=False)
                mm(ps, R(ah), R(bl), start=False, stop=False)
                return mm(ps, R(al), R(bh), start=False, stop=last_)

            def token_out(stage, units, x, x_low, src, banks=((0, 1), (2, 3))):
                for name, js in zip(units, banks):
                    cols = dict(UNITS + UNITS2)[name] // KD
                    for c in range(CHUNKS):
                        if c == 0:
                            ps = [take(pe, stage, j) for j in js]
                        ready(pe, *src[c])
                        pe.wait_ge(sem("w_low"), chunks_to(name, c))
                        wl, wh = part_at(name, c)
                        for a in range(2):
                            k = 2 * c + a
                            for t in range(TT):
                                tok = slice(t * P, (t + 1) * P)
                                last = three_pass(ps[t][:, 0:cols], ((x[:, k, tok], x_low[:, k, tok]), (wh[:, a, :], wl[:, a, :])),
                                                  k == 0, k == KD - 1)
                                if k == KD - 1:
                                    full(last, stage, js[t])
                        if c < 2:
                            last.then_inc(sem("w_used"), 1)

            def channel_out(stage, units, x, x_low, src):
                for u, name in enumerate(units):
                    ps = [take(pe, stage, 2 * u + i) for i in range(2)]
                    for c in range(CHUNKS):
                        ready(pe, *src[c])
                        pe.wait_ge(sem("w_low"), chunks_to(name, c))
                        wl, wh = part_at(name, c)
                        for a in range(2):
                            k = 2 * c + a
                            for i in range(4):
                                o = slice(i * P, (i + 1) * P)
                                last = three_pass(ps[i // 2][:, (i % 2) * S:(i % 2 + 1) * S],
                                                  ((wh[:, a, o], wl[:, a, o]), (x[:, k, :], x_low[:, k, :])),
                                                  k == 0 and i % 2 == 0, k == KD - 1 and i % 2 == 1)
                                if k == KD - 1 and i % 2:
                                    full(last, stage, 2 * u + i // 2)
                        if c < 2:
                            last.then_inc(sem("w_used"), 1)

            fw = ring[:, slot(PLACE["filt"]), :]
            w3, sin_m, cos_0 = fw[:, 0:2048], three(fw[:, 4096:4608], TT), three(fw[:, 4608:4864], TT)
            feat, fw1, fw2 = fw[0:EMB, 4864:5120], fw[0:EMB, 5120:5184], fw[0:FFN, 5184:5248]
            pe.wait_ge(sem("feat"), 16)
            ps = take(pe, "f1")
            full(mm(ps[0:FFN, 0:S], fw1, feat, start=True, stop=True), "f1")
            pe.wait_ge(sem("sine"), 1)
            ps = take(pe, "f2")
            full(mm(ps[0:FFN, 0:S], fw2, h1[0:FFN, :], start=True, stop=True), "f2")

            def hyena_tok(third):
                for j in range(2):
                    ready(pe, f"hy{third}", j)
                for t in range(TT):
                    ps = take(pe, f"hyT{third}", t)
                    for i in range(4):
                        last = tr(ps[:, i * P:(i + 1) * P], conv_t[:, i, t * P:(t + 1) * P], ident)
                    full(last, f"hyT{third}", t)

            def filters(n):
                pe.wait_ge(sem("sine"), 2)
                pe.wait_ge(sem("h2_one"), 1)
                for t in range(TT):
                    for d in range(2):
                        ps = take(pe, f"f3_{n}", 2 * t + d)
                        c = (2 * n + d) * HW
                        full(mm(ps[:, :], h2[0:FFN + 1, t * P:(t + 1) * P], w3[0:FFN + 1, c:c + HW],
                                start=True, stop=True), f"f3_{n}", 2 * t + d)

            def filter_spectra(n):
                pe.wait_ge(sem("parts"), 2 * TT * (n + 1))
                cases = [(fwd_c[:, :, 0:P], even), (fwd_c[:, :, P:S], even), (sin_m[:, :, 0:P], odd),
                         (sin_m[:, :, P:S], odd), (cos_0, even)]
                pe.wait_ge(sem("dft"), 16)
                for j, (m, src) in enumerate(cases):
                    ps = take(pe, f"sp{n}", j)
                    for t in range(TT):
                        last = mm(ps[:, :], m[:, t, :], src[:, t, :], start=t == 0, stop=t == TT - 1)
                    full(last, f"sp{n}", j)

            def z_spectrum(n):
                if n == 0:
                    for t in range(TT):
                        ready(pe, "hyT2", t)
                else:
                    pe.wait_ge(sem("zed"), TT * n)
                for f in range(TT):
                    for j, m in ((2 * f, fwd_c), (2 * f + 1, fwd_s)):
                        ps = take(pe, f"zs{n}", j)
                        for t in range(TT):
                            last = mm(ps[:, :], m[:, t, f * P:(f + 1) * P], Z[:, t, :], start=t == 0, stop=t == TT - 1)
                        full(last, f"zs{n}", j)

            def convolve(n):
                pe.wait_ge(sem("product"), TT * (n + 1))
                for t in range(TT):
                    ps = take(pe, f"cv{n}", t)
                    for f in range(TT):
                        mm(ps[:, :], inv_c[:, f, t * P:(t + 1) * P], spec_r[:, f, :], start=f == 0, stop=False)
                        last = mm(ps[:, :], inv_s[:, f, t * P:(t + 1) * P], spec_i[:, f, :],
                                  start=False, stop=f == TT - 1)
                    full(last, f"cv{n}", t)

            def ada(i):
                w = three(arrived(pe, f"ada{i}")[:, 0:4096], KD)
                ps = take(pe, f"ada{i}")
                for k in range(KD):
                    g = 32 * (k % 4)
                    last = mm(ps[g:g + 32, :], cm[:, k, :], w[:, k, :], start=k < 4, stop=k >= 4)
                full(last, f"ada{i}")

            def ada_col(i):
                ready(pe, f"ada{i}")
                ps = take(pe, f"adac{i}")
                for c in range(4):
                    last = mm(ps[:, c:c + 1], ada_sum(i)[:, c * P:(c + 1) * P], ones[:, 0:1], start=True, stop=True)
                full(last, f"adac{i}")

            arrived(pe, "filt")
            filters(0)
            pe.wait_ge(sem("tab"), 32)
            transposed("hT", XN, KD, "xn_x")
            filter_spectra(0)
            filters(1)
            token_out("lat", ["lat"], HT, low_x, banks_of("hT"))
            filter_spectra(1)
            channel_out("hy0", ["hy0"], HT, low_x, banks_of("hT"))
            channel_out("hy1", ["hy1"], HT, low_x, banks_of("hT"))
            hyena_tok(0)
            pe.wait_ge(sem("lat_n"), 3)
            for j, srcs in ((0, (lat[:, :, 0:P], lat[:, :, P:QR])), (1, (lat[:, :, QR:QR + KVR], krb))):
                ps = take(pe, "latT", j)
                for a, src in enumerate(srcs):
                    for t in range(TT):
                        last = tr(ps[:, a * S + t * P:a * S + (t + 1) * P], src[:, t, :], ident)
                full(last, "latT", j)
            channel_out("hy2", ["hy2"], HT, low_x, banks_of("hT"))
            hyena_tok(1)
            w = arrived(pe, "mla")
            wq, wk, wv = three(w[:, 0:2048], 2), w[:, 2048:2560], w[:, 2560:3072]
            for j in range(2):
                ready(pe, "latT", j)
            for j in range(4):
                ps = take(pe, "uq", j)
                for a in range(2):
                    h = 2 * j + a
                    for k in range(2):
                        last = mm(ps[:, a * S:(a + 1) * S], wq[:, k, h * P:(h + 1) * P], latTb[:, k, :],
                                  start=k == 0, stop=k == 1)
                full(last, "uq", j)
            for j in range(4):
                ps = take(pe, "uk", j)
                for a in range(2):
                    h = 2 * j + a
                    last = mm(ps[0:NOPE, a * S:(a + 1) * S], wk[:, h * NOPE:(h + 1) * NOPE], latTb[:, 2, :],
                              start=True, stop=True)
                full(last, "uk", j)
            for t in range(TT):
                ps = take(pe, "uv", t)
                full(mm(ps[:, :], latTb[:, 2, t * P:(t + 1) * P], wv, start=True, stop=True), "uv", t)
            hyena_tok(2)
            z_spectrum(0)
            for j in range(4):
                ready(pe, "uq", j)
                ready(pe, "uk", j)
            pe.wait_ge(sem("k_rope"), 1)
            for t in range(TT):
                ready(pe, "uv", t)

            def mla_scores(h):
                ps = take(pe, f"sc{h}")
                for t in range(TT):
                    last = mm(ps[:, t * S:(t + 1) * S], QT[:, h, t * P:(t + 1) * P], KT[:, h, :], start=True, stop=True)
                full(last, f"sc{h}")

            def probs_T(stage, src):
                ps = take(pe, stage)
                for kt in range(TT):
                    for t in range(TT):
                        last = tr(ps[:, kt * S + t * P:kt * S + (t + 1) * P], src[:, t, kt * P:(kt + 1) * P], ident)
                full(last, stage)

            mla_scores(0)
            mla_scores(1)
            pe.wait_ge(sem("cm"), 1)
            for h in range(H1):
                if h < 6:
                    ada(h)
                ready(pe, f"sc{h}")
                probs_T(f"pT{h}", prob[:, h % 2])
                if h < 6:
                    ada_col(h)
                if h + 2 < H1:
                    mla_scores(h + 2)
                ready(pe, f"pT{h}")
                ps = take(pe, f"pv{h}")
                for t in range(TT):
                    for kt in range(TT):
                        last = mm(ps[:, t * VD:(t + 1) * VD], probT[:, h % 2, kt, t * P:(t + 1) * P],
                                  V1[:, kt, h * VD:(h + 1) * VD], start=kt == 0, stop=kt == TT - 1)
                full(last, f"pv{h}")
                if h == 2:
                    convolve(0)
                if h == 5:
                    z_spectrum(1)
            convolve(1)
            transposed("memT", XN, KD, "xn_m")
            channel_out("mk", ["mk0", "mk1"], HT, low_m, banks_of("memT"))
            token_out("mv", ["mv0", "mv1"], HT, low_m, banks_of("memT"))
            for j in range(4):
                ps = take(pe, "mixT", j)
                src, c = (AO, 2 * j) if j < 2 else (Z, 2 * j - 4)
                for a in range(2):
                    for t in range(TT):
                        pe.wait_ge(sem("normed"), upto(NORMS, "ao_n" if j < 2 else "z_n", t))
                        last = tr(ps[:, a * S + t * P:a * S + (t + 1) * P], src[:, t, (c + a) * P:(c + a + 1) * P], ident)
                full(last, "mixT", j)
            token_out("wo", ["wo0", "wo1"], HT, low_m, banks_of("mixT"))
            transposed("cT", XN, KD, "xn_c")
            channel_out("mq", ["mq0", "mq1"], HT, low_m, banks_of("cT"))
            all_ready("mq", 4)
            all_ready("mk", 4)

            def x_scores(h):
                ps = take(pe, f"xs{h}")
                for t in range(TT):
                    for k in range(2):
                        last = mm(ps[:, t * S:(t + 1) * S], QX[:, 2 * h + k, t * P:(t + 1) * P], KM[:, 2 * h + k, :],
                                  start=k == 0, stop=k == 1)
                full(last, f"xs{h}")

            x_scores(0)
            x_scores(1)
            for h in range(XH):
                if h < 2:
                    ada(6 + h)
                pe.wait_ge(sem("x_prob"), TT * (h + 1))
                probs_T(f"xT{h}", prob[:, h % 2])
                if h < 2:
                    ada_col(6 + h)
                if h + 2 < XH:
                    x_scores(h + 2)
                ready(pe, f"xT{h}")
                ps = take(pe, f"xv{h}")
                for d in range(2):
                    for m in range(TT):
                        last = mm(ps[:, d * S:(d + 1) * S], VM[:, m, h * XHD + d * P:h * XHD + (d + 1) * P],
                                  probT[:, h % 2, m, :], start=m == 0, stop=m == TT - 1)
                full(last, f"xv{h}")
            token_out("mo", ["mo0", "mo1"], oT, low_m, [(f"xv{h}", 0) for h in range(XH)])

            def moe(b):
                transposed(f"rT{b}", XN, KD, f"xn_r{b}")
                pe.wait_ge(sem("wr"), 16 * b)
                w = three(wr[:, b - 1, :], KD)
                ps = take(pe, f"rt{b}")
                for k in range(KD):
                    ready(pe, f"rT{b}", k // 2)
                    for t in range(TT):
                        last = mm(ps[:, t * 64:t * 64 + G + NE], HT[:, k, t * P:(t + 1) * P], w[:, k, :],
                                  start=k + t == 0, stop=k == KD - 1 and t == TT - 1)
                full(last, f"rt{b}")
                if b == 1:
                    ada(8)
                    ada_col(8)
                pe.wait_ge(sem(f"hot{b}"), 1)
                ps = take(pe, f"cnt{b}")
                mm(ps[:, 0:NE], T("tri"), M12[:, 0, :], start=True, stop=True)
                mm(ps[:, NE:2 * NE], T("tri"), M12[:, 1, :], start=True, stop=False)
                mm(ps[:, NE:2 * NE], ones, M12[:, 0, :], start=False, stop=True)
                mm(ps[:, 2 * NE:3 * NE], ones, M12[:, 0, :], start=True, stop=False)
                full(mm(ps[:, 2 * NE:3 * NE], ones, M12[:, 1, :], start=False, stop=True), f"cnt{b}")
                if b == 1:
                    ada(9)
                    ada_col(9)
                pe.wait_ge(sem(f"sel{b}"), TT)
                pe.wait_ge(sem("xn_low"), TT * b)
                for k in range(KD):
                    ps = take(pe, f"gx{b}", k)
                    for t in range(TT):
                        for i, x in enumerate((xn_high, xn_low)):
                            last = mm(ps[:, :], R(x[:, t, k * P:(k + 1) * P]), R(sel[:, t, :]),
                                      start=t + i == 0, stop=t + i == TT)
                    full(last, f"gx{b}", k)
                pe.wait_ge(sem(f"selw{b}"), TT)
                for j in range(2):
                    ps = take(pe, f"swT{b}", j)
                    for a in range(2):
                        for t in range(TT):
                            last = tr(ps[:, a * S + t * P:a * S + (t + 1) * P],
                                      selw[:, t, (2 * j + a) * P:(2 * j + a + 1) * P], ident)
                    full(last, f"swT{b}", j)
                for j in range(2):
                    ready(pe, f"swT{b}", j)

                def gate_up(xw, w, i, ks):
                    for k in ks:
                        g = 64 * (k % 2)
                        last = mm(bank[i][g:g + WIN, :], xw[:, k, :], w[:, k * 512:(k + 1) * 512],
                                  start=k < 2, stop=k >= KD - 2)
                    return last

                def gu_T(i):
                    for c in range(4):
                        last = mm(bank[2][:, c * WIN:(c + 1) * WIN], gu_sb[:, i, c * P:(c + 1) * P], stack,
                                  start=True, stop=True)
                    return last

                def down(w):
                    for half in range(2):
                        for f in range(2):
                            o = KD * 512 + f * D + half * 512
                            last = mm(bank[3 + half][64 * f:64 * f + WIN, :], hb[:, f, :], w[:, o:o + 512],
                                      start=True, stop=True)
                    return last

                def down_T():
                    for c in range(KD):
                        last = mm(bank[5][:, c * WIN:(c + 1) * WIN], d_sb[:, c * P:(c + 1) * P], stack,
                                  start=True, stop=True)
                    return last

                base = MOE_AT[b - 1]

                def step(e, r, count, first=(), tail=True):
                    w = ring[:, slot(base + r), :]
                    i = r % 2
                    if 0 not in first:
                        pe.wait_ge(sem(f"gu_sb{b}"), e - 1)
                    pe.wait_ge(sem(f"xwin{b}"), e + 1)
                    pe.wait_ge(sem(f"slot_full{slot(base + r)}"), count)
                    gate_up(xwin[:, i], w, i, range(0, 4))
                    if 0 not in first:
                        pe.wait_ge(sem(f"d_lo{b}"), e - 1)
                        pe.wait_ge(sem(f"d_hi{b}"), e - 1)
                        if 2 not in first:
                            pe.wait_ge(sem(f"y_out{b}"), e - 2)
                        down_T().then_inc(sem(f"yT_done{b}"), 1)
                    if 1 not in first:
                        pe.wait_ge(sem(f"gu_sb{b}"), e)
                        if 0 not in first:
                            pe.wait_ge(sem(f"hb{b}"), e - 1)
                        gu_T(1 - i).then_inc(sem(f"guT_done{b}"), 1)
                    gate_up(xwin[:, i], w, i, range(4, 8)).then_inc(sem(f"gu_done{b}"), 1)
                    if 1 not in first:
                        pe.wait_ge(sem(f"hb{b}"), e)
                        before = 16 * (NE // RING) * (b - 1)
                        rounds = 16 * ((e - 1) // RING + 1) if isinstance(e, int) else \
                            (e - r) * (16 // RING) + (16 if r else 0)
                        pe.wait_ge(sem(f"slot_down{(r - 1) % RING}"), rounds + before)
                        pw = ring[:, slot(base + r - 1), :]
                        down(pw).then_inc(sem(f"down_done{b}"), 1)

                for e in range(RING):
                    skip_ = ({0: (0, 1, 2), 1: (0, 2), 2: (2,)}).get(e, ())
                    step(e, e, 16 * ((base + e) // RING + 1), skip_)
                with pe.Fori(RING, NE - RING + 1, RING) as e0:
                    for r in range(RING):
                        c0 = 16 * ((base + r) // RING + 1)
                        step(e0 + r, r, e0 * (16 // RING) + c0)
                pe.wait_ge(sem(f"d_lo{b}"), NE - 1)
                pe.wait_ge(sem(f"d_hi{b}"), NE - 1)
                pe.wait_ge(sem(f"y_out{b}"), NE - 2)
                down_T().then_inc(sem(f"yT_done{b}"), 1)
                pe.wait_ge(sem(f"gu_sb{b}"), NE)
                gu_T((NE - 1) % 2).then_inc(sem(f"guT_done{b}"), 1)
                pe.wait_ge(sem(f"hb{b}"), NE)
                pe.wait_ge(sem(f"slot_down{RING - 1}"), 16 * (NE // RING) * b)
                down(ring[:, slot(base + NE - 1), :]).then_inc(sem(f"down_done{b}"), 1)
                pe.wait_ge(sem(f"d_lo{b}"), NE)
                pe.wait_ge(sem(f"d_hi{b}"), NE)
                pe.wait_ge(sem(f"y_out{b}"), NE - 1)
                down_T().then_inc(sem(f"yT_done{b}"), 1)
                pe.wait_ge(sem(f"routed{b}"), 1)
                n = pe.value_load(tabi[0:1, 48:49], min_val=0, max_val=NX - 1)
                with pe.If(n > 0):
                    with pe.Fori(0, n) as j:
                        w = ring[:, slot(base), :]
                        pe.wait_ge(sem(f"extra_x{b}"), j + 1)
                        pe.wait_ge(sem(f"extra_w{b}"), j * 16 + 16)
                        gate_up(xwin[:, 0], w, 0, range(KD)).then_inc(sem(f"extra_gu{b}"), 1)
                        pe.wait_ge(sem(f"extra_gs{b}"), j + 1)
                        gu_T(0).then_inc(sem(f"extra_gT{b}"), 1)
                        pe.wait_ge(sem(f"extra_h{b}"), j + 1)
                        down(w).then_inc(sem(f"extra_down{b}"), 1)
                        pe.wait_ge(sem(f"extra_d{b}"), 2 * j + 2)
                        down_T().then_inc(sem(f"extra_yT{b}"), 1)
                pe.wait_ge(sem(f"y_out{b}"), NE)
                pe.wait_ge(sem(f"extra_y{b}"), n + 1)
                for j in range(8):
                    pt, half = j // 2, j % 2
                    ps = take(pe, f"yT{b}", j)
                    for c in range(4):
                        last = tr(ps[:, c * P:(c + 1) * P], ysT[:, 4 * half + c, pt * P:(pt + 1) * P], ident)
                    full(last, f"yT{b}", j)
                if b == 2:
                    gate_row("g2r", diag2, "diag2")
                for j in range(8):
                    ready(pe, f"yT{b}", j)
                for t in range(TT):
                    for half in range(2):
                        ps = take(pe, f"sct{b}", 2 * t + half)
                        for pt in range(NPAIR // P):
                            tok, cols = slice(t * P, (t + 1) * P), slice(half * 512, (half + 1) * 512)
                            last = three_pass(ps[:, :], ((swT[:, pt, tok], swT_low[:, pt, tok]),
                                                         (ytok[:, pt, cols], ytok_low[:, pt, cols])),
                                              pt == 0, pt == NPAIR // P - 1)
                        full(last, f"sct{b}", 2 * t + half)

            def gate_row(stage, dg, ready_sem):
                pe.wait_ge(sem(ready_sem), 1)
                for j in range(2):
                    ps = take(pe, stage, j)
                    full(mm(ps[:, :], ones, dg[:, 4 * j:4 * j + 4, :].rearrange("p a b -> p (a b)"),
                            start=True, stop=True), stage, j)

            moe(1)

            pe.wait_ge(sem("onehot"), 32)
            pe.wait_ge(sem("mask_row"), 1)
            ps = take(pe, "bias")
            full(mm(ps[0:H1, :], relb[0:BUCKETS + 1, :], oneh[0:BUCKETS + 1, :], start=True, stop=True), "bias")
            ada(10)
            ada(11)
            ada_col(10)
            ada_col(11)
            transposed("uT", XN, KD, "xn_u")
            channel_out("xl", ["win0"], HT, low_x, banks_of("uT"))
            gate_row("g1r", diag1, "diag1")
            channel_out("yl", ["win1"], HT, low_x, banks_of("uT"))
            pe.wait_ge(sem("gates_w"), 16)
            for j in range(2):
                ready(pe, "xl", j)
            for stage, o in (("ga", 0), ("gx", 4 * P)):
                for j in range(2):
                    ps = take(pe, stage, j)
                    for a in range(2):
                        i = 2 * j + a
                        last = mm(ps[:, a * S:(a + 1) * S], ROW[:, o + i * P:o + (i + 1) * P], xc[:, i, :],
                                  start=True, stop=True)
                    full(last, stage, j)
            channel_out("aq", ["win2"], HT, low_x, banks_of("uT"))
            channel_out("ak", ["win3"], HT, low_x, banks_of("uT"))
            token_out("av", ["win4"], HT, low_x, banks_of("uT"))
            for stage in ("aq", "ak", "av"):
                all_ready(stage, 2)

            def a_scores(h):
                g, i = 64 * (h % 2), h // 2
                ps = take(pe, f"as{h}")
                mm(ps[:, 0:P], Q2[g:g + 64, i, 0:P], K2[g:g + 64, i, 0:P], start=True, stop=True)
                full(mm(ps[:, P:P + S], Q2[g:g + 64, i, P:S], K2[g:g + 64, i, :], start=True, stop=True), f"as{h}")

            a_scores(0)
            a_scores(1)
            for h in range(H1):
                pe.wait_ge(sem("a_prob"), TT * (h + 1))
                ps = take(pe, f"aT{h}")
                for c in range(3):
                    last = tr(ps[:, c * P:(c + 1) * P], prob2[:, h % 2, c * P:(c + 1) * P], ident)
                full(last, f"aT{h}")
                if h + 2 < H1:
                    a_scores(h + 2)
                ready(pe, f"aT{h}")
                ps = take(pe, f"ap{h}")
                hc = slice(h * 64, (h + 1) * 64)
                mm(ps[:, 0:64], probT2[:, h % 2, 0:P], V2[:, 0, hc], start=True, stop=True)
                mm(ps[:, 64:128], probT2[:, h % 2, P:2 * P], V2[:, 0, hc], start=True, stop=False)
                full(mm(ps[:, 64:128], probT2[:, h % 2, 2 * P:3 * P], V2[:, 1, hc], start=False, stop=True), f"ap{h}")
            pe.wait_ge(sem("lru_sq"), 4)
            ps = take(pe, "lss")
            for t in range(TT):
                for i in range(4):
                    last = mm(ps[:, t:t + 1], sq[:, i, t * P:(t + 1) * P], ones[:, 0:1], start=i == 0, stop=i == 3)
            full(last, "lss")

            def wp(u, part):
                x, x_low = ((loT, lo_low), (aoT, ao_low))[part]
                for c in (2 * part, 2 * part + 1):
                    if c % 2 == 0:
                        ps = [take(pe, *WP[4 * u + 2 * part + t]) for t in range(TT)]
                    pe.wait_ge(sem("w_low"), chunks_to(f"wp{u}", c))
                    wl, wh = part_at(f"wp{u}", c)
                    for a in range(2):
                        i = 2 * (c % 2) + a
                        for t in range(TT):
                            tok = slice(t * P, (t + 1) * P)
                            last = three_pass(ps[t][:, :], ((x[:, i, tok], x_low[:, i, tok]), (wh[:, a, :], wl[:, a, :])),
                                              i == 0, i == 3)
                            if i == 3:
                                full(last, *WP[4 * u + 2 * part + t])
                    if c == 0:
                        last.then_inc(sem("w_used"), 1)

            pe.wait_ge(sem("lo_low"), 1)
            wp(0, 0)
            for j in range(2):
                ps = take(pe, "aoT", j)
                for a in range(2):
                    for t in range(TT):
                        pe.wait_ge(sem("normed"), upto(NORMS, "ao2_n", t))
                        last = tr(ps[:, a * S + t * P:a * S + (t + 1) * P],
                                  AO2[:, t, (2 * j + a) * P:(2 * j + a + 1) * P], ident)
                full(last, "aoT", j)
            all_ready("aoT", 2)
            wp(0, 1)
            wp(1, 0)
            wp(1, 1)
            moe(2)

        @block.scalar
        def _(act):
            A_ = nc.scalar.activation
            steps = [0]

            def link(ins):
                steps[0] += 1
                ins.then_inc(sem("act_step"), 1)
                act.wait_ge(sem("act_step"), steps[0])

            squared = [0]

            def square(junk_, src, total):
                if squared[0]:
                    act.wait_ge(sem("squares"), squared[0])
                squared[0] += 1
                A_(junk_, src, ACT.Square, accum_out=total).then_inc(sem("squares"), 1)

            def squares(tag, src, junk_, sums, wait):
                for t in range(TT):
                    wait(t)
                    square(junk_(t), src(t), sums[:, t:t + 1])

            def channel_evac(stage, dst, n, scale, bias=None, even=0):
                for j in range(even, n, 2):
                    ps = got(act, stage, j)
                    for a in range(2):
                        k = 2 * j + a
                        src = ps[:, a * S:(a + 1) * S]
                        if scale is None:
                            last = A_(dst[:, k, :], src, ACT.Copy)
                        elif bias is None:
                            last = A_(dst[:, k, :], src, ACT.Copy, scale=scale(k))
                        else:
                            last = A_(dst[:, k, :], src, ACT.Identity, scale=scale(k), bias=bias(k))
                    free(last, stage, j)

            act.wait_ge(sem("tab"), 32)
            A_(mod[:, 0:8], C("c_2", 0, 8), ACT.Silu).then_inc(sem("silu_c"), 1)
            lam = C("lru_lambda_2", 0, 4)
            spa, spy = sp_l[:, 0:4], sp_l[:, 4:8]
            link(A_(spa, lam, ACT.Abs))
            A_(spy, spa, ACT.Exp, scale=-1.0).then_inc(sem("lam_exp"), 1)
            act.wait_ge(sem("lam_one"), 1)
            A_(sp_l[:, 12:16], sp_l[:, 8:12], ACT.Ln).then_inc(sem("lam_ln"), 1)
            act.wait_ge(sem("arg"), 1)
            A_(h1[0:FFN, :], arg[0:FFN, :], ACT.Sin).then_inc(sem("sine"), 1)
            act.wait_ge(sem("arg"), 2)
            A_(h2[0:FFN, :], arg[0:FFN, :], ACT.Sin).then_inc(sem("sine"), 1)
            dec = arrived(act, "filt")[:, 2048:4096]
            link(A_(dec, dec, ACT.Abs))

            def hyena_conv(third):
                if third:
                    got(act, f"hyT{third - 1}", 1)
                for j in range(2):
                    ps = got(act, f"hy{third}", j)
                    for a in range(2):
                        i = 4 * third + 2 * j + a
                        A_(conv_t[:, 2 * j + a, :], ps[:, a * S:(a + 1) * S], ACT.Identity,
                           scale=C("hy_conv_w", 12 + i), bias=C("hy_conv_b", i)).then_inc(sem("mid_tap"), 1)

            def decays(n):
                for t in range(TT):
                    for d in range(2):
                        i = 4 * n + 2 * t + d
                        if i >= 2:
                            act.wait_ge(sem("parts"), i - 1)
                        c = (2 * n + d) * HW
                        A_(env[:, i % 2, :], dec[:, c:c + HW], ACT.Exp, scale=T("negt")[:, t:t + 1]
                           ).then_inc(sem("env"), 1)

            def high_evac(stage, dst, n, scale, bias=None):
                for j in range(n):
                    ps = got(act, stage, j)
                    for a in range(2):
                        k = 2 * j + a
                        src = ps[:, a * S:(a + 1) * S]
                        if scale is None:
                            last = A_(R(dst[:, k, :]), src, ACT.Copy)
                        elif bias is None:
                            last = A_(R(dst[:, k, :]), src, ACT.Copy, scale=scale(k))
                        else:
                            last = A_(R(dst[:, k, :]), src, ACT.Identity, scale=scale(k), bias=bias(k))
                    last.then_inc(sem("x_high"), 1)

            def copies(stage, dsts):
                for j, dst in enumerate(dsts):
                    ps = got(act, stage, j)
                    free(A_(dst, ps[:, :], ACT.Copy), stage, j)

            def spectra(n):
                copies(f"sp{n}", [k_c[n][:, 0, :], k_c[n][:, 1, :], k_s[n][:, 0, :], k_s[n][:, 1, :], k_c0[n]])

            def ada_evac(i):
                ps = got(act, f"ada{i}")
                free(A_(ada_sum(i), ps[:, :], ACT.Copy), f"ada{i}")

            decays(0)
            squares("x", lambda t: X[:, t, :], lambda t: XN[:, t, :], ssq_x,
                    lambda t: act.wait_ge(sem(f"x_in{t}"), 16))
            high_evac("hT", HT, 4, lambda k: C("mix_norm_g", k))
            high(act, "lat", (0, 1))
            spectra(0)
            decays(1)
            high(act, "lat", (2, 3))
            for t in range(TT):
                ready(act, "lat", t)
                square(latTb[:, 0, :], lat[:, t, 0:QR], ssq_l[:, t:t + 1])
                square(latTb[:, 1, 0:KVR], lat[:, t, QR:QR + KVR], ssq_l[:, 2 + t:3 + t])
            high(act, "hy0", (0, 1))
            spectra(1)
            high(act, "hy0", (2, 3))
            high(act, "hy1", (0, 1))
            hyena_conv(0)
            high(act, "hy1", (2, 3))
            copies("hyT0", [hytok[:, t, 0, :] for t in range(TT)])
            high(act, "hy2", (0, 1))
            hyena_conv(1)
            ps = got(act, "latT", 0)
            A_(latTb[:, 0, :], ps[:, 0:S], ACT.Copy, scale=C("q_norm_g", 0))
            free(A_(latTb[:, 1, :], ps[:, S:2 * S], ACT.Copy, scale=C("q_norm_g", 1)), "latT", 0)
            ps = got(act, "latT", 1)
            A_(latTb[:, 2, :], ps[:, 0:S], ACT.Copy, scale=C("kv_norm_g"))
            free(A_(latTb[:, 3, :], ps[:, S:2 * S], ACT.Copy), "latT", 1)
            high(act, "hy2", (2, 3))
            copies("hyT1", [hytok[:, t, 1, :] for t in range(TT)])
            hyena_conv(2)
            for j in range(4):
                ps = got(act, "uk", j)
                free(A_(KT[0:NOPE, 2 * j:2 * j + 2, :], three(ps[0:NOPE, :], 2), ACT.Copy), "uk", j)
            copies("uv", [V1[:, t, :] for t in range(TT)])
            copies("hyT2", [hytok[:, t, 2, :] for t in range(TT)])
            for h in range(H1):
                if h >= 2:
                    ada_evac(h - 2)
                ps = got(act, f"sc{h}")
                act.wait_ge(sem("neg_max"), h + 1)
                if h >= 2:
                    got(act, f"pT{h - 2}")
                for t in range(TT):
                    last = A_(prob[:, h % 2, t, :], ps[:, t * S:(t + 1) * S], ACT.Exp, bias=nmax[:, h, t:t + 1],
                              accum_out=rsum[:, h, t:t + 1])
                free(last, f"sc{h}")
            high(act, "mk0", (0, 1))
            act.dma_start(XN, A["mem"].rearrange("(t p) d -> p t d", p=P)).then_inc(sem("mem_in"), 16)
            ready(act, "pv7")
            squares("ao", lambda t: AO[:, t, :], lambda t: junk[:, 0:HW], ssq_o, lambda t: None)
            act.wait_ge(sem("mem_in"), 16)
            squares("m", lambda t: XN[:, t, :], lambda t: junk, ssq_m, lambda t: None)
            act.wait_ge(sem("zed"), 2 * TT)
            squares("z", lambda t: Z[:, t, :], lambda t: junk[:, 0:HW], ssq_o[:, 2:4], lambda t: None)
            high_evac("memT", HT, 4, lambda k: C("mem_norm_g", k))
            high(act, "mk0", (2, 3))
            high(act, "mk1", (0, 1))
            channel_evac("mk", KM, 2, None)
            high(act, "mk1", (2, 3))
            high(act, "mv0", (0, 1))
            ps = got(act, "mk", 2)
            A_(KM[:, 4, :], ps[:, 0:S], ACT.Copy)
            free(A_(KM[:, 5, :], ps[:, S:2 * S], ACT.Copy), "mk", 2)
            for u in range(2):
                high(act, f"mv{u}", (2, 3))
                high(act, ("mv1", "wo0")[u], (0, 1))
                ps = got(act, "mv", 2 * u)
                free(A_(VM[:, 0, u * 512:(u + 1) * 512], ps[:, :], ACT.Copy), "mv", 2 * u)
            high_evac("mixT", HT, 4, lambda k: C("attn_out_g", k))
            high(act, "wo0", (2, 3))
            high(act, "wo1", (0, 1, 2, 3))
            high(act, "mq0", (0, 1))
            squares("c", lambda t: X[:, t, :], lambda t: XN[:, t, :], ssq_c,
                    lambda t: (ready(act, "wo", t), ready(act, "wo", 2 + t)))
            high_evac("cT", HT, 4, lambda k: C("cross_norm_g", k))
            high(act, "mq0", (2, 3))
            high(act, "mq1", (0, 1))
            channel_evac("mq", QX, 2, None)
            high(act, "mq1", (2, 3))
            ps = got(act, "mq", 2)
            A_(QX[:, 4, :], ps[:, 0:S], ACT.Copy)
            free(A_(QX[:, 5, :], ps[:, S:2 * S], ACT.Copy), "mq", 2)
            def x_out(h):
                ps = got(act, f"xv{h}")
                A_(R(oT[:, 2 * h:2 * h + 2, :]), three(ps[:, :], 2), ACT.Copy).then_inc(sem("x_high"), 1)

            for h in range(XH):
                ps = got(act, f"xs{h}")
                act.wait_ge(sem("x_max"), h + 1)
                if h >= 2:
                    got(act, f"xT{h - 2}")
                for t in range(TT):
                    last = A_(prob[:, h % 2, t, :], ps[:, t * S:(t + 1) * S], ACT.Exp, bias=xmax[:, h, t:t + 1],
                              scale=float(XHD ** -0.5), accum_out=xsum[:, h, t:t + 1])
                free(last, f"xs{h}")
                if h in (1, 2):
                    ada_evac(5 + h)
                if h >= 2:
                    x_out(h - 2)
                if h >= 1:
                    ps = got(act, f"xT{h - 1}")
                    if h >= 3:
                        got(act, f"xv{h - 3}")
                    free(A_(probT[:, (h - 1) % 2, :, :], three(ps[:, :], TT), ACT.Copy), f"xT{h - 1}")
            ps = got(act, f"xT{XH - 1}")
            got(act, f"xv{XH - 3}")
            free(A_(probT[:, (XH - 1) % 2, :, :], three(ps[:, :], TT), ACT.Copy), f"xT{XH - 1}")
            high(act, "mo0", (0, 1))
            x_out(XH - 2)
            x_out(XH - 1)
            high(act, "mo0", (2, 3))
            high(act, "mo1", (0, 1, 2, 3))

            def moe(b):
                if b == 1:
                    squares("r", lambda t: X[:, t, :], lambda t: XN[:, t, :], ssq_r,
                            lambda t: (ready(act, "mo", t), ready(act, "mo", 2 + t)))
                    gain, shift = (lambda k: C("ffn_norm_g", k)), None
                else:
                    gain, shift = (lambda k: mod[:, 32 + k:33 + k]), (lambda k: mod[:, 24 + k:25 + k])
                channel_evac(f"rT{b}", HT, 4, gain, shift)
                for t in range(TT):
                    A_(R(xn_high[:, t, :]), XN[:, t, :], ACT.Copy).then_inc(sem("xn_high"), 1)
                act.wait_ge(sem(f"g_diff{b}"), 1)
                A_(gex, cand4, ACT.Exp).then_inc(sem(f"g_exp{b}"), 1)
                if b == 1:
                    ada_evac(8)
                act.wait_ge(sem(f"e_diff{b}"), 1)
                A_(ex2, m2, ACT.Exp).then_inc(sem(f"e_exp{b}"), 1)
                if b == 1:
                    ada_evac(9)
                for k in range(0, KD, 2):
                    ps = got(act, f"gx{b}", k)
                    if shift is None:
                        last = A_(xsT[:, k, 0:NPAIR], ps[:, :], ACT.Copy, scale=gain(k))
                    else:
                        last = A_(xsT[:, k, 0:NPAIR], ps[:, :], ACT.Identity, scale=gain(k), bias=shift(k))
                    free(last, f"gx{b}", k)
                for j in range(2):
                    ps = got(act, f"swT{b}", j)
                    A_(R(swT[:, 2 * j:2 * j + 2, :]), three(ps[:, :], 2), ACT.Copy).then_inc(sem("x_high"), 1)

                def silu(e, i):
                    act.wait_ge(sem(f"guT_done{b}"), e + 1)
                    A_(sg[:, i, :], bank[2][:, 0:2 * WIN], ACT.Silu).then_inc(sem(f"silu{b}"), 1)

                def evac_gu(e, i, first=False):
                    act.wait_ge(sem(f"gu_done{b}"), e + 1)
                    if not first:
                        act.wait_ge(sem(f"guT_done{b}"), e - 1)
                    A_(gu_sb[:, i, :], bank[i][:, :], ACT.Copy).then_inc(sem(f"gu_sb{b}"), 1)

                def evac_down(e, first=False):
                    act.wait_ge(sem(f"down_done{b}"), e + 1)
                    if not first:
                        act.wait_ge(sem(f"yT_done{b}"), e)
                    A_(d_sb[:, 0:512], bank[3][:, :], ACT.Copy).then_inc(sem(f"d_lo{b}"), 1)

                for e in range(RING):
                    if e >= 1:
                        silu(e - 1, (e - 1) % 2)
                    evac_gu(e, e % 2, e < 2)
                    if e >= 1:
                        evac_down(e - 1, e == 1)
                with act.Fori(RING, NE - RING + 1, RING) as e0:
                    for r in range(RING):
                        silu(e0 + (r - 1), (r - 1) % 2)
                        evac_gu(e0 + r, r % 2)
                        evac_down(e0 + (r - 1))
                silu(NE - 1, (NE - 1) % 2)
                evac_down(NE - 1)
                act.wait_ge(sem(f"routed{b}"), 1)
                n = act.value_load(tabi[0:1, 48:49], min_val=0, max_val=NX - 1)
                with act.If(n > 0):
                    with act.Fori(0, n) as j:
                        act.wait_ge(sem(f"extra_gu{b}"), j + 1)
                        A_(gu_sb[:, 0, :], bank[0][:, :], ACT.Copy).then_inc(sem(f"extra_gs{b}"), 1)
                        act.wait_ge(sem(f"extra_gT{b}"), j + 1)
                        A_(sg[:, 0, :], bank[2][:, 0:2 * WIN], ACT.Silu).then_inc(sem(f"extra_s{b}"), 1)
                        act.wait_ge(sem(f"extra_down{b}"), j + 2)
                        A_(d_sb[:, 0:512], bank[3][:, :], ACT.Copy).then_inc(sem(f"extra_d{b}"), 1)
                for j in range(8):
                    ps = got(act, f"yT{b}", j)
                    A_(R(ytok[:, j // 2, (j % 2) * 512:(j % 2 + 1) * 512]), ps[:, :], ACT.Copy).then_inc(sem("x_high"), 1)

            moe(1)
            squares("f", lambda t: X[:, t, :], lambda t: XN[:, 1, :], ssq_f,
                    lambda t: (ready(act, "sct1", 2 * t), ready(act, "sct1", 2 * t + 1)))

            ps = got(act, "bias")
            free(A_(brow[0:H1, :], ps[0:H1, :], ACT.Copy), "bias")
            ready(act, "bias")
            act.dma_start(bias_rows, brow[0:H1, 0:BW].unsqueeze(1).broadcast_to([H1, P, BW])).then_inc(sem("bias_out"), 16)
            act.wait_ge(sem("bias_out"), 16)
            for o, q0, nk in ((0, 0, P), (P, P, S)):
                act.dma_start(BT[:, :, o:o + nk], bass.AP(bias_rows.tensor, S - 1 - q0, [[BW - 1, P], [P * BW, H1], [1, nk]])
                              ).then_inc(sem("bias_in"), 16)
            ada_evac(10)
            ada_evac(11)
            high(act, "win0", (0, 1))
            act.wait_ge(sem("mod"), 1)
            high_evac("uT", HT, 4, lambda k: mod[:, 8 + k:9 + k], lambda k: mod[:, k:k + 1])
            high(act, "win0", (2, 3))
            high(act, "win1", (0, 1))
            for j in range(2):
                ps = got(act, "xl", j)
                for a in range(2):
                    i = 2 * j + a
                    A_(xc[:, i, :], ps[:, a * S:(a + 1) * S], ACT.Identity, scale=C("conv_w_2", 12 + i),
                       bias=C("conv_b_2", i)).then_inc(sem("last_tap"), 1)
            copies("g1r", [g1row[:, 0:512], g1row[:, 512:1024]])
            high(act, "win1", (2, 3))
            high(act, "win2", (0, 1))
            for j in range(2):
                ps = got(act, "yl", j)
                free(A_(gy[:, 2 * j:2 * j + 2, :], three(ps[:, :], 2), ACT.Gelu_apprx_tanh), "yl", j)
            for stage, dst, bias in (("ga", rg, "b_gate_a_2"), ("gx", ig, "b_gate_x_2")):
                for j in range(2):
                    ps = got(act, stage, j)
                    for a in range(2):
                        i = 2 * j + a
                        last = A_(dst[:, i, :], ps[:, a * S:(a + 1) * S], ACT.Sigmoid, bias=C(bias, i))
                    free(last, stage, j)
            high(act, "win2", (2, 3))
            high(act, "win3", (0, 1))
            act.wait_ge(sem("lam"), 1)
            ready(act, "ga", 1)
            for i in range(4):
                A_(th[:, i, :], rg[:, i, :], ACT.Tanh, scale=sp8[:, i:i + 1])
            for i in range(4):
                last = A_(aa[:, i, :], rg[:, i, :], ACT.Exp, scale=sp8n[:, i:i + 1])
            last.then_inc(sem("decay"), 1)
            high(act, "win3", (2, 3))
            high(act, "win4", (0, 1, 2, 3))
            high(act, "wp0", (0, 1))
            copies("av", [V2[:, t, :] for t in range(TT)])
            act.wait_ge(sem("mult2"), 1)
            A_(th[:, :, :], th[:, :, :], ACT.Sqrt).then_inc(sem("mult"), 1)
            for h in range(H1):
                act.wait_ge(sem("a_max"), h + 1)
                if h >= 2:
                    got(act, f"aT{h - 2}")
                A_(prob2[:, h % 2, 0:P], score[:, 0:P], ACT.Exp, bias=amax[:, h, 0:1],
                   accum_out=asum[:, h, 0:1]).then_inc(sem("a_prob"), 1)
                A_(prob2[:, h % 2, P:P + S], score[:, P:P + S], ACT.Exp, bias=amax[:, h, 1:2],
                   accum_out=asum[:, h, 1:2]).then_inc(sem("a_prob"), 1)
                if h == 3:
                    act.wait_ge(sem("lru_out"), 1)
                    for i in range(4):
                        A_(sq[:, i, :], hh[:, i, :], ACT.Square).then_inc(sem("lru_sq"), 1)
                        A_(R(loT[:, i, :]), hh[:, i, :], ACT.Copy, scale=C("norm_lru_g_2", i)).then_inc(sem("lo_g"), 1)
            ready(act, "ap7")
            squares("a", lambda t: AO2[:, t, :], lambda t: area(14336, HW), ssq_a, lambda t: None)
            for j in range(2):
                ps = got(act, "aoT", j)
                for a in range(2):
                    last = A_(R(aoT[:, 2 * j + a, :]), ps[:, a * S:(a + 1) * S], ACT.Copy,
                              scale=C("norm_attn_g_2", 2 * j + a))
                last.then_inc(sem("x_high"), 1)
            high(act, "wp0", (2, 3))
            high(act, "wp1", (0, 1, 2, 3))
            moe(2)
            copies("g2r", [g2row[:, 0:512], g2row[:, 512:1024]])

        @block.vector
        def _(dve):
            V = nc.vector
            steps = [0]

            def link(ins):
                steps[0] += 1
                ins.then_inc(sem("dve_step"), 1)
                dve.wait_ge(sem("dve_step"), steps[0])

            order = []

            def norm_done(tag):
                order.append(tag)
                assert tuple(order) == tuple(n for n, _ in NORMS[:len(order)])

            def normalised(tag, src, dst, rstd, done):
                dve.wait_ge(sem("roots"), upto(ROOTS, tag))
                for t in range(TT):
                    V.tensor_scalar(dst(t), src(t), rstd[:, t:t + 1], None, ALU.mult).then_inc(sem("normed"), 1)
                norm_done(done)

            def moments_of(i, t):
                link(V.bn_stats(bn_[i][t][:, 0:6], X[:, t, 0:512]))
                link(V.bn_stats(bn_[i][t][:, 6:12], X[:, t, 512:1024]))
                V.bn_aggr(mv_[i][:, t, :], bn_[i][t][:, :].rearrange("p (a b) -> p a b", a=2)).then_inc(sem("moments"), 1)

            def moments(i):
                for t in range(TT):
                    moments_of(i, t)

            def layer_norm(i, dst, done, between=lambda: None):
                if i:
                    moments(i)
                between()
                dve.wait_ge(sem("roots"), upto(ROOTS, f"ln{i}"))
                for t in range(TT):
                    V.tensor_scalar(dst[:, t, :], X[:, t, :], mv_[i][:, t, 0:1], rstd_n[i][:, t:t + 1],
                                    ALU.subtract, ALU.mult).then_inc(sem("normed"), 1)
                norm_done(done)

            def channel_evac(stage, dst, n, scale, bias=None, even=1):
                for j in range(even, n, 2):
                    ps = got(dve, stage, j)
                    for a in range(2):
                        k = 2 * j + a
                        src = ps[:, a * S:(a + 1) * S]
                        if scale is None:
                            last = V.tensor_copy(dst[:, k, :], src)
                        elif bias is None:
                            last = V.tensor_scalar(dst[:, k, :], src, scale(k), None, ALU.mult)
                        else:
                            last = V.tensor_scalar(dst[:, k, :], src, scale(k), bias(k), ALU.mult, ALU.add)
                    free(last, stage, j)

            x_highs = [0]

            def low_evac(stage, hi, dst, n, scale, bias=None, early=True):
                if not early:
                    got(dve, stage, n - 1)
                for j in range(n):
                    x_highs[0] += 1
                    ps = got(dve, stage, j)
                    dve.wait_ge(sem("x_high"), x_highs[0])
                    for a in range(2):
                        k = 2 * j + a
                        src = ps[:, a * S:(a + 1) * S]
                        if scale is None:
                            last = V.tensor_tensor(R(dst[:, k, :]), src, R(hi[:, k, :]), ALU.subtract)
                        elif bias is None:
                            last = V.scalar_tensor_tensor(out=R(dst[:, k, :]), in0=src, scalar=scale(k), in1=R(hi[:, k, :]),
                                                          op0=ALU.mult, op1=ALU.subtract)
                        else:
                            link(V.tensor_scalar(dst[:, k, :], src, scale(k), bias(k), ALU.mult, ALU.add))
                            last = V.tensor_tensor(R(dst[:, k, :]), dst[:, k, :], R(hi[:, k, :]), ALU.subtract)
                    free(last, stage, j)

            def sine_argument(stage, bias, freq):
                ps = got(dve, stage)
                y, n = arg[0:FFN, :], turn[0:FFN, :]
                free(V.tensor_scalar(y, ps[0:FFN, 0:S], C(bias, 0, 1, FFN), freq, ALU.add, ALU.mult), stage)
                ready(dve, stage)
                link(V.tensor_scalar(n, y, float(1 / TWO_PI), MAGIC, ALU.mult, ALU.add))
                link(V.tensor_scalar(n, n, MAGIC, None, ALU.subtract))
                link(V.scalar_tensor_tensor(out=y, in0=n, scalar=-PI_HI, in1=y, op0=ALU.mult, op1=ALU.add))
                link(V.scalar_tensor_tensor(out=y, in0=n, scalar=-PI_LO, in1=y, op0=ALU.mult, op1=ALU.add))
                V.tensor_scalar(y, y, PI_IN, -PI_IN, ALU.min, ALU.max).then_inc(sem("arg"), 1)

            dve.wait_ge(sem("tab"), 32)
            sine_argument("f1", "hy_b1", C("hy_freq", 0, 1, FFN))
            dve.wait_ge(sem("lam_exp"), 1)
            spy, one_y, ln_y, den, is0, ratio = [sp_l[:, 4 * i:4 * i + 4] for i in range(1, 7)]
            V.tensor_scalar(one_y, spy, 1.0, None, ALU.add).then_inc(sem("lam_one"), 1)
            dve.wait_ge(sem("silu_c"), 1)
            dve.wait_ge(sem("zeros"), 2)
            V.tensor_copy(cm[:, :, 0:1], mod[:, 0:8].unsqueeze(2)).then_inc(sem("cm"), 1)
            dve.wait_ge(sem("cm"), 1)
            sine_argument("f2", "hy_b2", C("hy_freq", 1, 1, FFN))
            dve.wait_ge(sem("lam_one"), 1)
            link(V.tensor_scalar(den, one_y, 1.0, None, ALU.subtract))
            link(V.tensor_scalar(is0, den, 0.0, None, ALU.is_equal))
            link(V.tensor_tensor(den, den, is0, ALU.add))
            link(V.reciprocal(ratio, den))
            dve.wait_ge(sem("lam_ln"), 1)
            link(V.tensor_tensor(den, ln_y, is0, ALU.add))
            link(V.tensor_tensor(ratio, ratio, den, ALU.mult))
            link(V.tensor_tensor(ratio, ratio, spy, ALU.mult))
            link(V.tensor_scalar(den, C("lru_lambda_2", 0, 4), -1.0, 0.0, ALU.mult, ALU.max))
            link(V.tensor_tensor(ratio, ratio, den, ALU.add))
            link(V.tensor_scalar(sp8, ratio, LRU_C, None, ALU.mult))
            V.tensor_scalar(sp8n, ratio, -LRU_C, None, ALU.mult).then_inc(sem("lam"), 1)

            def latents():
                for t in range(TT):
                    ps = got(dve, "lat", t)
                    free(V.tensor_copy(lat[:, t, :], ps[:, 0:LAT]), "lat", t)
                    ready(dve, "lat", t)
                dve.wait_ge(sem("zeros"), 1)
                kr, kc, ks = lat[:, :, QR + KVR:LAT], three(T("kcos"), TT), three(T("ksin"), TT)
                hf = ROPE // 2
                link(V.tensor_tensor(krb[:, :, 64:96], kr, kc, ALU.mult))
                link(V.tensor_tensor(krb[:, :, 96:96 + hf], kr[:, :, hf:ROPE], ks[:, :, 0:hf], ALU.mult))
                link(V.tensor_tensor(krb[:, :, 96 + hf:128], kr[:, :, 0:hf], ks[:, :, hf:ROPE], ALU.mult))
                link(V.tensor_tensor(krb[:, :, 64:96], krb[:, :, 64:96], krb[:, :, 96:128], ALU.add))
                V.tensor_copy(krb[:, :, 96:128], krb[:, :, 64:96]).then_inc(sem("lat_n"), 1)

            def modulation(i):
                ps = got(dve, f"adac{i}")
                m = mod[:, 4 * i:4 * i + 4]
                free(V.tensor_tensor(m, ps[:, 0:4], C("b_ada_2", 4 * i, 4), ALU.add), f"adac{i}")

            def outer_taps(third):
                for j in range(2):
                    ps = got(dve, f"hy{third}", j)
                    for a in range(2):
                        i = 4 * third + 2 * j + a
                        u, c = ps[:, a * S:(a + 1) * S], conv_t[:, 2 * j + a, :]
                        dve.wait_ge(sem("mid_tap"), 4 * third + 2 * j + 2)
                        link(V.scalar_tensor_tensor(out=c[:, 1:S], in0=u[:, 0:S - 1], scalar=C("hy_conv_w", i),
                                                    in1=c[:, 1:S], op0=ALU.mult, op1=ALU.add))
                        last = V.scalar_tensor_tensor(out=c[:, 0:S - 1], in0=u[:, 1:S], scalar=C("hy_conv_w", 24 + i),
                                                      in1=c[:, 0:S - 1], op0=ALU.mult, op1=ALU.add)
                    free(last, f"hy{third}", j)

            def filter_parts(n):
                for t in range(TT):
                    if n:
                        got(dve, "sp0", 4)
                    i = 4 * n + 2 * t
                    if i:
                        dve.wait_ge(sem("parts"), i)
                    dve.wait_ge(sem("env"), i + 1)
                    ps = got(dve, f"f3_{n}", 2 * t)
                    free(V.tensor_tensor(filt_f, ps[:, :], env[:, 0, :], ALU.mult), f"f3_{n}", 2 * t)
                    ps = got(dve, f"f3_{n}", 2 * t + 1)
                    dve.wait_ge(sem("env"), i + 2)
                    free(V.scalar_tensor_tensor(out=filt_b, in0=ps[:, :], scalar=T("tmask")[:, t:t + 1],
                                                in1=env[:, 1, :], op0=ALU.mult, op1=ALU.mult), f"f3_{n}", 2 * t + 1)
                    ready(dve, f"f3_{n}", 2 * t)
                    ready(dve, f"f3_{n}", 2 * t + 1)
                    V.tensor_tensor(even[:, t, :], filt_f, filt_b, ALU.add).then_inc(sem("parts"), 1)
                    V.tensor_tensor(odd[:, t, :], filt_f, filt_b, ALU.subtract).then_inc(sem("parts"), 1)

            filter_parts(0)
            normalised("x", lambda t: X[:, t, :], lambda t: XN[:, t, :], rstd_x, "xn_x")
            low_evac("hT", HT, low_x, 4, lambda k: C("mix_norm_g", k), early=False)
            low(dve, "lat", (0, 1))
            filter_parts(1)
            low(dve, "lat", (2, 3))
            latents()
            low(dve, "hy0", (0, 1, 2, 3))
            low(dve, "hy1", (0, 1))
            outer_taps(0)
            low(dve, "hy1", (2, 3))
            dve.wait_ge(sem("roots"), upto(ROOTS, "lkv"))
            for t in range(TT):
                V.tensor_scalar(lat[:, t, 0:QR], lat[:, t, 0:QR], rstd_l[:, t:t + 1], None, ALU.mult)
                last = V.tensor_scalar(lat[:, t, QR:QR + KVR], lat[:, t, QR:QR + KVR], rstd_l[:, 2 + t:3 + t],
                                       None, ALU.mult)
                last.then_inc(sem("lat_n"), 1)
            low(dve, "hy2", (0, 1))
            outer_taps(1)
            low(dve, "hy2", (2, 3))
            outer_taps(2)
            qtab = T("qtab").unsqueeze(1).broadcast_to([P, 2, S])
            for j in range(4):
                ps = got(dve, "uq", j)
                free(V.tensor_tensor(QT[:, 2 * j:2 * j + 2, :], three(ps[:, :], 2), qtab, ALU.mult), "uq", j)
            ready(dve, "latT", 1)
            V.tensor_copy(KT[64:128, :, :], latTb[64:128, 3:4, :].broadcast_to([64, H1, S])).then_inc(sem("k_rope"), 1)

            def spectrum_product(n):
                for f in range(TT):
                    cosf = k_c0[n] if f == 0 else k_c[n][:, 1, :]
                    a = got(dve, f"zs{n}", 2 * f)
                    V.tensor_tensor(spec_r[:, f, :], a[:, :], k_c[n][:, f, :], ALU.mult)
                    free(V.tensor_tensor(spec_i[:, f, :], a[:, :], k_s[n][:, f, :], ALU.mult), f"zs{n}", 2 * f)
                    b = got(dve, f"zs{n}", 2 * f + 1)
                    V.tensor_tensor(prod[:, 0, :], b[:, :], k_s[n][:, f, :], ALU.mult)
                    free(V.tensor_tensor(prod[:, 1, :], b[:, :], cosf, ALU.mult), f"zs{n}", 2 * f + 1)
                    ready(dve, f"zs{n}", 2 * f)
                    ready(dve, f"zs{n}", 2 * f + 1)
                    V.tensor_tensor(spec_r[:, f, :], spec_r[:, f, :], prod[:, 0, :], ALU.subtract)
                    V.tensor_tensor(spec_i[:, f, :], spec_i[:, f, :], prod[:, 1, :], ALU.add).then_inc(sem("product"), 1)
                    dve.wait_ge(sem("product"), TT * n + f + 1)

            def gated(n):
                dve.wait_ge(sem("skip_z"), TT * (n + 1))
                for t in range(TT):
                    ps = got(dve, f"cv{n}", t)
                    free(V.tensor_tensor(prod[:, t, :], ps[:, :], skip_z[:, t, :], ALU.add), f"cv{n}", t)
                    ready(dve, f"cv{n}", t)
                    V.tensor_tensor(Z[:, t, :], prod[:, t, :], hytok[:, t, n, :], ALU.mult).then_inc(sem("zed"), 1)

            def mla_max(h):
                ps = got(dve, f"sc{h}")
                link(V.reduce_max(nmax[:, h, :], three(ps[:, :], TT), AXX))
                V.tensor_scalar(nmax[:, h, :], nmax[:, h, :], -1.0, None, ALU.mult).then_inc(sem("neg_max"), 1)

            for t in range(TT):
                ready(dve, "hyT2", t)
            spectrum_product(0)
            mla_max(0)
            mla_max(1)
            for h in range(H1):
                ready(dve, f"sc{h}")
                link(V.reciprocal(rinv[:, h, :], rsum[:, h, :]))
                ps = got(dve, f"pT{h}")
                if h >= 2:
                    got(dve, f"pv{h - 2}")
                free(V.tensor_copy(probT[:, h % 2, :, :], three(ps[:, :], TT)), f"pT{h}")
                if h + 2 < H1:
                    mla_max(h + 2)
                if h < 6:
                    modulation(h)
                ps = got(dve, f"pv{h}")
                free(V.tensor_tensor(AO[:, :, h * VD:(h + 1) * VD], three(ps[:, 0:TT * VD], TT),
                                     rinv[:, h, :].unsqueeze(2).broadcast_to([P, TT, VD]), ALU.mult), f"pv{h}")
                if h == 2:
                    gated(0)
                if h == 5:
                    spectrum_product(1)
            gated(1)
            low(dve, "mk0", (0, 1))
            normalised("ao", lambda t: AO[:, t, :], lambda t: AO[:, t, :], rstd_o, "ao_n")
            normalised("m", lambda t: XN[:, t, :], lambda t: XN[:, t, :], rstd_m, "xn_m")
            normalised("z", lambda t: Z[:, t, :], lambda t: Z[:, t, :], rstd_o[:, 2:4], "z_n")
            low_evac("memT", HT, low_m, 4, lambda k: C("mem_norm_g", k))
            low(dve, "mk0", (2, 3))
            low(dve, "mk1", (0, 1))
            channel_evac("mk", KM, 2, None)
            low(dve, "mk1", (2, 3))
            low(dve, "mv0", (0, 1))
            channel_evac("mk", KM, 4, None, even=3)
            for u in range(2):
                low(dve, f"mv{u}", (2, 3))
                low(dve, ("mv1", "wo0")[u], (0, 1))
                ps = got(dve, "mv", 2 * u + 1)
                free(V.tensor_copy(VM[:, 1, u * 512:(u + 1) * 512], ps[:, :]), "mv", 2 * u + 1)
            low_evac("mixT", HT, low_m, 4, lambda k: C("attn_out_g", k))

            def residual(stage, units):
                low(dve, units[0], (2, 3))
                low(dve, units[1], (0, 1))
                for j in range(4):
                    if j == 2:
                        low(dve, units[1], (2, 3))
                    u, t = j // 2, j % 2
                    ps = got(dve, stage, j)
                    x = X[:, t, u * 512:(u + 1) * 512]
                    free(V.tensor_tensor(x, x, ps[:, :], ALU.add), stage, j)

            residual("wo", ("wo0", "wo1"))
            low(dve, "mq0", (0, 1))
            normalised("c", lambda t: X[:, t, :], lambda t: XN[:, t, :], rstd_c, "xn_c")
            low_evac("cT", HT, low_m, 4, lambda k: C("cross_norm_g", k))
            low(dve, "mq0", (2, 3))
            low(dve, "mq1", (0, 1))
            channel_evac("mq", QX, 2, None)
            low(dve, "mq1", (2, 3))
            channel_evac("mq", QX, 4, None, even=3)

            def x_max(h):
                ps = got(dve, f"xs{h}")
                link(V.reduce_max(xmax[:, h, :], three(ps[:, :], TT), AXX))
                V.tensor_scalar(xmax[:, h, :], xmax[:, h, :], -float(XHD ** -0.5), None, ALU.mult
                                ).then_inc(sem("x_max"), 1)

            def x_out(h):
                ps = got(dve, f"xv{h}")
                x_highs[0] += 1
                dve.wait_ge(sem("x_high"), x_highs[0])
                free(V.tensor_tensor(R(low_m[:, 2 * h:2 * h + 2, :]), three(ps[:, :], 2), R(oT[:, 2 * h:2 * h + 2, :]),
                                     ALU.subtract), f"xv{h}")

            x_max(0)
            x_max(1)
            for h in range(XH):
                ready(dve, f"xs{h}")
                link(V.reciprocal(xinv[:, h, :], xsum[:, h, :]))
                for t in range(TT):
                    p = prob[:, h % 2, t, :]
                    V.tensor_scalar(p, p, xinv[:, h, t:t + 1], None, ALU.mult).then_inc(sem("x_prob"), 1)
                if h < 2:
                    modulation(6 + h)
                if h + 2 < XH:
                    x_max(h + 2)
                if h >= 2:
                    x_out(h - 2)
            x_out(XH - 2)
            x_out(XH - 1)
            low(dve, "mo0", (0, 1))
            residual("mo", ("mo0", "mo1"))

            def first_hit(hit, values, cand, best, n):
                link(V.tensor_tensor(hit, values, best.unsqueeze(2).broadcast_to([P, TT, n]), ALU.is_equal))
                idx = T("g99" if n == G else "e99").unsqueeze(1).broadcast_to([P, TT, n])
                link(V.tensor_tensor(cand, hit, idx, ALU.mult))
                link(V.tensor_reduce(out=i1g, in_=cand, axis=AXX, op=ALU.min))
                link(V.tensor_tensor(hit, idx, i1g.unsqueeze(2).broadcast_to([P, TT, n]), ALU.is_equal))

            def moe(b):
                if b == 1:
                    normalised("r", lambda t: X[:, t, :], lambda t: XN[:, t, :], rstd_r, "xn_r1")
                    gain, shift = (lambda k: C("ffn_norm_g", k)), None
                else:
                    layer_norm(2, XN, "xn_r2")
                    gain, shift = (lambda k: mod[:, 32 + k:33 + k]), (lambda k: mod[:, 24 + k:25 + k])
                channel_evac(f"rT{b}", HT, 4, gain, shift)
                ps = got(dve, f"rt{b}")
                dve.wait_ge(sem("bias_r"), 32)
                dve.wait_ge(sem("zeros"), 3)
                lg = three(ps[:, 0:128], TT)[:, :, 0:G + NE]
                free(V.tensor_tensor(L, lg, biasr[b - 1].unsqueeze(1).broadcast_to([P, TT, G + NE]), ALU.add), f"rt{b}")
                ready(dve, f"rt{b}")
                lgg = L[:, :, 0:G]
                link(V.reduce_max(gmx, lgg, AXX))
                V.tensor_tensor(cand4, lgg, gmx.unsqueeze(2).broadcast_to([P, TT, G]), ALU.subtract
                                ).then_inc(sem(f"g_diff{b}"), 1)
                dve.wait_ge(sem(f"g_exp{b}"), 1)
                link(V.reduce_sum(gsum, gex, AXX))
                link(V.reciprocal(pgrp, gsum))
                first_hit(ohg, lgg, cand4, gmx, G)
                le = L[:, :, G:G + NE].rearrange("p t (g e) -> p t g e", g=G)
                link(V.tensor_tensor(spread, le, ohg.unsqueeze(3).broadcast_to([P, TT, G, EPG]), ALU.mult))
                link(V.reduce_sum(ein, spread.rearrange("p t g e -> p t e g"), AXX))
                link(V.reduce_max(m1, ein, AXX))
                first_hit(oh1, ein, cand8, m1, EPG)
                link(V.scalar_tensor_tensor(out=ein2, in0=oh1, scalar=NEG, in1=ein, op0=ALU.mult, op1=ALU.add))
                link(V.reduce_max(i2, ein2, AXX))
                first_hit(oh2, ein2, cand8, i2, EPG)
                V.tensor_tensor(m2, i2, m1, ALU.subtract).then_inc(sem(f"e_diff{b}"), 1)
                for oh, m in ((oh1, M1), (oh2, M2)):
                    link(V.tensor_tensor(m.rearrange("p t (g e) -> p t g e", g=G),
                                         ohg.unsqueeze(3).broadcast_to([P, TT, G, EPG]),
                                         oh.unsqueeze(2).broadcast_to([P, TT, G, EPG]), ALU.mult))
                V.tensor_tensor(M12, M1, M2, ALU.add).then_inc(sem(f"hot{b}"), 1)
                if b == 1:
                    modulation(8)
                dve.wait_ge(sem(f"e_exp{b}"), 1)
                link(V.tensor_scalar(w2, ex2, 1.0, None, ALU.add))
                link(V.reciprocal(w1, w2))
                link(V.tensor_tensor(w1, w1, pgrp, ALU.mult))
                link(V.tensor_tensor(w2, w1, ex2, ALU.mult))
                ps = got(dve, f"cnt{b}")
                link(V.tensor_copy(counts, ps[:, 2 * NE:3 * NE]))
                link(V.tensor_tensor_scan(incl, counts, zero32, 0.0, ALU.add, ALU.add))
                link(V.tensor_tensor(starts, incl, counts, ALU.subtract))
                free(V.tensor_tensor(posm, three(ps[:, 0:2 * NE], TT), starts.unsqueeze(1).broadcast_to([P, TT, NE]),
                                     ALU.add), f"cnt{b}")
                ready(dve, f"cnt{b}")
                for m, pos in ((M1, pos1), (M2, pos2)):
                    link(V.tensor_tensor(m, m, posm, ALU.mult))
                    link(V.reduce_sum(pos, m, AXX))
                iota = T("iota")
                for t in range(TT):
                    link(V.tensor_scalar(R(sel[:, t, :]), iota, pos1[:, t:t + 1], None, ALU.is_equal))
                    V.scalar_tensor_tensor(out=R(sel[:, t, :]), in0=iota, scalar=pos2[:, t:t + 1], in1=R(sel[:, t, :]),
                                           op0=ALU.is_equal, op1=ALU.add).then_inc(sem(f"sel{b}"), 1)
                for t in range(TT):
                    tmp = ysT[:, 0, 0:NPAIR]
                    V.tensor_scalar(selw[:, t, :], iota, pos1[:, t:t + 1], w1[:, t:t + 1], ALU.is_equal, ALU.mult)
                    link(V.tensor_scalar(tmp, iota, pos2[:, t:t + 1], w2[:, t:t + 1], ALU.is_equal, ALU.mult))
                    V.tensor_tensor(selw[:, t, :], selw[:, t, :], tmp, ALU.add).then_inc(sem(f"selw{b}"), 1)
                    dve.wait_ge(sem(f"selw{b}"), t + 1)
                if b == 1:
                    modulation(9)
                for k in range(1, KD, 2):
                    ps = got(dve, f"gx{b}", k)
                    if shift is None:
                        last = V.tensor_scalar(xsT[:, k, 0:NPAIR], ps[:, :], gain(k), None, ALU.mult)
                    else:
                        last = V.tensor_scalar(xsT[:, k, 0:NPAIR], ps[:, :], gain(k), shift(k), ALU.mult, ALU.add)
                    free(last, f"gx{b}", k)
                for j in range(2):
                    ps = got(dve, f"swT{b}", j)
                    x_highs[0] += 1
                    dve.wait_ge(sem("x_high"), x_highs[0])
                    sw = slice(2 * j, 2 * j + 2)
                    free(V.tensor_tensor(R(swT_low[:, sw, :]), three(ps[:, :], 2), R(swT[:, sw, :]), ALU.subtract),
                         f"swT{b}", j)
                V.memset(xsT[:, :, NPAIR:SORTED], 0.0).then_inc(sem(f"pad{b}"), 1)
                link(V.tensor_copy(tabi[0:1, 0:NE], starts[0:1, :]))
                dve.wait_ge(sem(f"pad{b}"), 1)
                for k in range(0, KD):
                    ready(dve, f"gx{b}", k)

                def window(e, i, table=0):
                    s = dve.value_load(tabi[0:1, bass.ds(table + e, 1)] if not isinstance(e, int)
                                       else tabi[0:1, table + e:table + e + 1], min_val=0, max_val=NPAIR)
                    return s

                def x_window(e, i, first=False):
                    s = window(e, i)
                    if not first:
                        dve.wait_ge(sem(f"gu_done{b}"), e - 1)
                    V.tensor_copy(xwin[:, i], xsT[:, :, bass.ds(s, WIN)]).then_inc(sem(f"xwin{b}"), 1)

                def y_window(e, first=False):
                    s = window(e, 0)
                    dve.wait_ge(sem(f"yT_done{b}"), e + 1)
                    if not first:
                        dve.wait_ge(sem(f"y_out{b}"), e)
                    V.tensor_copy(ysT[:, :, bass.ds(s, WIN)], three(bank[5][:, :], KD)).then_inc(sem(f"y_out{b}"), 1)

                def hidden(e, i, first=False):
                    dve.wait_ge(sem(f"silu{b}"), e + 1)
                    if not first:
                        dve.wait_ge(sem(f"down_done{b}"), e)
                    V.tensor_tensor(hb.rearrange("p a b -> p (a b)"), sg[:, i, :], bank[2][:, 2 * WIN:4 * WIN], ALU.mult
                                    ).then_inc(sem(f"hb{b}"), 1)

                def evac_down(e, first=False):
                    dve.wait_ge(sem(f"down_done{b}"), e + 1)
                    if not first:
                        dve.wait_ge(sem(f"yT_done{b}"), e)
                    V.tensor_copy(d_sb[:, 512:1024], bank[4][:, :]).then_inc(sem(f"d_hi{b}"), 1)

                def extra_windows():
                    r = slice(0, 1)
                    c1, s1, x1, xi1, xe1 = counts[r, :], starts[r, :], nx[r, :], xincl[r, :], xex[r, :]
                    link(V.tensor_scalar(x1, c1, float(WIN), None, ALU.is_gt))
                    for k in range(2, S // WIN):
                        link(V.scalar_tensor_tensor(out=x1, in0=c1, scalar=float(k * WIN), in1=x1, op0=ALU.is_gt, op1=ALU.add))
                    link(V.tensor_tensor_scan(xi1, x1, zero32[r, :], 0.0, ALU.add, ALU.add))
                    link(V.tensor_tensor(xe1, xi1, x1, ALU.subtract))
                    link(V.tensor_scalar(cm64[r, :], c1, float(WIN), None, ALU.subtract))
                    slots = T("iota")[r, 0:NX].unsqueeze(2).broadcast_to([1, NX, NE])

                    def each(v):
                        return v.unsqueeze(1).broadcast_to([1, NX, NE])

                    mk, tm, mb = mk8[r], tm8[r], mk8b[r]
                    link(V.tensor_tensor(mk, slots, each(xe1), ALU.is_ge))
                    link(V.tensor_tensor(mb, slots, each(xi1), ALU.is_lt))
                    link(V.tensor_tensor(mk, mk, mb, ALU.mult))
                    link(V.tensor_tensor(tm, slots, each(xe1), ALU.subtract))
                    link(V.tensor_scalar(tm, tm, 1.0, float(WIN), ALU.add, ALU.mult))
                    link(V.tensor_tensor(tm, tm, each(cm64[r, :]), ALU.min))
                    link(V.tensor_tensor(tm, tm, each(s1), ALU.add))
                    link(V.tensor_tensor(tm, tm, mk, ALU.mult))
                    link(V.reduce_sum(xst[r, :], tm, AXX))
                    link(V.tensor_tensor(mk, mk, each(T("eid")[r, :]), ALU.mult))
                    link(V.reduce_sum(xid[r, :], mk, AXX))
                    V.tensor_copy(tabi[0:1, 32:40], xst[r, :]).then_inc(sem(f"extra_down{b}"), 1)
                    V.tensor_copy(tabi[0:1, 40:48], xid[r, :]).then_inc(sem(f"extra_y{b}"), 1)
                    V.tensor_copy(tabi[0:1, 48:49], xi1[:, NE - 1:NE]).then_inc(sem(f"routed{b}"), 1)

                x_window(0, 0, True)
                x_window(1, 1, True)
                for e in range(RING):
                    if e >= 2:
                        y_window(e - 2, e == 2)
                    if e >= 1:
                        hidden(e - 1, (e - 1) % 2, e == 1)
                        x_window(e + 1, (e + 1) % 2)
                        evac_down(e - 1, e == 1)

                def experts(first, end):
                    with dve.Fori(first, end - RING + 1, RING) as e0:
                        for q in range(RING):
                            y_window(e0 + (q - 2))
                            hidden(e0 + (q - 1), (q - 1) % 2)
                            x_window(e0 + (q + 1), (q + 1) % 2)
                            evac_down(e0 + (q - 1))

                experts(RING, NE // 2)
                extra_windows()
                experts(NE // 2, NE)
                y_window(NE - 2)
                hidden(NE - 1, (NE - 1) % 2)
                evac_down(NE - 1)
                y_window(NE - 1)
                dve.wait_ge(sem(f"y_out{b}"), NE)
                dve.wait_ge(sem(f"xwin{b}"), NE + 1)
                n = dve.value_load(tabi[0:1, 48:49], min_val=0, max_val=NX - 1)
                with dve.If(n > 0):
                    with dve.Fori(0, n) as j:
                        s = dve.value_load(tabi[0:1, bass.ds(32 + j, 1)], min_val=0, max_val=NPAIR)
                        dve.wait_ge(sem(f"extra_down{b}"), j + 1)
                        V.tensor_copy(xwin[:, 0], xsT[:, :, bass.ds(s, WIN)]).then_inc(sem(f"extra_x{b}"), 1)
                        dve.wait_ge(sem(f"extra_s{b}"), j + 1)
                        V.tensor_tensor(hb.rearrange("p a b -> p (a b)"), sg[:, 0, :], bank[2][:, 2 * WIN:4 * WIN],
                                        ALU.mult).then_inc(sem(f"extra_h{b}"), 1)
                        dve.wait_ge(sem(f"extra_down{b}"), j + 2)
                        V.tensor_copy(d_sb[:, 512:1024], bank[4][:, :]).then_inc(sem(f"extra_d{b}"), 1)
                        dve.wait_ge(sem(f"extra_yT{b}"), j + 1)
                        V.tensor_copy(ysT[:, :, bass.ds(s, WIN)], three(bank[5][:, :], KD)).then_inc(sem(f"extra_y{b}"), 1)
                for j in range(8):
                    ps = got(dve, f"yT{b}", j)
                    x_highs[0] += 1
                    dve.wait_ge(sem("x_high"), x_highs[0])
                    cols = slice((j % 2) * 512, (j % 2 + 1) * 512)
                    free(V.tensor_tensor(R(ytok_low[:, j // 2, cols]), ps[:, :], R(ytok[:, j // 2, cols]), ALU.subtract),
                         f"yT{b}", j)

            moe(1)

            def block1_end(t):
                for u in range(2):
                    ps = got(dve, "sct1", 2 * t + u)
                    x = X[:, t, u * 512:(u + 1) * 512]
                    free(V.tensor_tensor(x, x, ps[:, :], ALU.add), "sct1", 2 * t + u)
                dve.wait_ge(sem("rows"), 16)
                dve.wait_ge(sem("roots"), upto(ROOTS, f"f{t}"))
                link(V.scalar_tensor_tensor(out=X[:, t, :], in0=X[:, t, :], scalar=rstd_f[:, t:t + 1],
                                            in1=ROW[:, 0:1024], op0=ALU.mult, op1=ALU.mult))
                moments_of(0, t)

            for t in range(TT):
                block1_end(t)

            modulation(10)
            modulation(11)
            ready(dve, "adac11")
            V.tensor_scalar(mod[:, 8:16], mod[:, 8:16], 1.0, None, ALU.add)
            V.tensor_scalar(mod[:, 32:40], mod[:, 32:40], 1.0, None, ALU.add).then_inc(sem("mod"), 1)
            idb = ident.unsqueeze(1).broadcast_to([P, KD, P])
            V.tensor_tensor(diag1, idb, mod[:, 16:24].unsqueeze(2).broadcast_to([P, KD, P]), ALU.mult
                            ).then_inc(sem("diag1"), 1)
            dve.wait_ge(sem("mod"), 1)
            layer_norm(0, XN, "xn_u", lambda: low(dve, "win0", (0, 1)))
            low_evac("uT", HT, low_x, 4, lambda k: mod[:, 8 + k:9 + k], lambda k: mod[:, k:k + 1], early=False)
            low(dve, "win0", (2, 3))
            low(dve, "win1", (0, 1))
            for j in range(2):
                ps = got(dve, "xl", j)
                for a in range(2):
                    i = 2 * j + a
                    u, c = ps[:, a * S:(a + 1) * S], xc[:, i, :]
                    dve.wait_ge(sem("last_tap"), 2 * j + 2)
                    for back in (1, 2, 3):
                        last = V.scalar_tensor_tensor(out=c[:, back:S], in0=u[:, 0:S - back],
                                                      scalar=C("conv_w_2", 4 * (3 - back) + i), in1=c[:, back:S],
                                                      op0=ALU.mult, op1=ALU.add)
                        if back < 3:
                            link(last)
                        elif a == 0:
                            link(last)
                free(last, "xl", j)
            low(dve, "win1", (2, 3))
            low(dve, "win2", (0, 1))
            low(dve, "win2", (2, 3))
            low(dve, "win3", (0, 1))
            channel_evac("aq", Q2, 2, None, even=0)
            channel_evac("aq", Q2, 2, None, even=1)
            low(dve, "win3", (2, 3))
            dve.wait_ge(sem("decay"), 1)
            for j in range(2):
                ready(dve, "gx", j)
                ready(dve, "yl", j)
            link(V.tensor_tensor(hh, aa, aa, ALU.mult))
            V.scalar_tensor_tensor(out=th, in0=hh, scalar=1.0, in1=th, op0=ALU.add, op1=ALU.mult).then_inc(sem("mult2"), 1)
            link(V.tensor_tensor(ig, ig, xc, ALU.mult))
            low(dve, "win4", (0, 1))
            channel_evac("ak", K2, 2, None, even=0)
            channel_evac("ak", K2, 2, None, even=1)
            low(dve, "win4", (2, 3))
            low(dve, "wp0", (0, 1))
            dve.wait_ge(sem("bias_in"), 32)

            def a_max(h):
                ps = got(dve, f"as{h}")
                if h >= 1:
                    dve.wait_ge(sem("a_prob"), TT * h)
                free(V.scalar_tensor_tensor(out=score, in0=ps[:, 0:P + S], scalar=0.125, in1=BT[:, h, :],
                                            op0=ALU.mult, op1=ALU.add), f"as{h}")
                ready(dve, f"as{h}")
                link(V.reduce_max(amax[:, h, 0:1], score[:, 0:P], AXX))
                link(V.reduce_max(amax[:, h, 1:2], score[:, P:P + S], AXX))
                V.tensor_scalar(amax[:, h, :], amax[:, h, :], -1.0, None, ALU.mult).then_inc(sem("a_max"), 1)

            a_max(0)
            a_max(1)
            for h in range(H1):
                dve.wait_ge(sem("a_prob"), TT * (h + 1))
                link(V.reciprocal(ainv[:, h, :], asum[:, h, :]))
                ps = got(dve, f"aT{h}")
                if h >= 2:
                    got(dve, f"ap{h - 2}")
                free(V.tensor_copy(probT2[:, h % 2, :], ps[:, 0:3 * P]), f"aT{h}")
                if h + 2 < H1:
                    a_max(h + 2)
                ps = got(dve, f"ap{h}")
                free(V.tensor_tensor(AO2[:, :, h * 64:(h + 1) * 64], three(ps[:, 0:128], TT),
                                     ainv[:, h, :].unsqueeze(2).broadcast_to([P, TT, 64]), ALU.mult), f"ap{h}")
                if h == 0:
                    dve.wait_ge(sem("mult"), 1)
                    link(V.tensor_tensor(ig, ig, th, ALU.mult))
                    for i in range(4):
                        link(V.tensor_tensor_scan(hh[:, i, :], aa[:, i, :], ig[:, i, :], 0.0, ALU.mult, ALU.add))
                    V.tensor_tensor(hh, hh, gy, ALU.mult).then_inc(sem("lru_out"), 1)
                if h == 5:
                    dve.wait_ge(sem("lo_g"), 4)
                    for i in range(4):
                        last = V.scalar_tensor_tensor(out=R(lo_low[:, i, :]), in0=hh[:, i, :], scalar=C("norm_lru_g_2", i),
                                                      in1=R(loT[:, i, :]), op0=ALU.mult, op1=ALU.subtract)
                    last.then_inc(sem("lo_low"), 1)
            ps = got(dve, "lss")
            free(V.tensor_copy(ssq_a[:, 2:4], ps[:, 0:2]), "lss")
            normalised("a", lambda t: AO2[:, t, :], lambda t: AO2[:, t, :], rstd_a, "ao2_n")
            low_evac("aoT", aoT, ao_low, 2, lambda k: C("norm_attn_g_2", k))
            low(dve, "wp0", (2, 3))
            dve.wait_ge(sem("roots"), upto(ROOTS, "lru"))
            mix = [gy[:, 2 * t:2 * t + 2, :].rearrange("p a b -> p (a b)") for t in range(TT)]
            for u in range(2):
                cols = slice(u * 512, (u + 1) * 512)
                low(dve, "wp1", (2 * u, 2 * u + 1))
                for t in range(TT):
                    ps = got(dve, *WP[4 * u + t])
                    link(V.scalar_tensor_tensor(out=mix[t], in0=ps[:, :], scalar=rstd_a[:, 2 + t:3 + t],
                                                in1=g1row[:, cols], op0=ALU.mult, op1=ALU.mult))
                    x = X[:, t, cols]
                    free(V.scalar_tensor_tensor(out=x, in0=x, scalar=ALPHA, in1=mix[t], op0=ALU.mult, op1=ALU.add),
                         *WP[4 * u + t])
                for t in range(TT):
                    ready(dve, *WP[4 * u + t])
                    ps = got(dve, *WP[4 * u + 2 + t])
                    link(V.tensor_tensor(mix[t], ps[:, :], g1row[:, cols], ALU.mult))
                    free(V.tensor_tensor(X[:, t, cols], X[:, t, cols], mix[t], ALU.add), *WP[4 * u + 2 + t])
                for t in range(TT):
                    ready(dve, *WP[4 * u + 2 + t])

            def full_layer_norm(i, rows, done, before=lambda t: None):
                for t in range(TT):
                    before(t)
                    moments_of(i, t)
                    dve.wait_ge(sem("rows"), rows)
                    dve.wait_ge(sem("moments"), TT * i + t + 1)
                    link(V.scalar_tensor_tensor(out=X[:, t, :], in0=X[:, t, :], scalar=mv_[i][:, t, 0:1],
                                                in1=ROW[:, 0:1024], op0=ALU.subtract, op1=ALU.mult))
                dve.wait_ge(sem("roots"), upto(ROOTS, f"ln{i}"))
                for t in range(TT):
                    V.scalar_tensor_tensor(out=X[:, t, :], in0=X[:, t, :], scalar=rstd_n[i][:, t:t + 1],
                                           in1=ROW[:, 1024:2048], op0=ALU.mult, op1=ALU.add).then_inc(sem(done), 1)
                for t in range(TT):
                    dve.wait_ge(sem(done), t + 1)

            full_layer_norm(1, 48, "x_mid")
            moe(2)
            got(dve, "g2r", 1)
            mixf = diag2.rearrange("p a b -> p (a b)")[:, 0:512]
            for j in range(2):
                ready(dve, "g2r", j)

            def moe_residual(t):
                for u in range(2):
                    j = 2 * t + u
                    ps = got(dve, "sct2", j)
                    free(V.tensor_tensor(mixf, ps[:, :], g2row[:, u * 512:(u + 1) * 512], ALU.mult), "sct2", j)
                    ready(dve, "sct2", j)
                    x = X[:, t, u * 512:(u + 1) * 512]
                    link(V.scalar_tensor_tensor(out=x, in0=x, scalar=ALPHA, in1=mixf, op0=ALU.mult, op1=ALU.add))

            full_layer_norm(3, 80, "x_end", moe_residual)

        @block.gpsimd
        def _(pool):
            G_ = nc.gpsimd
            steps = [0]

            def link(ins):
                steps[0] += 1
                ins.then_inc(sem("pool_step"), 1)
                pool.wait_ge(sem("pool_step"), steps[0])

            order = []

            def rooted(tag):
                order.append(tag)
                assert tuple(order) == tuple(n for n, _ in ROOTS[:len(order)])
                pool.wait_ge(sem("roots"), len(order))

            def root(waits, sums, out_, width, eps, done):
                for s in waits:
                    pool.wait_ge(sem("squares"), upto(SQUARES, s))
                link(G_.tensor_scalar(out_, sums, 1.0 / width, eps, ALU.mult, ALU.add))
                G_.tensor_tensor(out_, out_, half_neg[:, 0:out_.shape[1]], ALU.pow).then_inc(sem("roots"), 1)
                rooted(done)

            def broadcast_row(dst, name, n, done):
                a = A[name]
                pool.dma_start(dst, bass.AP(a.tensor, 0, [[0, P], [1, n]])).then_inc(sem(done), 16)

            link(G_.memset(half_neg, -0.5))
            G_.memset(h2[64:65, :], 1.0).then_inc(sem("h2_one"), 1)
            pool.wait_ge(sem("h2_one"), 1)
            for n, m in enumerate((krb[:, :, :], cm[:, :, :], zero32)):
                G_.memset(m, 0.0).then_inc(sem("zeros"), 1)
                pool.wait_ge(sem("zeros"), n + 1)
            pool.dma_start(wr[:, 0, :], A["wr"]).then_inc(sem("wr"), 16)
            for b, name in enumerate(("rbias", "rbias_2")):
                broadcast_row(biasr[b], name, G + NE, "bias_r")
            root(["x"], ssq_x, rstd_x, D, EPS1, "x")
            root(["l"], ssq_l[:, 0:2], rstd_l[:, 0:2], QR, EPS1, "lq")
            root(["l"], ssq_l[:, 2:4], rstd_l[:, 2:4], KVR, EPS1, "lkv")
            pool.wait_ge(sem("wr"), 16)
            pool.dma_start(wr[:, 1, :], A["wr_2"]).then_inc(sem("wr"), 16)
            pool.wait_ge(sem("skip"), 16)
            for n in range(ORDER):
                if n == 0:
                    for t in range(TT):
                        ready(pool, "hyT2", t)
                        got(pool, "hyT2", t)
                else:
                    pool.wait_ge(sem("zed"), TT)
                for t in range(TT):
                    G_.tensor_tensor(skip_z[:, t, :], Z[:, t, :], skip[:, n, :], ALU.mult).then_inc(sem("skip_z"), 1)
                    pool.wait_ge(sem("skip_z"), TT * n + t + 1)
            root(["ao"], ssq_o[:, 0:2], rstd_o[:, 0:2], HW, EPS1, "ao")
            root(["m"], ssq_m, rstd_m, D, EPS1, "m")
            root(["z"], ssq_o[:, 2:4], rstd_o[:, 2:4], HW, EPS1, "z")
            root(["c"], ssq_c, rstd_c, D, EPS1, "c")
            for j in range(2):
                ready(pool, "mixT", j)
            broadcast_row(ROW[:, 0:1024], "final_norm_g", D, "rows")
            root(["r"], ssq_r, rstd_r, D, EPS1, "r")

            def low_tokens(b):
                for t in range(TT):
                    pool.wait_ge(sem("xn_high"), TT * (b - 1) + t + 1)
                    G_.tensor_tensor(R(xn_low[:, t, :]), XN[:, t, :], R(xn_high[:, t, :]), ALU.subtract
                                     ).then_inc(sem("xn_low"), 1)
                    pool.wait_ge(sem("xn_low"), TT * (b - 1) + t + 1)

            low_tokens(1)
            ready(pool, "swT1", 1)
            pool.dma_start(oneh, A["onehot"]).then_inc(sem("onehot"), 16)
            pool.dma_start(relb[0:BUCKETS, :], A["rel_bias_2"]).then_inc(sem("onehot"), 16)
            G_.memset(relb[BUCKETS:BUCKETS + 1, :], NEG).then_inc(sem("mask_row"), 1)
            pool.wait_ge(sem("mask_row"), 1)
            for t in range(TT):
                pool.wait_ge(sem("squares"), upto(SQUARES, "f", t))
                root([], ssq_f[:, t:t + 1], rstd_f[:, t:t + 1], D, EPS1, f"f{t}")
            pool.wait_ge(sem("moments"), TT)
            pool.dma_start(ROW[:, 0:1024], A["gates_w"]).then_inc(sem("gates_w"), 16)
            link(G_.tensor_scalar(rstd_n[0], mv_[0][:, :, 1], EPS2, 1.0, ALU.add, ALU.mult))
            G_.tensor_tensor(rstd_n[0], rstd_n[0], half_neg[:, 0:2], ALU.pow).then_inc(sem("roots"), 1)
            rooted("ln0")
            for j in range(2):
                got(pool, "gx", j)
            broadcast_row(ROW[:, 0:1024], "ln1_g_2", D, "rows")
            broadcast_row(ROW[:, 1024:2048], "ln1_b_2", D, "rows")
            root(["a"], ssq_a[:, 0:2], rstd_a[:, 0:2], HW, EPS2, "a")
            ready(pool, "lss")
            root([], ssq_a[:, 2:4], rstd_a[:, 2:4], HW, EPS2, "lru")

            def ln_root(i):
                pool.wait_ge(sem("moments"), TT * (i + 1))
                link(G_.tensor_scalar(rstd_n[i], mv_[i][:, :, 1], EPS2, 1.0, ALU.add, ALU.mult))
                G_.tensor_tensor(rstd_n[i], rstd_n[i], half_neg[:, 0:2], ALU.pow).then_inc(sem("roots"), 1)
                rooted(f"ln{i}")

            ln_root(1)
            ln_root(2)
            pool.wait_ge(sem("x_mid"), TT)
            broadcast_row(ROW[:, 0:1024], "ln2_g_2", D, "rows")
            broadcast_row(ROW[:, 1024:2048], "ln2_b_2", D, "rows")
            low_tokens(2)
            got(pool, "rt2")
            G_.tensor_tensor(diag2, ident.unsqueeze(1).broadcast_to([P, KD, P]),
                             mod[:, 40:48].unsqueeze(2).broadcast_to([P, KD, P]), ALU.mult).then_inc(sem("diag2"), 1)
            pool.wait_ge(sem("diag2"), 1)
            ln_root(3)
            for t in range(TT):
                pool.wait_ge(sem("x_end"), t + 1)
                pool.dma_start(out[t * P:(t + 1) * P, :], X[:, t, :]).then_inc(sem("stored"), 16)
            pool.wait_ge(sem("stored"), 16 * TT)


def _ktiles(w):
    k, n = w.shape
    return np.ascontiguousarray(w.reshape(k // P, P, n).transpose(1, 0, 2).reshape(P, -1))


def _padded(w, rows=P):
    out = np.zeros((rows,) + w.shape[1:], w.dtype)
    out[:w.shape[0]] = w
    return out


def _experts(gate, up, down):
    n = gate.shape[0]
    out = np.empty((n, P, SLOT), gate.dtype)
    gu = out[:, :, :KD * 512].reshape(n, P, KD, 2, FE)
    gu[:, :, :, 0] = gate.reshape(n, KD, P, FE).transpose(0, 2, 1, 3)
    gu[:, :, :, 1] = up.reshape(n, KD, P, FE).transpose(0, 2, 1, 3)
    out[:, :, KD * 512:] = down.reshape(n, FE // P, P, D).transpose(0, 2, 1, 3).reshape(n, P, -1)
    return out


def _arrays(i):
    t, dft, filt, feat, onehot = _tables()
    g = {k: np.asarray(v) for k, v in i.items()}
    a = {"x": g["x"][0], "mem": g["mem"][0], "tab": t, "dft": dft, "onehot": onehot,
         "hy_skip": g["hy_skip"][0], "final_norm_g": g["final_norm_g"], "rel_bias_2": g["rel_bias_2"],
         "ln1_g_2": g["ln1_g_2"][0], "ln1_b_2": g["ln1_b_2"][0], "ln2_g_2": g["ln2_g_2"][0], "ln2_b_2": g["ln2_b_2"][0]}
    cols = []
    for name, w in COLS:
        v = g[name]
        if name in ("hy_b1", "hy_b2", "hy_freq"):
            cols.append(_padded(v.reshape(w, FFN).T))
        else:
            cols.append(v.reshape(w, P).T)
    a["col"] = np.concatenate(cols, 1)
    w_in = g["w_in"][0]
    a["lat"] = _ktiles(w_in[:, :LAT])
    for u in range(3):
        a[f"hy{u}"] = _ktiles(w_in[:, LAT + u * HW:LAT + (u + 1) * HW])
    w3 = _padded(np.concatenate([g["hy_w3"][0], g["hy_b3"]], 0))
    decay = np.broadcast_to(g["hy_decay"][0], (P, 2048))
    a["filt"] = np.concatenate([w3, decay, filt, feat, _padded(g["hy_w1"][0]), _padded(g["hy_w2"][0])], 1)
    uq = g["w_uq"][0].reshape(QR, H1, NOPE + ROPE)
    half = ROPE // 2
    uq = np.concatenate([uq, uq[:, :, NOPE + half:], uq[:, :, NOPE:NOPE + half]], 2).reshape(QR, H1 * P)
    ukv = g["w_ukv"][0].reshape(KVR, H1, NOPE + VD)
    a["mla"] = np.concatenate([_ktiles(uq), ukv[:, :, :NOPE].reshape(KVR, -1), ukv[:, :, NOPE:].reshape(KVR, -1)], 1)
    for name, key in (("mk", None), ("mv", None), ("wo", "w_out"), ("mq", "w_mq"), ("mo", "w_mo"), ("wp", "w_out_2")):
        w = g["w_mkv"][0][:, :D] if name == "mk" else g["w_mkv"][0][:, D:] if name == "mv" else g[key][0]
        for u in range(2):
            a[f"{name}{u}"] = _ktiles(w[:, u * 512:(u + 1) * 512])
    for u in range(12):
        a[f"ada{u}"] = _ktiles(g["w_ada_2"][0][:, u * 512:(u + 1) * 512])
    for u in range(5):
        a[f"win{u}"] = _ktiles(g["w_in_2"][0][:, u * 512:(u + 1) * 512])
    a["wr"] = _ktiles(np.concatenate([g["w_route_group"][0], g["w_route_expert"][0]], 1))
    a["wr_2"] = _ktiles(np.concatenate([g["w_router_group_2"][0], g["w_router_expert_2"][0]], 1))
    a["rbias"] = np.concatenate([g["b_route_group"][0], g["b_route_expert"][0]])
    a["rbias_2"] = np.concatenate([g["b_router_group_2"][0], g["b_router_expert_2"][0]])
    gates = np.zeros((P, 2, 4, P), np.float32)
    for q, name in enumerate(("w_gate_a_2", "w_gate_x_2")):
        w = g[name][0]
        for n in range(8):
            gates[64 * (n % 2):64 * (n % 2) + 64, q, n // 2, 64 * (n % 2):64 * (n % 2) + 64] = w[n]
    a["gates_w"] = gates.reshape(P, -1)
    a["experts"] = _experts(g["w_gate"][0].reshape(NE, D, FE), g["w_up"][0].reshape(NE, D, FE),
                            g["w_down"][0].reshape(NE, FE, D))
    a["experts_2"] = _experts(g["w1_2"][0], g["w3_2"][0], g["w2_2"][0])
    return {k: np.ascontiguousarray(v) for k, v in a.items()}


def kernel(**inputs):
    import concourse.bacc as bacc
    from concourse.bass_utils import run_bass_kernel_spmd as run

    nc = bacc.Bacc("TRN2", target_bir_lowering=False, num_devices=1)
    arrays = {f"in_{k}": v for k, v in _arrays(inputs).items()}
    aps = {k[3:]: nc.dram_tensor(k, v.shape, mybir.dt.from_np(v.dtype), kind="ExternalInput").ap()
           for k, v in arrays.items()}
    out = nc.dram_tensor("out", (S, D), F32, kind="ExternalOutput").ap()
    two_blocks(nc, aps, out)
    r = run(nc, [arrays], core_ids=[0])
    return r.results[0]["out"].reshape(1, S, D)
```
